# Optimizing a Trainium2 kernel written in Bass

```python
import math
import jax, jax.numpy as jnp
from jax import lax
import numpy as np

D_MODEL = 1024
BATCH = 1
SEQ = 512
DEPTH = 2

N_MIXERS = 2
N_MLA_LAYERS = (DEPTH + 1) // 2
N_DIFF_LAYERS = DEPTH // 2

MLA_NOPE = 128
MLA_ROPE = 64
MLA_V = 128
MLA_HEADS = D_MODEL // MLA_V
MLA_Q_LORA = 384
MLA_KV_LORA = 256
MLA_ROPE_THETA = 10000.0

DIFF_HEAD_DIM = 64
DIFF_HEADS = D_MODEL // (2 * DIFF_HEAD_DIM)
DIFF_ROT_DIM = DIFF_HEAD_DIM // 4
ROPE_THETA = 500000.0

D_FF = 4 * D_MODEL
Q_BLOCK = 128
DEEPNORM_ALPHA = (2 * DEPTH) ** 0.25
DEEPNORM_BETA = (8 * DEPTH) ** -0.25
LN_EPS = 1e-5
RMS_EPS = 1e-6


def _layernorm(x, g, b):
    xf = x.astype(jnp.float32)
    mu = jnp.mean(xf, axis=-1, keepdims=True)
    var = jnp.mean(jnp.square(xf - mu), axis=-1, keepdims=True)
    y = (xf - mu) * lax.rsqrt(var + LN_EPS) * g.astype(jnp.float32) + b.astype(jnp.float32)
    return y.astype(x.dtype)

def _rmsnorm(x, g):
    xf = x.astype(jnp.float32)
    y = xf * lax.rsqrt(jnp.mean(jnp.square(xf), axis=-1, keepdims=True) + RMS_EPS)
    return (y * g.astype(jnp.float32)).astype(x.dtype)

def _rope(x, positions, theta):
    d = x.shape[-1]
    inv_freq = theta ** (-jnp.arange(0, d, 2, dtype=jnp.float32) / d)
    ang = positions.astype(jnp.float32)[:, :, None] * inv_freq
    cos = jnp.cos(ang)[:, :, None, :]
    sin = jnp.sin(ang)[:, :, None, :]
    xf = x.astype(jnp.float32)
    x1, x2 = xf[..., : d // 2], xf[..., d // 2:]
    out = jnp.concatenate([x1 * cos - x2 * sin, x2 * cos + x1 * sin], axis=-1)
    return out.astype(x.dtype)

def _partial_rope(x, positions, rot_dim, theta):
    return jnp.concatenate([_rope(x[..., :rot_dim], positions, theta), x[..., rot_dim:]], axis=-1)

def _to_blocks(t):
    b, s = t.shape[0], t.shape[1]
    return t.reshape(b, s // Q_BLOCK, Q_BLOCK, *t.shape[2:]).swapaxes(0, 1)

def _from_blocks(t):
    n, b, qb = t.shape[0], t.shape[1], t.shape[2]
    return t.swapaxes(0, 1).reshape(b, n * qb, *t.shape[3:])

def _causal_probs(q_blk, k, q_start, scale):
    s = jnp.einsum('bqhd,bkhd->bhqk', q_blk, k).astype(jnp.float32) * scale
    q_idx = q_start + jnp.arange(q_blk.shape[1])
    k_idx = jnp.arange(k.shape[1])
    s = jnp.where(k_idx[None, :] <= q_idx[:, None], s, -jnp.inf)
    return jax.nn.softmax(s, axis=-1)

def _mla(x, positions, w_dq, q_norm, w_uq, w_dkv, kv_norm, w_ukv, w_o):
    b, s, _ = x.shape
    h = MLA_HEADS
    cq = _rmsnorm(x @ w_dq, q_norm)
    q = (cq @ w_uq).reshape(b, s, h, MLA_NOPE + MLA_ROPE)
    q = jnp.concatenate([q[..., :MLA_NOPE], _rope(q[..., MLA_NOPE:], positions, MLA_ROPE_THETA)], axis=-1)
    ckv = x @ w_dkv
    c_kv = _rmsnorm(ckv[..., :MLA_KV_LORA], kv_norm)
    k_pe = _rope(ckv[..., None, MLA_KV_LORA:], positions, MLA_ROPE_THETA)
    kv = (c_kv @ w_ukv).reshape(b, s, h, MLA_NOPE + MLA_V)
    k = jnp.concatenate([kv[..., :MLA_NOPE], jnp.broadcast_to(k_pe, (b, s, h, MLA_ROPE))], axis=-1)
    v = kv[..., MLA_NOPE:]
    scale = (MLA_NOPE + MLA_ROPE) ** -0.5
    starts = jnp.arange(s // Q_BLOCK) * Q_BLOCK

    def block(args):
        q_blk, start = args
        p = _causal_probs(q_blk, k, start, scale)
        return jnp.einsum('bhqk,bkhd->bqhd', p.astype(v.dtype), v)

    o = _from_blocks(lax.map(block, (_to_blocks(q), starts)))
    return o.reshape(b, s, h * MLA_V) @ w_o

def _diff_attn(x, positions, w_qkv, lq1, lk1, lq2, lk2, subln, w_o, lambda_init):
    b, s, _ = x.shape
    h, dh = DIFF_HEADS, DIFF_HEAD_DIM
    q, k, v = jnp.split(x @ w_qkv, 3, axis=-1)
    q = _partial_rope(q.reshape(b, s, 2 * h, dh), positions, DIFF_ROT_DIM, ROPE_THETA).reshape(b, s, h, 2, dh)
    k = _partial_rope(k.reshape(b, s, 2 * h, dh), positions, DIFF_ROT_DIM, ROPE_THETA).reshape(b, s, h, 2, dh)
    v = v.reshape(b, s, h, 2 * dh)
    k1, k2 = k[..., 0, :], k[..., 1, :]
    lam = (jnp.exp(jnp.sum(lq1.astype(jnp.float32) * lk1.astype(jnp.float32)))
           - jnp.exp(jnp.sum(lq2.astype(jnp.float32) * lk2.astype(jnp.float32)))
           + lambda_init)
    scale = dh ** -0.5
    starts = jnp.arange(s // Q_BLOCK) * Q_BLOCK

    def block(args):
        q_blk, start = args
        p1 = _causal_probs(q_blk[..., 0, :], k1, start, scale)
        p2 = _causal_probs(q_blk[..., 1, :], k2, start, scale)
        a = p1 - lam * p2
        return jnp.einsum('bhqk,bkhd->bqhd', a.astype(v.dtype), v)

    o = _from_blocks(lax.map(block, (_to_blocks(q), starts)))
    o = _rmsnorm(o, subln) * (1.0 - lambda_init)
    return o.reshape(b, s, h * 2 * dh) @ w_o

def _sqrelu_mlp(x, w_up, w_down):
    return jnp.square(jax.nn.relu(x @ w_up)) @ w_down

def first_inputs(seed: int = 0) -> dict:
    key = jax.random.key(seed)
    ks = jax.random.split(key, 24)
    f32 = jnp.float32
    nrm = lambda k, shape, scale: jax.random.normal(k, shape, f32) * scale
    na, nd, L = N_MLA_LAYERS, N_DIFF_LAYERS, DEPTH
    x = jax.random.normal(ks[0], (BATCH, SEQ, D_MODEL), f32)
    offsets = jax.random.randint(ks[1], (BATCH, 1), 0, 4096, dtype=jnp.int32)
    positions = (jnp.arange(SEQ, dtype=jnp.int32)[None, :] + offsets).astype(jnp.int32)
    return {
        "x": x,
        "positions": positions,
        "ln_mix_g": 1.0 + nrm(ks[2], (L, D_MODEL), 0.02),
        "ln_mix_b": nrm(ks[3], (L, D_MODEL), 0.02),
        "mla_w_dq": nrm(ks[4], (na, D_MODEL, MLA_Q_LORA), D_MODEL ** -0.5),
        "mla_q_norm": 1.0 + nrm(ks[5], (na, MLA_Q_LORA), 0.02),
        "mla_w_uq": nrm(ks[6], (na, MLA_Q_LORA, MLA_HEADS * (MLA_NOPE + MLA_ROPE)), MLA_Q_LORA ** -0.5),
        "mla_w_dkv": nrm(ks[7], (na, D_MODEL, MLA_KV_LORA + MLA_ROPE), D_MODEL ** -0.5),
        "mla_kv_norm": 1.0 + nrm(ks[8], (na, MLA_KV_LORA), 0.02),
        "mla_w_ukv": nrm(ks[9], (na, MLA_KV_LORA, MLA_HEADS * (MLA_NOPE + MLA_V)), MLA_KV_LORA ** -0.5),
        "mla_w_o": nrm(ks[10], (na, MLA_HEADS * MLA_V, D_MODEL), DEEPNORM_BETA * (MLA_HEADS * MLA_V) ** -0.5),
        "diff_w_qkv": nrm(ks[11], (nd, D_MODEL, 3 * DIFF_HEADS * 2 * DIFF_HEAD_DIM), D_MODEL ** -0.5),
        "diff_lambda_q1": nrm(ks[12], (nd, DIFF_HEAD_DIM), 0.1),
        "diff_lambda_k1": nrm(ks[13], (nd, DIFF_HEAD_DIM), 0.1),
        "diff_lambda_q2": nrm(ks[14], (nd, DIFF_HEAD_DIM), 0.1),
        "diff_lambda_k2": nrm(ks[15], (nd, DIFF_HEAD_DIM), 0.1),
        "diff_subln": 1.0 + nrm(ks[16], (nd, 2 * DIFF_HEAD_DIM), 0.02),
        "diff_w_o": nrm(ks[17], (nd, DIFF_HEADS * 2 * DIFF_HEAD_DIM, D_MODEL), DEEPNORM_BETA * D_MODEL ** -0.5),
        "ln_ffn_g": 1.0 + nrm(ks[18], (L, D_MODEL), 0.02),
        "ln_ffn_b": nrm(ks[19], (L, D_MODEL), 0.02),
        "ffn_w_up": nrm(ks[20], (L, D_MODEL, D_FF), D_MODEL ** -0.5),
        "ffn_w_down": nrm(ks[21], (L, D_FF, D_MODEL), DEEPNORM_BETA * D_FF ** -0.5),
    }

def first_block(x, positions, ln_mix_g, ln_mix_b, mla_w_dq, mla_q_norm, mla_w_uq, mla_w_dkv,
              mla_kv_norm, mla_w_ukv, mla_w_o, diff_w_qkv, diff_lambda_q1, diff_lambda_k1,
              diff_lambda_q2, diff_lambda_k2, diff_subln, diff_w_o, ln_ffn_g, ln_ffn_b,
              ffn_w_up, ffn_w_down):
    for i in range(DEPTH):
        j = i // N_MIXERS
        if i % N_MIXERS == 0:
            m = _mla(x, positions, mla_w_dq[j], mla_q_norm[j], mla_w_uq[j], mla_w_dkv[j],
                     mla_kv_norm[j], mla_w_ukv[j], mla_w_o[j])
        else:
            lambda_init = 0.8 - 0.6 * math.exp(-0.3 * i)
            m = _diff_attn(x, positions, diff_w_qkv[j], diff_lambda_q1[j], diff_lambda_k1[j],
                           diff_lambda_q2[j], diff_lambda_k2[j], diff_subln[j], diff_w_o[j],
                           lambda_init)
        x = _layernorm(DEEPNORM_ALPHA * x + m, ln_mix_g[i], ln_mix_b[i])
        x = _layernorm(DEEPNORM_ALPHA * x + _sqrelu_mlp(x, ffn_w_up[i], ffn_w_down[i]),
                       ln_ffn_g[i], ln_ffn_b[i])
    return x


CHUNK = 64
FOX_HEADS = 8
FOX_HEAD_DIM = D_MODEL // FOX_HEADS
RET_HEADS = 4
RET_QK_DIM = D_MODEL // RET_HEADS
RET_V_DIM = 2 * D_MODEL // RET_HEADS
D_FF_2 = -(-8 * D_MODEL // (3 * 256)) * 256
ROPE_BASE = 10000.0
EPS = 1e-6
N_FOX_LAYERS = (DEPTH + 1) // 2
N_RET_LAYERS = DEPTH // 2


def rmsnorm(x, g):
    xf = x.astype(jnp.float32)
    y = xf * lax.rsqrt(jnp.mean(xf * xf, axis=-1, keepdims=True) + EPS)
    return (y * g.astype(jnp.float32)).astype(x.dtype)

def forgetting_attention(h, w_in, b_f, w_out):
    B, S, _ = h.shape
    H, dh = FOX_HEADS, FOX_HEAD_DIM
    proj = h @ w_in
    q = proj[..., :D_MODEL].reshape(B, S, H, dh).transpose(0, 2, 1, 3)
    k = proj[..., D_MODEL:2 * D_MODEL].reshape(B, S, H, dh).transpose(0, 2, 1, 3)
    v = proj[..., 2 * D_MODEL:3 * D_MODEL].reshape(B, S, H, dh).transpose(0, 2, 1, 3)
    log_f = jax.nn.log_sigmoid((proj[..., 3 * D_MODEL:] + b_f).astype(jnp.float32))
    c = jnp.cumsum(log_f, axis=1).transpose(0, 2, 1)
    nb = S // Q_BLOCK
    qb = q.reshape(B, H, nb, Q_BLOCK, dh).transpose(2, 0, 1, 3, 4)
    cb = c.reshape(B, H, nb, Q_BLOCK).transpose(2, 0, 1, 3)
    pos = jnp.arange(S)
    qpos = pos.reshape(nb, Q_BLOCK)
    scale = dh ** -0.5

    def block(args):
        qi, ci, pi = args
        s = jnp.einsum('bhqd,bhkd->bhqk', qi, k).astype(jnp.float32) * scale
        s = s + (ci[..., :, None] - c[:, :, None, :])
        s = jnp.where(pi[:, None] >= pos[None, :], s, -jnp.inf)
        p = jax.nn.softmax(s, axis=-1).astype(v.dtype)
        return jnp.einsum('bhqk,bhkd->bhqd', p, v)

    o = lax.map(block, (qb, cb, qpos))
    o = o.transpose(1, 0, 3, 2, 4).reshape(B, S, H * dh)
    return o @ w_out

def rotate(t, cos, sin):
    half = t.shape[-1] // 2
    t1, t2 = t[..., :half], t[..., half:]
    return jnp.concatenate([t1 * cos - t2 * sin, t1 * sin + t2 * cos], axis=-1)

def retention(h, w_in, w_out):
    B, S, _ = h.shape
    H, dk, dv, C = RET_HEADS, RET_QK_DIM, RET_V_DIM, CHUNK
    N = S // C
    proj = h @ w_in
    q = proj[..., :D_MODEL].reshape(B, S, H, dk)
    k = proj[..., D_MODEL:2 * D_MODEL].reshape(B, S, H, dk)
    v = proj[..., 2 * D_MODEL:4 * D_MODEL].reshape(B, S, H, dv)
    g = proj[..., 4 * D_MODEL:]
    half = dk // 2
    inv = ROPE_BASE ** (-jnp.arange(half, dtype=jnp.float32) / half)
    ang = jnp.arange(S, dtype=jnp.float32)[:, None] * inv[None, :]
    cos, sin = jnp.cos(ang)[:, None, :], jnp.sin(ang)[:, None, :]
    q = rotate(q.astype(jnp.float32), cos, sin)
    k = rotate(k.astype(jnp.float32), cos, sin) * (dk ** -0.5)
    v = v.astype(jnp.float32)
    log_gamma = jnp.log(jnp.asarray(1.0 - 2.0 ** (-5.0 - np.arange(H)), dtype=jnp.float32))
    idx = jnp.arange(C, dtype=jnp.float32)
    d_intra = jnp.exp(log_gamma[:, None, None] * jnp.abs(idx[:, None] - idx[None, :]))
    q_decay = jnp.exp(log_gamma[:, None] * (idx[None, :] + 1.0))
    k_decay = jnp.exp(log_gamma[:, None] * (C - 1.0 - idx[None, :]))
    chunk_decay = jnp.exp(log_gamma * C)
    to_chunks = lambda t: t.reshape(B, N, C, H, t.shape[-1]).transpose(1, 0, 3, 2, 4)
    qc, kc, vc = to_chunks(q), to_chunks(k), to_chunks(v)

    def step(state, inp):
        qi, ki, vi = inp
        a = jnp.einsum('bhid,bhjd->bhij', qi, ki) * d_intra
        inner = jnp.einsum('bhij,bhjv->bhiv', a, vi)
        cross = jnp.einsum('bhid,bhdv->bhiv', qi, state) * q_decay[None, :, :, None]
        new_state = state * chunk_decay[None, :, None, None] + jnp.einsum(
            'bhjd,bhjv->bhdv', ki * k_decay[None, :, :, None], vi)
        return new_state, inner + cross

    state0 = jnp.zeros((B, H, dk, dv), jnp.float32)
    _, y = lax.scan(step, state0, (qc, kc, vc))
    y = y.transpose(1, 0, 3, 2, 4).reshape(B, S, H, dv)
    mu = jnp.mean(y, axis=-1, keepdims=True)
    var = jnp.mean(jnp.square(y - mu), axis=-1, keepdims=True)
    y = ((y - mu) * lax.rsqrt(var + EPS)).reshape(B, S, H * dv).astype(h.dtype)
    return (jax.nn.silu(g) * y) @ w_out

def swiglu(h, w_in, w_out):
    gu = h @ w_in
    return (jax.nn.silu(gu[..., :D_FF_2]) * gu[..., D_FF_2:]) @ w_out

def second_inputs(seed: int = 0) -> dict:
    key = jax.random.key(seed)
    ks = jax.random.split(key, 12)
    f32 = jnp.float32
    x = jax.random.normal(ks[0], (BATCH, SEQ, D_MODEL), f32)
    norm_mix = 1.0 + 0.02 * jax.random.normal(ks[1], (DEPTH, D_MODEL), f32)
    norm_ffn = 1.0 + 0.02 * jax.random.normal(ks[2], (DEPTH, D_MODEL), f32)
    fox_w_in = jax.random.normal(ks[3], (N_FOX_LAYERS, D_MODEL, 3 * D_MODEL + FOX_HEADS), f32) * D_MODEL ** -0.5
    fox_b_f = 3.0 + 0.5 * jax.random.normal(ks[4], (N_FOX_LAYERS, FOX_HEADS), f32)
    fox_w_out = jax.random.normal(ks[5], (N_FOX_LAYERS, D_MODEL, D_MODEL), f32) * D_MODEL ** -0.5
    ret_w_in = jax.random.normal(ks[6], (N_RET_LAYERS, D_MODEL, 6 * D_MODEL), f32) * D_MODEL ** -0.5
    ret_w_out = jax.random.normal(ks[7], (N_RET_LAYERS, 2 * D_MODEL, D_MODEL), f32) * (2 * D_MODEL) ** -0.5
    ffn_w_in = jax.random.normal(ks[8], (DEPTH, D_MODEL, 2 * D_FF_2), f32) * D_MODEL ** -0.5
    ffn_w_out = jax.random.normal(ks[9], (DEPTH, D_FF_2, D_MODEL), f32) * D_FF_2 ** -0.5
    final_norm = 1.0 + 0.02 * jax.random.normal(ks[10], (D_MODEL,), f32)
    return {"x": x, "norm_mix": norm_mix, "norm_ffn": norm_ffn,
            "fox_w_in": fox_w_in, "fox_b_f": fox_b_f, "fox_w_out": fox_w_out,
            "ret_w_in": ret_w_in, "ret_w_out": ret_w_out,
            "ffn_w_in": ffn_w_in, "ffn_w_out": ffn_w_out, "final_norm": final_norm}

def second_block(x, norm_mix, norm_ffn, fox_w_in, fox_b_f, fox_w_out, ret_w_in, ret_w_out,
              ffn_w_in, ffn_w_out, final_norm):
    for i in range(DEPTH):
        h = rmsnorm(x, norm_mix[i])
        j = i // N_MIXERS
        if i % N_MIXERS == 0:
            x = x + forgetting_attention(h, fox_w_in[j], fox_b_f[j], fox_w_out[j])
        else:
            x = x + retention(h, ret_w_in[j], ret_w_out[j])
        h = rmsnorm(x, norm_ffn[i])
        x = x + swiglu(h, ffn_w_in[i], ffn_w_out[i])
    return rmsnorm(x, final_norm)


def setup_inputs(seed=0):
    out = dict(first_inputs(seed))
    for name, value in second_inputs(seed + 1).items():
        if name != "x":
            out[name + "_2"] = value
    return out


def reference(
    x, positions, ln_mix_g, ln_mix_b, mla_w_dq, mla_q_norm, mla_w_uq, mla_w_dkv, mla_kv_norm,
    mla_w_ukv, mla_w_o, diff_w_qkv, diff_lambda_q1, diff_lambda_k1, diff_lambda_q2,
    diff_lambda_k2, diff_subln, diff_w_o, ln_ffn_g, ln_ffn_b, ffn_w_up, ffn_w_down, norm_mix_2,
    norm_ffn_2, fox_w_in_2, fox_b_f_2, fox_w_out_2, ret_w_in_2, ret_w_out_2, ffn_w_in_2,
    ffn_w_out_2, final_norm_2,
):
    x = first_block(
        x, positions, ln_mix_g, ln_mix_b, mla_w_dq, mla_q_norm, mla_w_uq, mla_w_dkv,
        mla_kv_norm, mla_w_ukv, mla_w_o, diff_w_qkv, diff_lambda_q1, diff_lambda_k1,
        diff_lambda_q2, diff_lambda_k2, diff_subln, diff_w_o, ln_ffn_g, ln_ffn_b, ffn_w_up,
        ffn_w_down,
    )
    return second_block(
        x, norm_mix_2, norm_ffn_2, fox_w_in_2, fox_b_f_2, fox_w_out_2, ret_w_in_2, ret_w_out_2,
        ffn_w_in_2, ffn_w_out_2, final_norm_2,
    )


_drawn_inputs = setup_inputs


def setup_inputs(seed=0):
    import zlib

    import numpy as np

    out = dict(_drawn_inputs(seed))
    spreads = {}
    factors = {'mla_q_norm': 8.0,
     'mla_kv_norm': 8.0,
     'diff_lambda_q2': 8.0,
     'diff_subln': 5.651,
     'final_norm_2': 23.687,
     'norm_ffn_2': 2.692,
     'norm_mix_2': 2.89}
    for name, (base, spread) in spreads.items():
        noise = np.random.default_rng([zlib.crc32(name.encode()), seed]).standard_normal(out[name].shape)
        drawn = base * np.exp(spread * noise) if base else spread * noise
        out[name] = __import__('jax').numpy.asarray(drawn.astype(out[name].dtype))
    for name, factor in factors.items():
        out[name] = (out[name] * factor).astype(out[name].dtype)
    return out
```

```python
import math
from contextlib import ExitStack

import concourse.bass as bass
import numpy as np
from concourse import mybir

F32 = mybir.dt.float32
F32R = mybir.dt.float32r
I32 = mybir.dt.int32
ACT = mybir.ActivationFunctionType
ALU = mybir.AluOpType
AX = mybir.AxisListType.X

P = 128
T = 512
TT = T // P
D = 1024
KC = D // P
PAIRS = 4
NOPE, ROPE, MV = 128, 64, 128
QL, KVL = 384, 256
FF = 4096
G1 = FF // 256
FF2 = 2816
G2 = FF2 // 256
RH, RDK, RDV = 4, 256, 512
ALPHA = 4 ** 0.25
LN_EPS, RMS_EPS = 1e-5, 1e-6
LAMBDA_INIT = 0.8 - 0.6 * math.exp(-0.3)
MLA_SCALE = (NOPE + ROPE) ** -0.5
DIFF_SCALE = 64 ** -0.5
FOX_SCALE = 128 ** -0.5
RET_SCALE = RDK ** -0.5
SLOT = 3 * 384 + 2 * 512
MASKED = -1e30
TWO_PI = (6.28125, 0.0019340515136718750, 2 * math.pi - 6.28125 - 0.0019340515136718750)
ROUND = 12582912.0

ROWS = {}
for _name, _n in (("ln_mix_g", 16), ("ln_mix_b", 16), ("ln_ffn_g", 16), ("ln_ffn_b", 16), ("norm_mix_2", 16),
                  ("norm_ffn_2", 16), ("mla_q_norm", 3), ("mla_kv_norm", 2), ("diff_subln", 1)):
    ROWS[_name] = (sum(n for _, n in ROWS.values()), _n)
NROWS = sum(n for _, n in ROWS.values())

PLAIN_SCORES = [(q, [(q, 0, 0)]) for q in range(TT)]
DIFF_SCORES = [(1, [(0, 0, 384), (2, 0, 0)]), (4, [(0, 1, 384), (2, 1, 0)]), (2, [(1, 0, 0), (1, 1, 256)]),
               (0, [(3, 0, 0)]), (3, [(3, 1, 0)])]
TURN_AT = {0: (0, 0), 1: (1, 0), 3: (1, 384), 2: (2, 0)}
TURNED = {kb: 512 * b + c for kb, (b, c) in TURN_AT.items()}
PACKED = {q: P * (q * (q + 1) // 2) for q in range(TT)}


def score_tiles(t):
    tiles = []
    for bank, places in DIFF_SCORES if t == "diff" else PLAIN_SCORES:
        end = len(tiles) + len(places)
        tiles += [(q, n, bank, at, end) for q, n, at in places]
    return tiles


def along(i, counts):
    counts = list(counts)
    if i is None:
        assert len(counts) == 1
        return counts[0]
    step = counts[1] - counts[0]
    assert counts == [counts[0] + step * n for n in range(len(counts))] and counts[0] > 0
    return i * step + counts[0] if step else counts[0]


def plan():
    units, blocks = [], []

    def unit(name, dmas=1):
        units.append((name, dmas))

    def done(name, *parts):
        blocks.extend((name, x) for x in parts)

    unit("kv"), done("kv", 0, 1)
    unit("pe", 3), done("pe", 0, 1)
    unit("cq"), done("cq", 0, 1)
    for p in range(PAIRS + 1):
        if p < PAIRS:
            unit(f"mla.p{p}", 5), done(f"mla.p{p}", "q0", "k0", "q1", "k1", "pe", "v0", "v1", "v2", "v3")
        if p:
            unit(f"mla.o{p - 1}"), done(f"mla.o{p - 1}", *range(KC))

    def relu_mlp(t):
        for g in range(G1 + 1):
            if g < G1:
                unit(f"{t}.u{g}"), done(f"{t}.u{g}", 0, 1)
            if g:
                unit(f"{t}.d{g - 1}"), done(f"{t}.d{g - 1}", *range(KC))

    def pairs(t):
        for p in range(PAIRS + 1):
            if p < PAIRS:
                unit(f"{t}.q{p}"), unit(f"{t}.k{p}"), unit(f"{t}.v{p}")
                for j in range(2):
                    done(f"{t}.q{p}", j), done(f"{t}.k{p}", j)
                done(f"{t}.v{p}", *range(TT))
            if p:
                unit(f"{t}.o{p - 1}"), done(f"{t}.o{p - 1}", *range(KC))

    def swiglu(t):
        for g in range(G2 + 1):
            if g < G2:
                unit(f"{t}.g{g}"), done(f"{t}.g{g}", 0, 1)
                unit(f"{t}.u{g}"), done(f"{t}.u{g}", 0, 1)
            if g:
                unit(f"{t}.d{g - 1}"), done(f"{t}.d{g - 1}", *range(KC))

    relu_mlp("ffn0")
    pairs("diff")
    relu_mlp("ffn1")
    pairs("fox")
    swiglu("sw0")
    for h in range(RH + 1):
        if h < RH:
            for x in "qk":
                unit(f"ret.{x}{h}"), done(f"ret.{x}{h}", 0, 1)
            for x in "vg":
                for half in range(2):
                    unit(f"ret.{x}{half}{h}"), done(f"ret.{x}{half}{h}", *range(TT))
        if h:
            for half in range(2):
                unit(f"ret.o{half}{h - 1}"), done(f"ret.o{half}{h - 1}", *range(4))
    swiglu("sw1")
    return units, blocks


UNITS, BLOCKS = plan()
NU = len(UNITS)
INDEX = {name: n for n, (name, _) in enumerate(UNITS)}
BLOCK = {b: n + 1 for n, b in enumerate(BLOCKS)}
UNIT_DONE = {}
for (_name, _), _n in BLOCK.items():
    UNIT_DONE[_name] = max(_n, UNIT_DONE.get(_name, 0))
LANDED, _sum = [], [0, 0]
for _n, (_name, _dmas) in enumerate(UNITS):
    _sum[_n % 2] += 16 * _dmas
    LANDED.append(_sum[_n % 2])

HEADS = 2 * PAIRS
ONCE_PER_HEAD = {"q_in": HEADS, "k_in": HEADS, "o_hi": HEADS, "o_lo": HEADS, "row_rec": HEADS, "values": HEADS,
                 "turned": 3 * HEADS, "turned_in": 3 * HEADS, "probs": TT * HEADS, "v_in": TT * PAIRS, "acc": KC * PAIRS}
SHARED = [
    ("layernorm", ("ln0", "ln1", "ln2", "ln3"),
     {"summed": KC, "mean": 1, "centered": KC, "sq": KC, "sums": 1, "std": 1, "rcol": 1, "diag": TT, "spread": 1,
      "scaled": KC, "done": KC}),
    ("input", ("mla", "ffn0", "diff", "ffn1", "fox", "sw0", "ret", "sw1"), {"h_hi": KC, "h_lo": KC}),
    ("rms", ("fox", "sw0", "ret", "sw1", "out"),
     {"sq": KC, "norm_sums": 1, "norm_std": 1, "norm_rcol": 1, "norm_diag": TT, "norm_spread": 1, "norm_in": 1}),
    ("relu_mlp", ("ffn0", "ffn1"), {"relu": 2 * G1, "squared": 2 * G1, "a_hi": 2 * G1, "a_lo": 2 * G1, "acc": KC * G1}),
    ("swiglu", ("sw0", "sw1"), {"g_in": 2 * G2, "u_in": 2 * G2, "silu": 2 * G2, "prod": 2 * G2, "a_hi": 2 * G2,
                                "a_lo": 2 * G2, "acc": KC * G2}),
    ("softmax", ("mla", "diff", "fox"), ONCE_PER_HEAD),
    ("rope", ("mla", "diff"), {"rope_steps": 8, "rope_abs": 1, "rope_made": 2}),
]
COUNTED = {f"{stage}_{event}": (f"{kind}_{event}", total * n)
           for kind, stages, events in SHARED for n, stage in enumerate(stages) for event, total in events.items()}
for _event in ("scores", "masked", "neg_max", "exps"):
    for _stage, _n in (("mla", 0), ("diff", 1), ("fox", 3)):
        COUNTED[f"{_stage}_{_event}"] = (f"softmax_{_event}", _n * TT * HEADS)


def slot(names):
    s = {INDEX[n] % 2 for n in names}
    assert len(s) == 1
    return s.pop()


def block_done(i, names, part):
    return along(i, [BLOCK[n, part] for n in names])


def after(names, by=1):
    return [UNITS[INDEX[n] + by][0] for n in names]


class Memory:

    def __init__(self, nc, dram):
        self.nc, self.dram = nc, dram


def memory(nc, ctx, dram):
    def sb(name, shape, dt=F32):
        return ctx.enter_context(nc.sbuf_tensor(name, shape, dt))

    m = Memory(nc, dram)
    sems = {}

    def sem(name):
        name = COUNTED.get(name, (name, 0))[0]
        if name not in sems:
            sems[name] = ctx.enter_context(nc.semaphore(name))
        return sems[name]

    def upto(name, n):
        return sem(name), n + COUNTED.get(name, (name, 0))[1]

    m.sem, m.upto = sem, upto
    m.bank = [ctx.enter_context(nc.psum_tensor(f"bank{n}", [P, 512], F32)) for n in range(8)]

    m.w_raw, m.w_hi, m.w_lo = sb("w_raw", [P, 2, SLOT]), sb("w_hi", [P, 2, SLOT], F32R), sb("w_lo", [P, 2, SLOT], F32R)
    m.x = sb("x_residual", [P, KC, T])
    m.h_hi, m.h_lo = sb("h_hi", [P, KC, T], F32R), sb("h_lo", [P, KC, T], F32R)
    m.act_hi, m.act_lo = sb("act_hi", [P, 7, T], F32R), sb("act_lo", [P, 7, T], F32R)
    tok = sb("tokbuf", [P, KC * T])
    m.x_tok = tok[:, :].rearrange("p (t d) -> p t d", t=TT)
    m.sq = tok[:, :].rearrange("p (k t) -> p k t", k=KC)
    m.neg_c = m.sq
    m.decay = tok[:, 0:RH * T].rearrange("p (h t) -> p h t", h=RH)
    m.ret_cos, m.ret_sin = tok[:, RH * T:RH * T + T], tok[:, RH * T + T:RH * T + 2 * T]
    m.ret_tables = tok[:, 0:(RH + 2) * T]

    work = sb("work", [P, 11520])

    def view(at, n, a=None):
        w = work[:, at:at + n]
        return w if a is None else w.rearrange("p (a b) -> p a b", a=a)

    m.rows = view(0, P)
    m.q, m.k, m.v = view(0, 1024, 2), view(1024, 1024, 2), view(2048, 1024, TT)
    m.q_pe, m.k_pe = view(3072, 512), view(3584, 512)
    m.probs, m.probs2, m.turned = view(4096, 1280), view(5376, 1280), view(6656, 1280)
    m.tmp = view(7936, 1536, 3)
    m.sel, m.c_rows = view(5376, 1024, 8), view(3584, 512)
    m.rv, m.rg, m.ra, m.ry, m.rtmp = view(2048, 2048, TT), view(4096, 2048, TT), view(6144, 1280), view(7424, 2048, TT), view(9472, 2048, 4)
    m.relu, m.square = view(0, 1024, 2), view(1024, 1024, 2)
    m.gate, m.silu, m.up, m.prod = view(0, 1024, 2), view(1024, 1024, 2), view(2048, 1024, 2), view(3072, 1024, 2)
    m.rb_q = view(9472, 512)
    m.pos, m.ang, m.turns = view(9984, 512), view(10496, 512), view(11008, 512)

    m.rb = sb("rstd_rows", [P, T])
    m.diag = sb("diag", [P, TT, P])
    m.rope_cos, m.rope_sin = sb("rope_cos", [P, T]), sb("rope_sin", [P, T])
    m.gain_final = sb("gain_final", [P, D])
    m.consts = sb("consts", [P, 3 * P + 4])
    m.ident, m.causal, m.tri = (m.consts[:, P * n:P * n + P] for n in range(3))
    m.rope_cols = m.consts[:, 3 * P:3 * P + 4]
    m.ones, m.mean_w = sb("ones", [P, P]), sb("mean_weights", [P, P])
    m.cols = sb("cols", [P, NROWS])
    m.eps = sb("eps", [P, 3])
    m.std, m.rcol = sb("std", [P, 2 * TT]), sb("rstd_cols", [P, 2 * TT])
    m.neg_max, m.row_sum, m.row_rec = sb("neg_max", [P, 8]), sb("row_sum", [P, 8]), sb("row_rec", [P, 8])
    m.lam_in, m.lam = sb("lam_in", [P, 4, 64]), sb("lam", [P, 8])
    m.wf, m.wf_hi, m.wf_lo = sb("wf", [P, KC, 8]), sb("wf_hi", [P, KC, 8], F32R), sb("wf_lo", [P, KC, 8], F32R)
    m.b_f, m.gate_f, m.c_cols = sb("b_f", [P, 8]), sb("gate_f", [P, 6, TT, 8]), sb("c_cols", [P, TT, 8])
    m.y_stats, m.y_mean = sb("y_stats", [P, TT, 6]), sb("y_mean", [P, TT, 2])
    m.y_std, m.y_rstd, m.y_shift = sb("y_std", [P, TT]), sb("y_rstd", [P, TT]), sb("y_shift", [P, TT])
    return m


def col(m, name, n):
    at = ROWS[name][0] + n
    return m.cols[:, at:at + 1]


def weight(m, names, width, kc):
    s = slot(names)
    return tuple(w[:, s, 0:width].rearrange("p (k n) -> p k n", k=kc) for w in (m.w_hi, m.w_lo))


def sp_program(m, sp):
    d, s = m.dram, m.sem

    def raw(names, at, width, kc=None):
        v = m.w_raw[:, slot(names), at:at + width]
        return v.rearrange("p (k n) -> p k n", k=kc) if kc else v

    def load(names, parts, i=None):
        if INDEX[names[0]] >= 2:
            sp.wait_ge(*m.upto("w_lo_ready", along(i, [INDEX[n] - 1 for n in names])))
        for dst, src in parts:
            sp.dma_start(dst, src).then_inc(s(f"w_landed{slot(names)}"), 16)

    def cols(w, first, n):
        return w.rearrange("(k p) n -> p k n", p=P)[:, :, bass.ds(first, n)]

    def rows(w, first, n, c0=0, c1=D):
        return w.rearrange("(k p) n -> p k n", p=P)[:, bass.ds(first, n), c0:c1]

    def wide(names, w, firsts, i=None):
        load(names, [(raw(names, 0, 2048, KC), cols(w, along(i, firsts) if i is not None else firsts[0], 256))], i)

    def tall(names, w, firsts, i=None):
        load(names, [(raw(names, 0, 2048, 2), rows(w, along(i, firsts) if i is not None else firsts[0], 2))], i)

    sp.dma_start(m.consts[:, :], d["c_square"]).then_inc(s("consts_in"), 16)
    for t in range(TT):
        sp.dma_start(m.x_tok[:, t, :], d["x"][0, t * P:(t + 1) * P, :]).then_inc(s("x_in"), 16)
    wide(["kv"], d["mla_w_dkv"][0], [0])
    pe_cols = m.w_raw[:, slot(["pe"]), 0:2048].rearrange("p (k n) -> p k n", k=KC)
    load(["pe"], [(pe_cols[:, :, 0:64], cols(d["mla_w_dkv"][0], KVL, ROPE)),
                  (pe_cols[:, :, 64:128], cols(d["mla_w_dkv"][0], KVL, ROPE)),
                  (pe_cols[:, :, 128:256], cols(d["mla_w_dq"][0], 0, P))])
    for name, (at, n) in ROWS.items():
        v = d[name]
        v = v.rearrange("l (k p) -> (l k) p", p=P)
        sp.dma_start(m.rows[at:at + n, :], v).then_inc(s("rows_in"), 16)
    sp.dma_start(m.pos.bitcast(I32), d["positions"].broadcast_to([P, T])).then_inc(s("pos_in"), 16)
    wide(["cq"], d["mla_w_dq"][0], [P])

    def mla_pair(p):
        n = [f"mla.p{p}"]
        uq = raw(n, 0, 1152, 3)
        parts = [(uq[:, :, at:at + width], cols(d["mla_w_uq"][0], p * 2 * (NOPE + ROPE) + first, width)) for at, first, width in
                 ((0, 0, NOPE), (NOPE, NOPE + ROPE, NOPE), (2 * NOPE, NOPE, ROPE), (2 * NOPE + ROPE, 2 * NOPE + ROPE, ROPE))]
        load(n, parts + [(raw(n, 1152, 1024, 2), cols(d["mla_w_ukv"][0], p * 512, 512))])

    mla_pair(0)
    for n, x in enumerate(("q1", "k1", "q2", "k2")):
        sp.dma_start(m.lam_in[:, n, :], d[f"diff_lambda_{x}"].broadcast_to([P, 64])).then_inc(s("lam_in"), 16)
    sp.dma_start(m.wf[:, :, :], cols(d["fox_w_in_2"][0], 3 * D, 8)).then_inc(s("wf_in"), 16)
    sp.dma_start(m.b_f[:, :], d["fox_b_f_2"].broadcast_to([P, 8])).then_inc(s("wf_in"), 16)
    sp.dma_start(m.gain_final[:, :], d["final_norm_2"].rearrange("(a n) -> a n", a=1).broadcast_to([P, D]))\
        .then_inc(s("gain_in"), 16)
    for p in range(1, PAIRS):
        mla_pair(p)
        tall([f"mla.o{p - 1}"], d["mla_w_o"][0], [2 * p - 2])
    tall([f"mla.o{PAIRS - 1}"], d["mla_w_o"][0], [2 * PAIRS - 2])

    def relu_mlp(t, layer, before_loop=None):
        up, down = d["ffn_w_up"][layer], d["ffn_w_down"][layer]
        wide([f"{t}.u0"], up, [0])
        if before_loop:
            before_loop()
        with sp.Fori(0, G1 - 1) as i:
            gs = range(G1 - 1)
            wide([f"{t}.u{g + 1}" for g in gs], up, [256 * (g + 1) for g in gs], i)
            load([f"{t}.d{g}" for g in gs], [(raw([f"{t}.d{g}" for g in gs], 0, 2048, 2), rows(down, i * 2, 2))], i)
        tall([f"{t}.d{G1 - 1}"], down, [2 * (G1 - 1)])

    def pairs(t, w_in, w_out):
        for n, x in enumerate("qkv"):
            wide([f"{t}.{x}0"], w_in, [D * n])
        with sp.Fori(0, PAIRS - 1) as i:
            ps = range(1, PAIRS)
            for n, x in enumerate("qkv"):
                wide([f"{t}.{x}{p}" for p in ps], w_in, [D * n + 256 * p for p in ps], i)
            names = [f"{t}.o{p - 1}" for p in ps]
            load(names, [(raw(names, 0, 2048, 2), rows(w_out, i * 2, 2))], i)
        tall([f"{t}.o{PAIRS - 1}"], w_out, [2 * (PAIRS - 1)])

    def swiglu(t, layer):
        w_in, w_out = d["ffn_w_in_2"][layer], d["ffn_w_out_2"][layer]
        wide([f"{t}.g0"], w_in, [0])
        wide([f"{t}.u0"], w_in, [FF2])
        with sp.Fori(0, (G2 - 1) // 2) as i:
            for e in range(2):
                gs = range(1 + e, G2, 2)
                wide([f"{t}.g{g}" for g in gs], w_in, [256 * g for g in gs], i)
                wide([f"{t}.u{g}" for g in gs], w_in, [FF2 + 256 * g for g in gs], i)
                names = [f"{t}.d{g - 1}" for g in gs]
                load(names, [(raw(names, 0, 2048, 2), rows(w_out, i * 4 + 2 * e, 2))], i)
        tall([f"{t}.d{G2 - 1}"], w_out, [2 * (G2 - 1)])

    def positions_again():
        sp.wait_ge(*m.upto("mla_rope_made", 2))
        sp.dma_start(m.pos.bitcast(I32), d["positions"].broadcast_to([P, T])).then_inc(s("pos_in"), 16)

    relu_mlp("ffn0", 0, positions_again)
    pairs("diff", d["diff_w_qkv"][0], d["diff_w_o"][0])
    relu_mlp("ffn1", 1)

    wide(["fox.q0"], d["fox_w_in_2"][0], [0])
    for n, x in enumerate("kv"):
        wide([f"fox.{x}0"], d["fox_w_in_2"][0], [D * (n + 1)])
    sp.wait_ge(*m.upto("diff_acc", 8 * PAIRS))
    sp.dma_start(m.sel[0:8, :, :], d["c_sel"]).then_inc(s("sel_in"), 16)
    with sp.Fori(0, PAIRS - 1) as i:
        ps = range(1, PAIRS)
        for n, x in enumerate("qkv"):
            wide([f"fox.{x}{p}" for p in ps], d["fox_w_in_2"][0], [D * n + 256 * p for p in ps], i)
        names = [f"fox.o{p - 1}" for p in ps]
        load(names, [(raw(names, 0, 2048, 2), rows(d["fox_w_out_2"][0], i * 2, 2))], i)
    tall([f"fox.o{PAIRS - 1}"], d["fox_w_out_2"][0], [2 * (PAIRS - 1)])

    swiglu("sw0", 0)

    w_in, w_out = d["ret_w_in_2"][0], d["ret_w_out_2"][0]

    def ret_head(hs, i=None):
        at = (lambda first, width: along(i, [first + width * h for h in hs]) if i is not None else first + width * hs[0])
        for n, x in enumerate("qk"):
            names = [f"ret.{x}{h}" for h in hs]
            load(names, [(raw(names, 0, 2048, KC), cols(w_in, at(D * n, RDK), 256))], i)
        for n, x in enumerate("vg"):
            for half in range(2):
                names = [f"ret.{x}{half}{h}" for h in hs]
                load(names, [(raw(names, 0, 2048, KC), cols(w_in, at(2 * D + 2 * D * n + 256 * half, RDV), 256))], i)

    def ret_out(hs, i=None):
        for half in range(2):
            names = [f"ret.o{half}{h}" for h in hs]
            first = i * 4 if i is not None else 4 * hs[0]
            load(names, [(raw(names, 0, 2048, 4), rows(w_out, first, 4, 512 * half, 512 * half + 512))], i)

    load(["ret.q0"], [(raw(["ret.q0"], 0, 2048, KC), cols(w_in, 0, 256))])
    for name, first in (("k0", D), ("v00", 2 * D)):
        wide([f"ret.{name}"], w_in, [first])
    sp.wait_ge(*m.upto("ret_norm_sums", 1))
    sp.dma_start(m.ret_tables, d["c_ret"]).then_inc(s("ret_tables_in"), 16)
    for name, first in (("v10", 2 * D + 256), ("g00", 4 * D), ("g10", 4 * D + 256)):
        wide([f"ret.{name}"], w_in, [first])
    with sp.Fori(0, RH - 1) as i:
        ret_head(range(1, RH), i)
        ret_out(range(RH - 1), i)
    ret_out([RH - 1])
    swiglu("sw1", 1)

    for t in range(TT):
        sp.wait_ge(*m.upto("out_rows", 2 * (t + 1)))
        sp.dma_start(d["out"][0, t * P:(t + 1) * P, :], m.x_tok[:, t, :]).then_inc(s("out_stored"), 16)
    sp.wait_ge(*m.upto("out_stored", 16 * TT))


def pool_program(m, pool):
    s, nc = m.sem, m.nc

    def split_low(n, sl, width):
        pool.wait_ge(*m.upto("w_hi_ready", n))
        nc.gpsimd.tensor_tensor(m.w_lo[:, sl, 0:width], m.w_raw[:, sl, 0:width], m.w_hi[:, sl, 0:width].bitcast(F32),
                                ALU.subtract).then_inc(s("w_lo_ready"), 1)

    first_plain = INDEX["ffn0.u0"]
    for n in range(first_plain):
        split_low(n + 1, n % 2, SLOT if UNITS[n][0].startswith("mla.p") else 2048)
    split_low(first_plain + 1, first_plain % 2, 2048)
    rest = NU - first_plain - 1
    assert rest % 2 == 1
    with pool.Fori(0, rest // 2) as i:
        for e in range(2):
            split_low(i * 2 + (first_plain + 2 + e), (first_plain + 1 + e) % 2, 2048)
    split_low(NU, (NU - 1) % 2, 2048)


def pe_weights(m, pe, names, i=None):
    pe.wait_ge(*m.upto("w_lo_ready", along(i, [INDEX[n] + 1 for n in names])))


def pe_features(m, pe, out, w, c0, x, kc, ready=None):
    mm = m.nc.tensor.matmul
    for k in range(kc):
        if ready:
            ready(k)
        hi, lo = w[0][:, k, c0:c0 + P], w[1][:, k, c0:c0 + P]
        mm(out, hi, x[0][:, k, :], start=k == 0, stop=False)
        mm(out, hi, x[1][:, k, :], start=False, stop=False)
        last = mm(out, lo, x[0][:, k, :], start=False, stop=k == kc - 1)
    last.then_inc(m.sem("blocks_done"), 1)


def pe_tokens(m, pe, out, w, x, kc, t, n=256, c0=0):
    mm = m.nc.tensor.matmul
    for k in range(kc):
        hi, lo = x[0][:, k, t * P:(t + 1) * P], x[1][:, k, t * P:(t + 1) * P]
        mm(out, hi, w[0][:, k, c0:c0 + n], start=k == 0, stop=False)
        mm(out, hi, w[1][:, k, c0:c0 + n], start=False, stop=False)
        last = mm(out, lo, w[0][:, k, c0:c0 + n], start=False, stop=k == kc - 1)
    return last


def pe_sums(m, squares, out):
    for t in range(TT):
        for n, sq in enumerate(squares):
            last = m.nc.tensor.matmul(out[:, t:t + 1], sq[:, t * P:(t + 1) * P], m.ones[:, 0:1],
                                      start=n == 0, stop=n == len(squares) - 1)
    return last


def pe_spread(m, out):
    for t in range(TT):
        last = m.nc.tensor.matmul(out[:, t * P:(t + 1) * P], m.ones[:, :], m.diag[:, t, :], start=True, stop=True)
    return last


def h_ready(m, pe, t):
    def ready(k):
        pe.wait_ge(*m.upto(f"{t}_h_hi", k + 1))
        pe.wait_ge(*m.upto(f"{t}_h_lo", k + 1))
    return ready


def pe_start(m, pe):
    s, b, nc = m.sem, m.bank, m.nc
    h = (m.h_hi, m.h_lo)
    pe.wait_ge(*m.upto("consts_in", 16))
    pe.wait_ge(*m.upto("x_in", 16 * TT))
    for k in range(KC):
        for t in range(TT):
            last = nc.tensor.transpose(b[k][:, t * P:(t + 1) * P], m.x_tok[:, t, k * P:(k + 1) * P], m.ident)
        last.then_inc(s("x_turned"), 1)
    ready = h_ready(m, pe, "mla")
    for n, name in enumerate(("kv", "pe", "cq")):
        pe_weights(m, pe, [name])
        for j in range(2):
            k = 2 * n + j
            pe.wait_ge(*m.upto("mla_h_lo", k + 1))
            pe_features(m, pe, b[k][:, :], weight(m, [name], 2048, KC), j * P, h, KC, ready if k == 0 else None)
            if k == 0:
                pe.wait_ge(*m.upto("rows_in", 16 * len(ROWS)))
                pe.wait_ge(*m.upto("mla_h_lo", KC))
                nc.tensor.transpose(b[7][:, 0:NROWS], m.rows[0:NROWS, :], m.ident[0:NROWS, 0:NROWS]).then_inc(s("cols_turned"), 1)
    pe.wait_ge(*m.upto("set_up", 2))
    for n, (first, count) in enumerate(((0, 2), (2, 3))):
        pe.wait_ge(*m.upto("lat_lo", first + count))
        pe_sums(m, [m.sq[:, j, :] for j in range(first, first + count)], b[n][:, 0:TT]).then_inc(s("lat_sums"), 1)
    for n in range(2):
        pe.wait_ge(*m.upto("lat_diag", TT * (n + 1)))
        pe_spread(m, b[n]).then_inc(s("lat_spread"), 1)


def pe_turn(m, pe, t, c):
    s, b, nc = m.sem, m.bank, m.nc
    pe.wait_ge(*m.upto(f"{t}_probs", c(4, 4)))
    for kbs in ((0,), (1, 3), (2,)):
        for kb in kbs:
            bank, at = TURN_AT[kb]
            for q in range(kb, TT):
                src = m.probs[:, PACKED[q] + kb * P:PACKED[q] + kb * P + P]
                last = nc.tensor.transpose(b[bank][:, at + (q - kb) * P:at + (q - kb) * P + P], src, m.ident)
        last.then_inc(s(f"{t}_turned"), 1)


def pe_values(m, pe, t, c, j, out):
    s, nc = m.sem, m.nc
    for n, kb in enumerate((0, 1, 3, 2)):
        pe.wait_ge(*m.upto(f"{t}_turned_in", c(3, (1, 2, 2, 3)[n])))
        w = T - kb * P
        last = nc.tensor.matmul(out[:, kb * P:T], m.v[:, kb, j * P:(j + 1) * P], m.turned[:, TURNED[kb]:TURNED[kb] + w],
                                start=n == 0, stop=n == 3, skip_group_check=True)
    last.then_inc(s(f"{t}_values"), 1)


def pe_pairs(m, pe, t):
    s, b, mm = m.sem, m.bank, m.nc.tensor.matmul
    u0, u1, o_bank = b[5], b[6], b[7]
    h = (m.h_hi, m.h_lo)
    q_lat, kv_lat = (m.act_hi[:, 2:5, :], m.act_lo[:, 2:5, :]), (m.act_hi[:, 0:2, :], m.act_lo[:, 0:2, :])
    heads_out = (m.act_hi[:, 5:7, :], m.act_lo[:, 5:7, :])

    def step(i, ps, project, attend):
        first = ps[0] == 0

        def left(sem, per, more):
            pe.wait_ge(*m.upto(f"{t}_{sem}", along(i, [per * p + more for p in ps])))

        def left_before(sem, per, more):
            pe.wait_ge(*m.upto(f"{t}_{sem}", along(i, [per * (p - 1) + more for p in ps])))

        def output_added(n):
            pe.wait_ge(*m.upto(f"{t}_acc", along(i, [KC * (p - 2) + n for p in ps])))

        def per_head(j):
            def c(per, more):
                return along(i, [per * (2 * (p - 1) + j) + more for p in ps])
            return c

        def unit(x):
            return [f"mla.p{p}" if t == "mla" else f"{t}.{x}{p}" for p in ps]

        def parts(x):
            sl = slot(unit(x))
            at, n, k = (0, 1152, 3) if x == "q" else (1152, 1024, 2)
            return tuple(w[:, sl, at:at + n].rearrange("p (k n) -> p k n", k=k) for w in (m.w_hi, m.w_lo))

        def queries(j):
            if j == 1:
                left("q_in", 2, 1)
            elif ps[0] == 1:
                left_before("v_in", TT, TT)
            elif ps[0] > 1:
                output_added(6)
            if t == "mla":
                if j == 0:
                    pe_weights(m, pe, unit("q"), i)
                pe_features(m, pe, u0[:, :], parts("q"), j * NOPE, q_lat, 3)
            else:
                if j == 0:
                    pe_weights(m, pe, unit("q"), i)
                ready = h_ready(m, pe, t) if first and j == 0 else None
                pe_features(m, pe, u0[:, :], weight(m, unit("q"), 2048, KC), j * P, h, KC, ready)

        def keys(j):
            if j == 1:
                left("k_in", 2, 1)
            elif ps[0] == 1:
                left_before("v_in", TT, TT)
            elif ps[0] > 1:
                output_added(7)
            if t == "mla":
                pe_features(m, pe, u1[:, :], parts("k"), j * (NOPE + MV), kv_lat, 2)
            else:
                if j == 0:
                    pe_weights(m, pe, unit("k"), i)
                pe_features(m, pe, u1[:, :], weight(m, unit("k"), 2048, KC), j * P, h, KC)

        def rotated_queries():
            left("q_in", 2, 2)
            pe_features(m, pe, u0[:, :], parts("q"), 2 * NOPE, q_lat, 3)

        def values(tile):
            if tile == 0 and t == "mla":
                left("pe_in", 1, 1)
            elif tile == 0:
                pe_weights(m, pe, unit("v"), i)
                left("q_in", 2, 2)
            elif tile == 2:
                left("k_in", 2, 2)
            out = (u0, u1)[tile // 2][:, 256 * (tile % 2):256 * (tile % 2) + 256]
            if t == "mla":
                w = tuple(a.rearrange("p k (j n) -> p k j n", j=2)[:, :, :, NOPE:NOPE + MV] for a in parts("k"))
                for k in range(2):
                    hi, lo = (a[:, k, tile * P:(tile + 1) * P] for a in kv_lat)
                    mm(out, hi, w[0][:, k], start=k == 0, stop=False)
                    mm(out, hi, w[1][:, k], start=False, stop=False)
                    last = mm(out, lo, w[0][:, k], start=False, stop=k == 1)
            else:
                last = pe_tokens(m, pe, out, weight(m, unit("v"), 2048, KC), h, KC, tile)
            last.then_inc(s("blocks_done"), 1)

        def scores(j):
            left_before("q_in", 2, j + 1)
            left_before("k_in", 2, j + 1)
            if t == "mla":
                left_before("pe_in", 1, 1)
            if t == "diff" and j == 0 and ps[0] > 1:
                output_added(5)
            for nth, (q, n, bank, at, _) in enumerate(score_tiles(t)):
                w = (q + 1) * P
                tile = slice(q * P, (q + 1) * P)
                out = b[bank][:, at:at + w]
                if t == "diff":
                    half = slice(64 * n, 64 * n + 64)
                    if (n, bank) == (1, 2):
                        pe.wait_ge(*m.upto("diff_scores", per_head(j)(2 * TT, nth)))
                    mm(out, m.q[half, j, tile], m.k[half, j, 0:w], start=True, stop=True).then_inc(s("diff_scores"), 1)
                    continue
                last = mm(out, m.q[:, j, tile], m.k[:, j, 0:w], start=True, stop=t != "mla")
                if t == "mla":
                    half = slice(ROPE * j, ROPE * j + ROPE)
                    last = mm(out, m.q_pe[half, tile], m.k_pe[half, 0:w], start=False, stop=True)
                last.then_inc(s(f"{t}_scores"), 1)

        def attention(j):
            c = per_head(j)
            pe_turn(m, pe, t, c)
            if j == 1:
                pe.wait_ge(*m.upto("diff_o_taken" if t == "diff" else f"{t}_o_lo", c(1, 0)))
            elif ps[0] > 1:
                output_added(8)
            left_before("v_in", TT, TT)
            pe_values(m, pe, t, c, j, o_bank)

        def head_sums(j):
            if t == "diff" and attend:
                pe.wait_ge(*m.upto("diff_o_sq", per_head(j)(1, 1)))
                pe_sums(m, [m.tmp[:, 1, :]], o_bank[:, 0:TT]).then_inc(s("diff_sub_sums"), 1)

        def head_spread(j):
            if t == "diff" and attend:
                pe.wait_ge(*m.upto("diff_sub_diag", per_head(j)(TT, TT)))
                pe_spread(m, o_bank).then_inc(s("diff_sub_spread"), 1)

        def output():
            names = [f"{t}.o{p - 1}" for p in ps]
            pe_weights(m, pe, names, i)
            if project:
                left("v_in", TT, TT)
            left_before("o_lo", 2, 2)
            for n in range(KC):
                if n >= 4:
                    left_before("acc", KC, n - 3)
                pe_features(m, pe, b[4 + n % 4][:, :], weight(m, names, 2048, 2), n * P, heads_out, 2)

        gates = pe_fox_gates(m, pe) if t == "fox" and first else [lambda: None] * 5
        if attend:
            scores(0)
        if project:
            queries(0), gates[0](), keys(0), gates[1]()
        if attend:
            attention(0), scores(1)
        if project:
            queries(1), gates[2]()
        head_sums(0)
        if project:
            keys(1), gates[3]()
            if t == "mla":
                rotated_queries()
        head_spread(0)
        if attend:
            attention(1)
        if project:
            values(0)
        head_sums(1)
        if project:
            values(1), values(2)
        head_spread(1)
        if project:
            values(3), gates[4]()
        if attend:
            output()

    if t == "mla":
        pe.wait_ge(*m.upto("lat_lo", 5))
    step(None, [0], True, False)
    step(None, [1], True, True)
    with pe.Fori(0, PAIRS - 2) as i:
        step(i, list(range(2, PAIRS)), True, True)
    step(None, [PAIRS], False, True)


def pe_fox_gates(m, pe):
    s, b, mm, nc = m.sem, m.bank, m.nc.tensor.matmul, m.nc

    def norm_sums():
        pe.wait_ge(*m.upto("fox_sq", KC))
        pe_sums(m, [m.sq[:, k, :] for k in range(KC)], b[4][:, 0:TT]).then_inc(s("fox_norm_sums"), 1)

    def norm_spread_and_logits():
        pe.wait_ge(*m.upto("fox_wf_lo", 1))
        for t in range(TT):
            last = pe_tokens(m, pe, b[2][:, 8 * t:8 * t + 8], (m.wf_hi, m.wf_lo), (m.h_hi, m.h_lo), KC, t, 8)
        last.then_inc(s("fox_logits"), 1)
        pe.wait_ge(*m.upto("fox_norm_diag", TT))
        pe_spread(m, b[3]).then_inc(s("fox_norm_spread"), 1)

    def running_sums():
        pe.wait_ge(*m.upto("fox_log_f", 1))
        for q in range(TT):
            for t in range(q + 1):
                last = mm(b[4][:, 128 + 8 * q:136 + 8 * q], m.tri if t == q else m.ones[:, :], m.gate_f[:, 2, t, :],
                          start=t == 0, stop=t == q)
        last.then_inc(s("fox_sums"), 1)

    def turn_sums():
        pe.wait_ge(*m.upto("fox_c_cols", 1))
        for t in range(TT):
            last = nc.tensor.transpose(b[0][0:8, t * P:(t + 1) * P], m.c_cols[:, t, :], m.ident)
        last.then_inc(s("fox_c_turned"), 1)

    def spread_sums():
        pe.wait_ge(*m.upto("fox_c_rows", 1))
        pe.wait_ge(*m.upto("sel_in", 16))
        for n in range(8):
            if n >= 2:
                pe.wait_ge(*m.upto("fox_neg_c", n - 1))
            mm(b[4 + 3 * (n % 2)][:, :], m.sel[0:8, n, :], m.c_rows[0:8, :], start=True, stop=True).then_inc(s("fox_c_spread"), 1)

    return [norm_sums, norm_spread_and_logits, running_sums, turn_sums, spread_sums]


def pe_layernorm(m, pe, t):
    s, b = m.sem, m.bank
    pe.wait_ge(*m.upto(f"{t}_summed", KC))
    m.nc.tensor.matmul(b[0][:, :], m.mean_w[:, :], m.rb[:, :], start=True, stop=True).then_inc(s(f"{t}_mean"), 1)
    pe.wait_ge(*m.upto(f"{t}_sq", KC))
    pe_sums(m, [m.sq[:, k, :] for k in range(KC)], b[1][:, 0:TT]).then_inc(s(f"{t}_sums"), 1)
    pe.wait_ge(*m.upto(f"{t}_diag", TT))
    pe_spread(m, b[2]).then_inc(s(f"{t}_spread"), 1)


def pe_relu_mlp(m, pe, t):
    s, b = m.sem, m.bank
    h = (m.h_hi, m.h_lo)

    def up(gs, i=None):
        names = [f"{t}.u{g}" for g in gs]
        pe_weights(m, pe, names, i)
        for j in range(2):
            if gs[0]:
                pe.wait_ge(*m.upto(f"{t}_relu", along(i, [2 * g + j - 1 for g in gs])))
            pe_features(m, pe, b[j][:, :], weight(m, names, 2048, KC), j * P, h, KC,
                        h_ready(m, pe, t) if gs[0] == 0 and j == 0 else None)

    def down(gs, i=None):
        names = [f"{t}.d{g}" for g in gs]
        at = 2 * (gs[0] % 2)
        pe_weights(m, pe, names, i)
        pe.wait_ge(*m.upto(f"{t}_a_lo", along(i, [2 * g + 2 for g in gs])))
        for n in range(KC):
            if gs[0] or n >= 4:
                pe.wait_ge(*m.upto(f"{t}_acc", along(i, [KC * g + n - 3 for g in gs])))
            pe_features(m, pe, b[4 + n % 4][:, :], weight(m, names, 2048, 2), n * P,
                        (m.act_hi[:, at:at + 2, :], m.act_lo[:, at:at + 2, :]), 2)

    up([0])
    up([1])
    down([0])
    with pe.Fori(0, (G1 - 2) // 2) as i:
        for e in range(2):
            up(range(2 + e, G1, 2), i)
            down(range(1 + e, G1 - 1, 2), i)
    down([G1 - 1])


def pe_swiglu(m, pe, t):
    s, b = m.sem, m.bank
    h = (m.h_hi, m.h_lo)

    def wide(x, gs, i, j):
        first = x == "g" and gs[0] == 0 and j == 0
        names = [f"{t}.{x}{g}" for g in gs]
        if j == 0:
            pe_weights(m, pe, names, i)
        if gs[0]:
            pe.wait_ge(*m.upto(f"{t}_{x}_in", along(i, [2 * g + j - 1 for g in gs])))
        pe_features(m, pe, b[j + 2 * (x == "u")][:, :], weight(m, names, 2048, KC), j * P, h, KC, h_ready(m, pe, t) if first else None)

    def down(gs, i=None):
        names = [f"{t}.d{g}" for g in gs]
        at = 2 * (gs[0] % 2)
        pe_weights(m, pe, names, i)
        pe.wait_ge(*m.upto(f"{t}_a_lo", along(i, [2 * g + 2 for g in gs])))
        for n in range(KC):
            if gs[0] or n >= 4:
                pe.wait_ge(*m.upto(f"{t}_acc", along(i, [KC * g + n - 3 for g in gs])))
            pe_features(m, pe, b[4 + n % 4][:, :], weight(m, names, 2048, 2), n * P,
                        (m.act_hi[:, at:at + 2, :], m.act_lo[:, at:at + 2, :]), 2)

    wide("g", [0], None, 0)
    pe_norm_sums(m, pe, t, b[3])
    wide("g", [0], None, 1)
    pe_norm_spread(m, pe, t, b[2])
    for j in range(2):
        if j == 0:
            pe.wait_ge(*m.upto(f"{t}_norm_in", 1))
        wide("u", [0], None, j)
    for x in "gu":
        for j in range(2):
            wide(x, [1], None, j)
    down([0])
    with pe.Fori(0, (G2 - 3) // 2) as i:
        for e in range(2):
            gs = range(2 + e, G2 - 1, 2)
            for x in "gu":
                for j in range(2):
                    wide(x, gs, i, j)
            down(range(1 + e, G2 - 2, 2), i)
    for x in "gu":
        for j in range(2):
            wide(x, [G2 - 1], None, j)
    down([G2 - 2])
    down([G2 - 1])


def pe_norm_sums(m, pe, t, bank):
    pe.wait_ge(*m.upto(f"{t}_sq", KC))
    pe_sums(m, [m.sq[:, k, :] for k in range(KC)], bank[:, 0:TT]).then_inc(m.sem(f"{t}_norm_sums"), 1)


def pe_norm_spread(m, pe, t, bank):
    pe.wait_ge(*m.upto(f"{t}_norm_diag", TT))
    pe_spread(m, bank).then_inc(m.sem(f"{t}_norm_spread"), 1)


def pe_retention(m, pe):
    s, b, mm, nc = m.sem, m.bank, m.nc.tensor.matmul, m.nc
    h = (m.h_hi, m.h_lo)

    def step(i, hs, project, attend):
        first = hs[0] == 0

        def left(sem, per, more):
            pe.wait_ge(*m.upto(f"ret_{sem}", along(i, [per * x + more for x in hs])))

        def left_before(sem, per, more):
            pe.wait_ge(*m.upto(f"ret_{sem}", along(i, [per * (x - 1) + more for x in hs])))

        def features(x, j):
            names = [f"ret.{x}{n}" for n in hs]
            if j == 0:
                pe_weights(m, pe, names, i)
            if x == "k":
                left("q_in", 2, j + 1)
            elif not first:
                left_before("g_in", 2 * TT, 2 * TT)
            pe_features(m, pe, b[j][:, :], weight(m, names, 2048, KC), j * P, h, KC,
                        h_ready(m, pe, "ret") if first and x == "q" and j == 0 else None)

        def tokens(x, half):
            names = [f"ret.{x}{half}{n}" for n in hs]
            pe_weights(m, pe, names, i)
            for t in range(TT):
                if x == "v" and half == 0:
                    if t < 2:
                        left("k_in", 2, t + 1)
                    elif hs[0] > 1:
                        pe.wait_ge(*m.upto("ret_acc", along(i, [KC * (n - 2) + KC for n in hs])))
                else:
                    before = ("v", 0) if half else ("v", 1)
                    if x == "v" or half == 0:
                        left("v_in", 2 * TT, TT * before[1] + t + 1)
                    else:
                        left("g_in", 2 * TT, t + 1)
                pe_tokens(m, pe, b[(0, 1, 6, 7)[t]][:, 0:256], weight(m, names, 2048, KC), h, KC, t).then_inc(s("blocks_done"), 1)

        def scores():
            left_before("k_roped", 1, 1)
            for kb in (0, 1, 3, 2):
                bank, at = TURN_AT[kb]
                if kb == 2 and hs[0] > 1:
                    pe.wait_ge(*m.upto("ret_acc", along(i, [KC * (n - 2) + 5 for n in hs])))
                for j in range(2):
                    last = mm(b[2 + bank][:, at:at + T - kb * P], m.k[:, j, kb * P:(kb + 1) * P], m.q[:, j, kb * P:T],
                              start=j == 0, stop=j == 1)
                last.then_inc(s("ret_scores"), 1)

        def values():
            left_before("decayed", TT, TT)
            left_before("v_in", 2 * TT, 2 * TT)
            for q in range(TT):
                if q == 3 and hs[0] > 1:
                    pe.wait_ge(*m.upto("ret_acc", along(i, [KC * (n - 2) + 6 for n in hs])))
                for kb in range(q + 1):
                    at = TURNED[kb] + (q - kb) * P
                    last = mm(b[2 + q][:, :], m.ra[:, at:at + P], m.rv[:, kb, :], start=kb == 0, stop=kb == q)
                last.then_inc(s("ret_values"), 1)

        def turn():
            left_before("gated", TT, TT)
            for c in range(4):
                for q in range(TT):
                    last = nc.tensor.transpose(b[2 + c][:, q * P:(q + 1) * P], m.ry[:, q, c * P:(c + 1) * P], m.ident)
                last.then_inc(s("ret_turned"), 1)

        def output():
            left_before("o_lo", 4, 4)
            for half in range(2):
                names = [f"ret.o{half}{n - 1}" for n in hs]
                pe_weights(m, pe, names, i)
                for n in range(4):
                    if half:
                        left_before("acc", KC, n + 1)
                    elif n >= 2 and project:
                        left("g_in", 2 * TT, TT + n + 1)
                    pe_features(m, pe, b[4 + n][:, :], weight(m, names, 2048, 4), n * P,
                                (m.act_hi[:, 0:4, :], m.act_lo[:, 0:4, :]), 4)

        if attend:
            scores()
        if project:
            features("q", 0)
            if first:
                pe_norm_sums(m, pe, "ret", b[5])
            features("q", 1)
            if first:
                pe_norm_spread(m, pe, "ret", b[4])
        if attend:
            values()
        if project:
            features("k", 0), features("k", 1)
        if attend:
            turn()
        if project:
            for x in "vg":
                tokens(x, 0), tokens(x, 1)
        if attend:
            output()

    step(None, [0], True, False)
    step(None, [1], True, True)
    with pe.Fori(0, RH - 2) as i:
        step(i, list(range(2, RH)), True, True)
    step(None, [RH], False, True)


def pe_end(m, pe):
    s, b = m.sem, m.bank
    pe_norm_sums(m, pe, "out", b[0])
    for t in range(TT):
        for half in range(2):
            bank = b[1 + (2 * t + half) % 4]
            if t >= 2:
                pe.wait_ge(*m.upto("out_rows", 2 * t + half - 3))
            for k in range(4):
                last = m.nc.tensor.transpose(bank[:, k * P:(k + 1) * P], m.x[:, 4 * half + k, t * P:(t + 1) * P], m.ident)
            last.then_inc(s("out_turned"), 1)


def pe_program(m, pe):
    pe_start(m, pe)
    pe_pairs(m, pe, "mla")
    pe_layernorm(m, pe, "ln0")
    pe_relu_mlp(m, pe, "ffn0")
    pe_layernorm(m, pe, "ln1")
    pe_pairs(m, pe, "diff")
    pe_layernorm(m, pe, "ln2")
    pe_relu_mlp(m, pe, "ffn1")
    pe_layernorm(m, pe, "ln3")
    pe_pairs(m, pe, "fox")
    pe_swiglu(m, pe, "sw0")
    pe_retention(m, pe)
    pe_swiglu(m, pe, "sw1")
    pe_end(m, pe)


def act_split(m, act, names, i=None):
    n0, sl = INDEX[names[0]], slot(names)
    width = SLOT if names[0].startswith("mla.p") else 2048
    act.wait_ge(*m.upto(f"w_landed{sl}", along(i, [LANDED[INDEX[n]] for n in names])))
    if n0 >= 2:
        act.wait_ge(*m.upto("blocks_done", along(i, [UNIT_DONE[UNITS[INDEX[n] - 2][0]] for n in names])))
    m.nc.scalar.activation(m.w_hi[:, sl, 0:width], m.w_raw[:, sl, 0:width], ACT.Copy).then_inc(m.sem("w_hi_ready"), 1)


def act_rope(m, act, t, steps):
    s, run = m.sem, m.nc.scalar.activation
    c = 2 * (t == "diff")
    act.wait_ge(*m.upto(f"{t}_rope_steps", steps))
    act.wait_ge(*m.upto("set_up", 5))
    run(m.rope_sin[:, :], m.ang, ACT.Sin, scale=m.rope_cols[:, c + 1:c + 2]).then_inc(s(f"{t}_rope_made"), 1)
    run(m.turns, m.ang, ACT.Abs).then_inc(s(f"{t}_rope_abs"), 1)
    act.wait_ge(*m.upto(f"{t}_rope_abs", 1))
    run(m.rope_cos[:, :], m.turns, ACT.Sin, scale=-1.0, bias=m.eps[:, 2:3]).then_inc(s(f"{t}_rope_made"), 1)


def act_start(m, act):
    s, b, run = m.sem, m.bank, m.nc.scalar.activation
    act_split(m, act, ["kv"])
    for k in range(KC):
        act.wait_ge(*m.upto("x_turned", k + 1))
        run(m.h_hi[:, k, :], b[k][:, :], ACT.Copy).then_inc(s("mla_h_hi"), 1)
        run(m.x[:, k, :], b[k][:, :], ACT.Copy, scale=ALPHA).then_inc(s("x_scaled"), 1)
        if k == 3:
            act_split(m, act, ["pe"])
    act.wait_ge(*m.upto("cols_turned", 1))
    run(m.cols[:, :], b[7][:, 0:NROWS], ACT.Copy).then_inc(s("cols_in"), 1)
    act_rope(m, act, "mla", ROPE_STEPS)
    act_split(m, act, ["cq"])

    def latent(n, bank, name, part, gain, at):
        act.wait_ge(*m.upto("blocks_done", BLOCK[name, part]))
        if n == 0:
            act.wait_ge(*m.upto("cols_in", 1))
        run(m.act_hi[:, n, :], bank[:, :], ACT.Copy, scale=col(m, gain, at)).then_inc(s("lat_hi"), 1)
        run(m.sq[:, n, :], bank[:, :], ACT.Square).then_inc(s("lat_sq"), 1)

    latent(0, b[0], "kv", 0, "mla_kv_norm", 0)
    latent(1, b[1], "kv", 1, "mla_kv_norm", 1)
    latent(2, b[3], "pe", 1, "mla_q_norm", 0)
    act_split(m, act, ["mla.p0"])
    latent(3, b[4], "cq", 0, "mla_q_norm", 1)
    latent(4, b[5], "cq", 1, "mla_q_norm", 2)
    for n, width in enumerate((KVL, QL)):
        act.wait_ge(*m.upto("lat_sums", n + 1))
        run(m.std[:, TT * n:TT * n + TT], b[n][:, 0:TT], ACT.Sqrt, scale=1 / width, bias=m.eps[:, 1:2])\
            .then_inc(s("lat_std"), 1)
    for n, (bank, rows) in enumerate(((b[0], m.rb[:, :]), (b[1], m.rb_q))):
        act.wait_ge(*m.upto("lat_spread", n + 1))
        run(rows, bank[:, :], ACT.Copy).then_inc(s("lat_rows"), 1)


def act_std(m, act, t, bank):
    s, run = m.sem, m.nc.scalar.activation
    act.wait_ge(*m.upto(f"{t}_norm_sums", 1))
    run(m.std[:, 0:TT], bank[:, 0:TT], ACT.Sqrt, scale=1 / D, bias=m.eps[:, 1:2]).then_inc(s(f"{t}_norm_std"), 1)


def act_rows(m, act, t, bank):
    act.wait_ge(*m.upto(f"{t}_norm_spread", 1))
    m.nc.scalar.activation(m.rb[:, :], bank[:, :], ACT.Copy).then_inc(m.sem(f"{t}_norm_in"), 1)


def act_input(m, act, t, done, count, gain, row):
    s, run = m.sem, m.nc.scalar.activation
    for k in range(KC):
        act.wait_ge(*m.upto(done, count + k + 1))
        if gain:
            run(m.h_hi[:, k, :], m.x[:, k, :], ACT.Copy, scale=col(m, gain, KC * row + k)).then_inc(s(f"{t}_h_hi"), 1)
        run(m.sq[:, k, :], m.x[:, k, :], ACT.Square).then_inc(s(f"{t}_sq"), 1)


def act_layernorm(m, act, t, to, shift, row):
    s, run = m.sem, m.nc.scalar.activation
    for k in range(KC):
        act.wait_ge(*m.upto(f"{t}_centered", k + 1))
        run(m.sq[:, k, :], m.x[:, k, :], ACT.Square).then_inc(s(f"{t}_sq"), 1)
    act.wait_ge(*m.upto(f"{t}_sums", 1))
    run(m.std[:, 0:TT], m.bank[1][:, 0:TT], ACT.Sqrt, scale=1 / D, bias=m.eps[:, 0:1]).then_inc(s(f"{t}_std"), 1)
    if to:
        for k in range(KC):
            act.wait_ge(*m.upto(f"{t}_scaled", k + 1))
            run(m.h_hi[:, k, :], m.x[:, k, :], ACT.Identity, bias=col(m, shift, KC * row + k)).then_inc(s(f"{to}_h_hi"), 1)


def act_pairs(m, act, t):
    s, b, run = m.sem, m.bank, m.nc.scalar.activation
    u0, u1, o_bank = b[5], b[6], b[7]

    def step(i, ps, project, attend):
        last = {p: (f"{t}.o{p - 1}" if p else f"{t}.v0" if t != "mla" else "mla.p0") for p in ps}

        def per_head(j):
            def c(per, more):
                return along(i, [per * (2 * (p - 1) + j) + more for p in ps])
            return c

        def exps(j):
            c = per_head(j)
            maps = 2 if t == "diff" else 1
            for q, n, bank, at, end in score_tiles(t):
                w = (q + 1) * P
                out = (m.probs, m.probs2)[n][:, PACKED[q]:PACKED[q] + w]
                src = out if t == "fox" else b[bank][:, at:at + w]
                act.wait_ge(*m.upto(f"{t}_neg_max", c(TT * maps, end)))
                run(out, src, ACT.Exp, bias=m.neg_max[:, TT * n + q:TT * n + q + 1],
                    accum_out=m.row_sum[:, TT * n + q:TT * n + q + 1]).then_inc(s(f"{t}_exps"), 1)

        def turned(j):
            for n, w in enumerate((512, 512, 256)):
                act.wait_ge(*m.upto(f"{t}_turned", per_head(j)(3, n + 1)))
                run(m.turned[:, 512 * n:512 * n + w], b[n][:, 0:w], ACT.Copy).then_inc(s(f"{t}_turned_in"), 1)

        def head_out(j):
            act.wait_ge(*m.upto(f"{t}_values", per_head(j)(1, 1)))
            if t == "diff":
                run(m.tmp[:, 0, :], o_bank[:, :], ACT.Copy).then_inc(s("diff_o_raw"), 1)
                run(m.tmp[:, 1, :], o_bank[:, :], ACT.Square).then_inc(s("diff_o_sq"), 1)
            else:
                run(m.act_hi[:, 5 + j, :], o_bank[:, :], ACT.Copy).then_inc(s(f"{t}_o_hi"), 1)

        def head_std(j):
            if t == "diff" and attend:
                act.wait_ge(*m.upto("diff_sub_sums", per_head(j)(1, 1)))
                run(m.std[:, 0:TT], o_bank[:, 0:TT], ACT.Sqrt, scale=1 / 128, bias=m.eps[:, 1:2]).then_inc(s("diff_sub_std"), 1)

        def head_hi(j):
            if t == "diff" and attend:
                act.wait_ge(*m.upto("diff_o_taken", per_head(j)(1, 1)))
                run(m.act_hi[:, 5 + j, :], m.tmp[:, 2, :], ACT.Copy).then_inc(s("diff_o_hi"), 1)

        def values(tiles):
            names = [f"mla.p{p}" if t == "mla" else f"{t}.v{p}" for p in ps]
            for tile in tiles:
                part = tile | 1
                act.wait_ge(*m.upto("blocks_done", block_done(i, names, f"v{part}" if t == "mla" else part)))
                src = (u0, u1)[tile // 2][:, 256 * (tile % 2):256 * (tile % 2) + 256]
                scale = 1.0 if t == "diff" else m.rcol[:, tile:tile + 1]
                run(m.v[:, tile, :], src, ACT.Copy, scale=scale).then_inc(s(f"{t}_v_in"), 1)

        def split(names):
            act_split(m, act, names, i)

        if t == "mla" and attend:
            split([f"mla.o{p - 1}" for p in ps] if project else after(["mla.o3"]))
        if t != "mla" and ps[0] == 0:
            split([f"{t}.k0"])
        if t == "fox" and ps[0] == 0:
            act_fox_gates(m, act, lambda: split(["fox.v0"]), lambda: split(["fox.q1"]))
        if attend:
            exps(0), turned(0), head_out(0), exps(1)
        head_std(0)
        if project and t != "mla" and not (t == "fox" and ps[0] == 0):
            split([f"{t}.v{p}" for p in ps])
        head_hi(0)
        if attend:
            turned(1), head_out(1)
        if project and t != "mla" and not (t == "fox" and ps[0] == 0):
            split([f"{t}.o{p - 1}" for p in ps] if attend else [f"{t}.q1"])
        if project:
            values([0, 1])
        head_std(1)
        if project:
            values([2])
        head_hi(1)
        if project:
            values([3])
            if t == "mla":
                split([f"mla.p{p + 1}" if p < PAIRS - 1 else f"mla.o{p}" for p in ps])
            else:
                done = [last[p] for p in ps]
                if attend:
                    split(after(done, 1))
                    split(after(done, 2))
                else:
                    split([f"{t}.k1"])
        if t == "fox" and ps[0] == 0:
            act_fox_sums(m, act)

    step(None, [0], True, False)
    step(None, [1], True, True)
    with act.Fori(0, PAIRS - 2) as i:
        step(i, list(range(2, PAIRS)), True, True)
    step(None, [PAIRS], False, True)


def act_fox_gates(m, act, split_v, split_q):
    s, b, run = m.sem, m.bank, m.nc.scalar.activation
    act_std(m, act, "fox", b[4])
    act_rows(m, act, "fox", b[3])
    e = m.gate_f[:, 1, :, :]
    act.wait_ge(*m.upto("fox_z", TT))
    run(e, m.gate_f[:, 0, :, :], ACT.Abs).then_inc(s("fox_gate_steps"), 1)
    act.wait_ge(*m.upto("fox_gate_steps", 1))
    run(e, e, ACT.Exp, scale=-1.0).then_inc(s("fox_gate_steps"), 1)
    act.wait_ge(*m.upto("fox_log1p", 1))
    run(m.gate_f[:, 3, :, :], m.gate_f[:, 4, :, :], ACT.Ln).then_inc(s("fox_gate_steps"), 1)
    split_v()
    act.wait_ge(*m.upto("fox_c_turned", 1))
    run(m.c_rows[0:8, :], b[0][0:8, :], ACT.Copy, scale=-1.0).then_inc(s("fox_c_rows"), 1)
    split_q()


def act_fox_sums(m, act):
    s = m.sem
    for n in range(8):
        act.wait_ge(*m.upto("fox_c_spread", n + 1))
        m.nc.scalar.activation(m.neg_c[:, n, :], m.bank[4 + 3 * (n % 2)][:, :], ACT.Copy).then_inc(s("fox_neg_c"), 1)


def act_relu_mlp(m, act, t):
    s, b, run = m.sem, m.bank, m.nc.scalar.activation

    def up(gs, i=None):
        names = [f"{t}.u{g}" for g in gs]
        act_split(m, act, after(names), i)
        for j in range(2):
            act.wait_ge(*m.upto("blocks_done", block_done(i, names, j)))
            if gs[0]:
                act.wait_ge(*m.upto(f"{t}_squared", along(i, [2 * g + j - 1 for g in gs])))
            run(m.relu[:, j, :], b[j][:, :], ACT.Relu).then_inc(s(f"{t}_relu"), 1)
            act.wait_ge(*m.upto(f"{t}_relu", along(i, [2 * g + j + 1 for g in gs])))
            run(m.act_hi[:, 2 * (gs[0] % 2) + j, :], m.relu[:, j, :], ACT.Square).then_inc(s(f"{t}_a_hi"), 1)

    def down(gs, i=None):
        act_split(m, act, after([f"{t}.d{g}" for g in gs]), i)

    up([0])
    up([1])
    down([0])
    with act.Fori(0, (G1 - 2) // 2) as i:
        for e in range(2):
            up(range(2 + e, G1, 2), i)
            down(range(1 + e, G1 - 1, 2), i)
    down([G1 - 1])


def act_swiglu(m, act, t, last):
    s, b, run = m.sem, m.bank, m.nc.scalar.activation

    def gate(gs, i=None):
        act_split(m, act, after([f"{t}.g{g}" for g in gs]), i)
        if gs[0] == 0:
            act_std(m, act, t, b[3])
            act_rows(m, act, t, b[2])
        for j in range(2):
            act.wait_ge(*m.upto(f"{t}_g_in", along(i, [2 * g + j + 1 for g in gs])))
            run(m.silu[:, j, :], m.gate[:, j, :], ACT.Silu).then_inc(s(f"{t}_silu"), 1)

    def up(gs, i=None):
        act_split(m, act, after([f"{t}.u{g}" for g in gs]), i)
        for j in range(2):
            act.wait_ge(*m.upto(f"{t}_prod", along(i, [2 * g + j + 1 for g in gs])))
            run(m.act_hi[:, 2 * (gs[0] % 2) + j, :], m.prod[:, j, :], ACT.Copy).then_inc(s(f"{t}_a_hi"), 1)

    def down(gs, i=None):
        if not (last and gs[-1] == G2 - 1):
            act_split(m, act, after([f"{t}.d{g}" for g in gs]), i)

    gate([0]), up([0])
    gate([1]), up([1]), down([0])
    with act.Fori(0, (G2 - 3) // 2) as i:
        for e in range(2):
            gs = range(2 + e, G2 - 1, 2)
            gate(gs, i), up(gs, i), down(range(1 + e, G2 - 2, 2), i)
    gate([G2 - 1]), up([G2 - 1]), down([G2 - 2])
    down([G2 - 1])


def act_retention(m, act):
    s, b, run = m.sem, m.bank, m.nc.scalar.activation

    def step(i, hs, project, attend):
        def left_before(sem, per, more):
            act.wait_ge(*m.upto(f"ret_{sem}", along(i, [per * (x - 1) + more for x in hs])))

        def split(names):
            act_split(m, act, names, i)

        if project:
            split([f"ret.k{n}" for n in hs])
            if hs[0] == 0:
                act_std(m, act, "ret", b[5])
                act_rows(m, act, "ret", b[4])
            split([f"ret.v0{n}" for n in hs])
        if attend:
            left_before("y_mean", TT, TT)
            run(m.y_std[:, :], m.y_mean[:, :, 1], ACT.Sqrt, bias=m.eps[:, 1:2]).then_inc(s("ret_y_std"), 1)
            left_before("y_shift", 1, 1)
            for q in range(TT):
                run(m.ry[:, q, :], b[2 + q][:, :], ACT.Identity, scale=m.y_rstd[:, q:q + 1], bias=m.y_shift[:, q:q + 1])\
                    .then_inc(s("ret_y_normed"), 1)
        if project:
            split([f"ret.v1{n}" for n in hs])
        if attend:
            for c in range(4):
                left_before("turned", 4, c + 1)
                run(m.act_hi[:, c, :], b[2 + c][:, :], ACT.Copy).then_inc(s("ret_o_hi"), 1)
        if project:
            for x in "vg":
                for half in range(2):
                    names = [f"ret.{x}{half}{n}" for n in hs]
                    if (x, half) != ("v", 0):
                        split(after(names))
                    if x == "g" and half == 0 and attend:
                        left_before("gated", TT, TT)
                    for t in range(TT):
                        act.wait_ge(*m.upto("blocks_done", block_done(i, names, t)))
                        out = (m.rv if x == "v" else m.rg)[:, t, 256 * half:256 * half + 256]
                        run(out, b[(0, 1, 6, 7)[t]][:, 0:256], ACT.Copy if x == "v" else ACT.Silu, scale=m.rcol[:, t:t + 1])\
                            .then_inc(s(f"ret_{x}_in"), 1)
        if attend:
            for half in range(2):
                split(after([f"ret.o{half}{n - 1}" for n in hs]))

    step(None, [0], True, False)
    step(None, [1], True, True)
    with act.Fori(0, RH - 2) as i:
        step(i, list(range(2, RH)), True, True)
    step(None, [RH], False, True)


def act_program(m, act):
    s = m.sem
    act_start(m, act)
    act_pairs(m, act, "mla")
    act_layernorm(m, act, "ln0", "ffn0", "ln_mix_b", 0)
    act.wait_ge(*m.upto("mla_pe_in", PAIRS))
    act_rope(m, act, "diff", ROPE_STEPS)
    act_relu_mlp(m, act, "ffn0")
    act_layernorm(m, act, "ln1", "diff", "ln_ffn_b", 0)
    run = m.nc.scalar.activation
    act.wait_ge(*m.upto("wf_in", 32))
    run(m.wf_hi[:, :, :], m.wf[:, :, :], ACT.Copy).then_inc(s("fox_wf_hi"), 1)
    act.wait_ge(*m.upto("lam_dots", 2))
    run(m.lam[:, 2:4], m.lam[:, 0:2], ACT.Exp).then_inc(s("lam_exp"), 1)
    act_pairs(m, act, "diff")
    act_layernorm(m, act, "ln2", "ffn1", "ln_mix_b", 1)
    act_relu_mlp(m, act, "ffn1")
    act_layernorm(m, act, "ln3", None, None, 1)
    act_input(m, act, "fox", "ln3_done", 0, "norm_mix_2", 0)
    act_pairs(m, act, "fox")
    act_input(m, act, "sw0", "fox_acc", KC * (PAIRS - 1), "norm_ffn_2", 0)
    act_swiglu(m, act, "sw0", False)
    act_input(m, act, "ret", "sw0_acc", KC * (G2 - 1), "norm_mix_2", 1)
    act_retention(m, act)
    act_input(m, act, "sw1", "ret_acc", KC * (RH - 1), "norm_ffn_2", 1)
    act_swiglu(m, act, "sw1", True)
    act_input(m, act, "out", "sw1_acc", KC * (G2 - 1), None, 0)
    act_std(m, act, "out", m.bank[0])


ROPE_STEPS = 8


def dve_rope(m, dve, t, n_in):
    s, v = m.sem, m.nc.vector
    c = 2 * (t == "diff")
    step = [0]

    def done(ins):
        ins.then_inc(s(f"{t}_rope_steps"), 1)
        step[0] += 1
        if step[0] < ROPE_STEPS:
            dve.wait_ge(*m.upto(f"{t}_rope_steps", step[0]))

    dve.wait_ge(*m.upto("pos_in", 16 * n_in))
    dve.wait_ge(*m.upto("consts_in", 16))
    done(v.tensor_copy(m.ang, m.pos.bitcast(I32)))
    done(v.tensor_scalar(m.ang, m.ang, m.rope_cols[:, c:c + 1], None, ALU.mult))
    done(v.tensor_scalar(m.turns, m.ang, 1 / (2 * math.pi), ROUND, ALU.mult, ALU.add))
    done(v.tensor_scalar(m.turns, m.turns, -ROUND, None, ALU.add))
    for part in TWO_PI:
        done(v.scalar_tensor_tensor(out=m.ang, in0=m.turns, scalar=-part, in1=m.ang, op0=ALU.mult, op1=ALU.add))
    done(v.tensor_scalar(m.ang, m.ang, -3.1415925, 3.1415925, ALU.max, ALU.min))


def dve_rstd(m, dve, t, count=1, per=1):
    s, v = m.sem, m.nc.vector
    v.reciprocal(m.rcol[:, 0:TT], m.std[:, 0:TT]).then_inc(s(f"{t}_rcol"), 1)
    dve.wait_ge(*m.upto(f"{t}_rcol", count))
    for k in range(TT):
        v.tensor_scalar(m.diag[:, k, :], m.ident, m.rcol[:, k:k + 1], None, ALU.mult).then_inc(s(f"{t}_diag"), 1)


def dve_rotate(m, dve, out, src, swapped, turned, sem_steps, before):
    s, v = m.sem, m.nc.vector
    for n in range(4):
        v.tensor_copy(swapped[32 * n:32 * n + 32, :], src[32 * (n ^ 1):32 * (n ^ 1) + 32, :]).then_inc(s(sem_steps), 1)
    v.tensor_tensor(turned, src, m.rope_cos[:, :], ALU.mult).then_inc(s(sem_steps), 1)
    dve.wait_ge(*m.upto(sem_steps, before(4)))
    v.tensor_tensor(swapped, swapped, m.rope_sin[:, :], ALU.mult).then_inc(s(sem_steps), 1)
    dve.wait_ge(*m.upto(sem_steps, before(6)))
    return v.tensor_tensor(out, turned, swapped, ALU.add)


def dve_start(m, dve):
    s, b, v = m.sem, m.bank, m.nc.vector
    v.memset(m.ones[:, :], 1.0).then_inc(s("set_up"), 1)
    v.memset(m.mean_w[:, :], 1.0 / D).then_inc(s("set_up"), 1)
    for n, value in enumerate((LN_EPS, RMS_EPS, math.pi / 2)):
        v.memset(m.eps[:, n:n + 1], value).then_inc(s("set_up"), 1)
    for k in range(KC):
        dve.wait_ge(*m.upto("x_scaled", k + 1))
        v.tensor_tensor(m.h_lo[:, k, :], b[k][:, :], m.h_hi[:, k, :].bitcast(F32), ALU.subtract).then_inc(s("mla_h_lo"), 1)
    dve_rope(m, dve, "mla", 1)

    def latent(n, bank, gain, at):
        dve.wait_ge(*m.upto("lat_sq", n + 1))
        v.scalar_tensor_tensor(out=m.act_lo[:, n, :], in0=bank[:, :], scalar=col(m, gain, at), in1=m.act_hi[:, n, :].bitcast(F32),
                               op0=ALU.mult, op1=ALU.subtract).then_inc(s("lat_lo"), 1)

    latent(0, b[0], "mla_kv_norm", 0)
    latent(1, b[1], "mla_kv_norm", 1)
    dve.wait_ge(*m.upto("blocks_done", BLOCK["pe", 0]))
    dve.wait_ge(*m.upto("mla_rope_made", 2))
    dve_rotate(m, dve, m.k_pe, b[2][:, :], m.tmp[:, 0, :], m.tmp[:, 1, :], "k_pe_steps", lambda n: n).then_inc(s("k_pe_in"), 1)
    latent(2, b[3], "mla_q_norm", 0)
    latent(3, b[4], "mla_q_norm", 1)
    latent(4, b[5], "mla_q_norm", 2)
    for n in range(2):
        at = TT * n
        dve.wait_ge(*m.upto("lat_std", n + 1))
        v.reciprocal(m.rcol[:, at:at + TT], m.std[:, at:at + TT]).then_inc(s("lat_rcol"), 1)
        dve.wait_ge(*m.upto("lat_rcol", n + 1))
        if n:
            dve.wait_ge(*m.upto("lat_spread", 1))
        for k in range(TT):
            v.tensor_scalar(m.diag[:, k, :], m.ident, m.rcol[:, at + k:at + k + 1], None, ALU.mult).then_inc(s("lat_diag"), 1)


def dve_add_block(m, dve, t, n, bank, names, part, i, steps, first):
    s, v = m.sem, m.nc.vector
    dve.wait_ge(*m.upto("blocks_done", block_done(i, names, part)))
    if not first:
        dve.wait_ge(*m.upto(f"{t}_acc", along(i, [KC * (g - 1) + n + 1 for g in steps])))
    v.tensor_tensor(m.x[:, n, :], m.x[:, n, :], bank[:, :], ALU.add).then_inc(s(f"{t}_acc"), 1)


def dve_sum_chunk(m, dve, t, done, count, k):
    s, v = m.sem, m.nc.vector
    dve.wait_ge(*m.upto(done, count + k + 1))
    if k:
        dve.wait_ge(*m.upto(f"{t}_summed", k))
        v.tensor_tensor(m.rb[:, :], m.rb[:, :], m.x[:, k, :], ALU.add).then_inc(s(f"{t}_summed"), 1)
    else:
        v.tensor_copy(m.rb[:, :], m.x[:, k, :]).then_inc(s(f"{t}_summed"), 1)


def dve_layernorm(m, dve, t, to, gain, shift, row):
    s, b, v = m.sem, m.bank, m.nc.vector
    dve.wait_ge(*m.upto(f"{t}_mean", 1))
    for k in range(KC):
        v.tensor_tensor(m.x[:, k, :], m.x[:, k, :], b[0][:, :], ALU.subtract).then_inc(s(f"{t}_centered"), 1)
    dve.wait_ge(*m.upto(f"{t}_std", 1))
    dve_rstd(m, dve, t)
    dve.wait_ge(*m.upto(f"{t}_spread", 1))

    def low(k):
        dve.wait_ge(*m.upto(f"{to}_h_hi", k + 1))
        v.scalar_tensor_tensor(out=m.h_lo[:, k, :], in0=m.x[:, k, :], scalar=col(m, shift, KC * row + k),
                               in1=m.h_hi[:, k, :].bitcast(F32), op0=ALU.add, op1=ALU.subtract).then_inc(s(f"{to}_h_lo"), 1)

    for k in range(KC):
        dve.wait_ge(*m.upto(f"{t}_sq", k + 1))
        v.scalar_tensor_tensor(out=m.x[:, k, :], in0=m.x[:, k, :], scalar=col(m, gain, KC * row + k), in1=b[2][:, :],
                               op0=ALU.mult, op1=ALU.mult).then_inc(s(f"{t}_scaled"), 1)
        if to:
            if k:
                low(k - 1)
        else:
            dve.wait_ge(*m.upto(f"{t}_scaled", k + 1))
            v.tensor_scalar(m.x[:, k, :], m.x[:, k, :], col(m, shift, KC * row + k), None, ALU.add).then_inc(s(f"{t}_done"), 1)
    if to:
        low(KC - 1)
        for k in range(KC):
            v.tensor_scalar(m.x[:, k, :], m.x[:, k, :], col(m, shift, KC * row + k), ALPHA, ALU.add, ALU.mult)\
                .then_inc(s(f"{t}_done"), 1)


def dve_input_low(m, dve, t, gain, row, k):
    s, v = m.sem, m.nc.vector
    dve.wait_ge(*m.upto(f"{t}_h_hi", k + 1))
    v.scalar_tensor_tensor(out=m.h_lo[:, k, :], in0=m.x[:, k, :], scalar=col(m, gain, KC * row + k),
                           in1=m.h_hi[:, k, :].bitcast(F32), op0=ALU.mult, op1=ALU.subtract).then_inc(s(f"{t}_h_lo"), 1)


def dve_norm_rstd(m, dve, t):
    dve.wait_ge(*m.upto(f"{t}_norm_std", 1))
    dve_rstd(m, dve, f"{t}_norm")


def dve_last_blocks(m, dve, add, t, count, then):
    for n in range(KC + 1):
        if n < KC:
            add(n)
        if n and then[0] == "mean":
            dve_sum_chunk(m, dve, then[1], f"{t}_acc", count, n - 1)
        elif n and then[0] == "input":
            dve_input_low(m, dve, *then[1:], n - 1)


def dve_pairs(m, dve, t, then):
    s, b, v = m.sem, m.bank, m.nc.vector
    u0, u1, o_bank = b[5], b[6], b[7]

    def step(i, ps, project, attend):
        def per_head(j):
            def c(per, more):
                return along(i, [per * (2 * (p - 1) + j) + more for p in ps])
            return c

        def unit(x):
            return [f"mla.p{p}" if t == "mla" else f"{t}.{x}{p}" for p in ps]

        def softmax(j):
            c = per_head(j)
            maps = 2 if t == "diff" else 1
            for nth, (q, n, bank, at, end) in enumerate(score_tiles(t)):
                w = (q + 1) * P
                dve.wait_ge(*m.upto(f"{t}_scores", c(TT * maps, end)))
                if t == "fox":
                    head = along(i, [2 * (p - 1) + j for p in ps]) if ps[0] > 1 else 2 * (ps[0] - 1) + j
                    neg_c = m.neg_c[:, bass.ds(head, 1), 0:w] if i is not None else m.neg_c[:, head, 0:w]
                    c_col = m.c_cols[:, q, bass.ds(head, 1)]
                    src = m.probs[:, PACKED[q]:PACKED[q] + w]
                    v.scalar_tensor_tensor(out=src, in0=neg_c, scalar=c_col, in1=b[bank][:, at:at + w],
                                           op0=ALU.add, op1=ALU.add).then_inc(s("fox_forgot"), 1)
                    dve.wait_ge(*m.upto("fox_forgot", c(TT, q + 1)))
                else:
                    src = b[bank][:, at:at + w]
                last = src[:, q * P:w]
                v.tensor_tensor(last, last, m.causal, ALU.add).then_inc(s(f"{t}_masked"), 1)
                dve.wait_ge(*m.upto(f"{t}_masked", c(TT * maps, nth + 1)))
                v.tensor_reduce(m.neg_max[:, TT * n + q:TT * n + q + 1], src, AX, ALU.max, negate=True).then_inc(s(f"{t}_neg_max"), 1)
            dve.wait_ge(*m.upto(f"{t}_exps", c(TT * maps, TT * maps)))
            v.reciprocal(m.row_rec[:, 0:TT * maps], m.row_sum[:, 0:TT * maps]).then_inc(s(f"{t}_row_rec"), 1)
            dve.wait_ge(*m.upto(f"{t}_row_rec", c(1, 1)))
            if t == "diff":
                v.tensor_scalar(m.row_rec[:, TT:2 * TT], m.row_rec[:, TT:2 * TT], m.lam[:, 5:6], None, ALU.mult).then_inc(s("diff_second_rec"), 1)
                dve.wait_ge(*m.upto("diff_second_rec", c(1, 1)))
            for q in range(TT):
                w = (q + 1) * P
                out = m.probs[:, PACKED[q]:PACKED[q] + w]
                rec = m.row_rec[:, q:q + 1]
                if t == "diff":
                    second = m.probs2[:, PACKED[q]:PACKED[q] + w]
                    v.tensor_scalar(second, second, m.row_rec[:, TT + q:TT + q + 1], None, ALU.mult).then_inc(s("diff_second"), 1)
                    dve.wait_ge(*m.upto("diff_second", c(TT, q + 1)))
                    v.scalar_tensor_tensor(out=out, in0=out, scalar=rec, in1=second, op0=ALU.mult, op1=ALU.add).then_inc(s("diff_probs"), 1)
                else:
                    v.tensor_scalar(out, out, rec, None, ALU.mult).then_inc(s(f"{t}_probs"), 1)

        def take(x, j):
            part = f"{x}{j}" if t == "mla" else j
            dve.wait_ge(*m.upto("blocks_done", block_done(i, unit(x), part)))
            bank, out = ((u0, m.q) if x == "q" else (u1, m.k))
            if t == "diff":
                n = [2 * p + j for p in ps]
                scale = DIFF_SCALE if x == "q" else 1.0
                swapped, turned = (m.rtmp[:, 2 * (x == "k") + e, :] for e in range(2))
                if ps[0] or j:
                    dve.wait_ge(*m.upto(f"diff_{x}_in", along(i, n)))
                steps = f"diff_{x}_steps"
                v.scalar_tensor_tensor(out=turned, in0=bank[:, :], scalar=scale, in1=m.rope_cos[:, :], op0=ALU.mult, op1=ALU.mult).then_inc(s(steps), 1)
                v.stream_shuffle(swapped, bank[:, :], ROT_SWAP).then_inc(s(steps), 1)
                dve.wait_ge(*m.upto(steps, along(i, [3 * a + 2 for a in n])))
                v.scalar_tensor_tensor(out=swapped, in0=swapped, scalar=scale, in1=m.rope_sin[:, :], op0=ALU.mult, op1=ALU.mult).then_inc(s(steps), 1)
                dve.wait_ge(*m.upto(steps, along(i, [3 * a + 3 for a in n])))
                v.tensor_tensor(out[:, j, :], turned, swapped, ALU.add).then_inc(s(f"diff_{x}_in"), 1)
                return
            rows = m.rb_q if t == "mla" and x == "q" else m.rb[:, :]
            scale = 1.0 if x == "k" else MLA_SCALE if t == "mla" else FOX_SCALE
            v.scalar_tensor_tensor(out=out[:, j, :], in0=bank[:, :], scalar=scale, in1=rows, op0=ALU.mult, op1=ALU.mult)\
                .then_inc(s(f"{t}_{x}_in"), 1)

        def take_rotated():
            dve.wait_ge(*m.upto("blocks_done", block_done(i, unit("q"), "pe")))
            if ps[0]:
                dve.wait_ge(*m.upto("mla_pe_in", along(i, ps)))
            v.scalar_tensor_tensor(out=m.tmp[:, 2, :], in0=u0[:, :], scalar=MLA_SCALE, in1=m.rb_q, op0=ALU.mult, op1=ALU.mult)\
                .then_inc(s("mla_pe_scaled"), 1)
            dve.wait_ge(*m.upto("mla_pe_scaled", along(i, [p + 1 for p in ps])))
            dve_rotate(m, dve, m.q_pe, m.tmp[:, 2, :], m.tmp[:, 0, :], m.tmp[:, 1, :], "mla_pe_steps",
                       lambda n: along(i, [6 * p + n for p in ps])).then_inc(s("mla_pe_in"), 1)

        def head_low(j):
            dve.wait_ge(*m.upto(f"{t}_o_hi", per_head(j)(1, 1)))
            src = m.tmp[:, 2, :] if t == "diff" else o_bank[:, :]
            v.tensor_tensor(m.act_lo[:, 5 + j, :], src, m.act_hi[:, 5 + j, :].bitcast(F32), ALU.subtract).then_inc(s(f"{t}_o_lo"), 1)

        def head_rstd(j):
            if t == "diff" and attend:
                dve.wait_ge(*m.upto("diff_sub_std", per_head(j)(1, 1)))
                dve_rstd(m, dve, "diff_sub", per_head(j)(1, 1))

        def head_norm(j):
            dve.wait_ge(*m.upto("diff_sub_spread", per_head(j)(1, 1)))
            dve.wait_ge(*m.upto("diff_o_raw", per_head(j)(1, 1)))
            v.scalar_tensor_tensor(out=m.tmp[:, 2, :], in0=m.tmp[:, 0, :], scalar=m.lam[:, 6:7], in1=o_bank[:, :],
                                   op0=ALU.mult, op1=ALU.mult).then_inc(s("diff_o_taken"), 1)
            head_low(j)

        if t == "fox" and ps[0] == 0:
            dve_fox_gates(m, dve, take)
        elif t == "fox" and ps[0] == 1:
            dve.wait_ge(*m.upto("fox_neg_c", 8))
        if t == "mla" and ps[0] == 0:
            dve.wait_ge(*m.upto("lat_rows", 2))
        if attend:
            softmax(0)
        if project and not (t == "fox" and ps[0] == 0):
            take("q", 0), take("k", 0)
        if attend:
            if t != "diff":
                head_low(0)
            softmax(1)
        head_rstd(0)
        if project and not (t == "fox" and ps[0] == 0):
            take("q", 1)
            if t != "diff":
                take("k", 1)
        if project and t == "mla":
            take_rotated()
        if attend:
            if t == "diff":
                head_norm(0)
            if t != "diff":
                head_low(1)
        if project and t == "diff":
            take("k", 1)
        head_rstd(1)
        if attend:
            if t == "diff":
                head_norm(1)

            def add(n):
                dve_add_block(m, dve, t, n, b[4 + n % 4], [f"{t}.o{p - 1}" for p in ps], n, i, [p - 1 for p in ps], ps[0] == 1)
            if project:
                for n in range(KC):
                    add(n)
            else:
                dve_last_blocks(m, dve, add, t, KC * (PAIRS - 1), then)

    step(None, [0], True, False)
    step(None, [1], True, True)
    with dve.Fori(0, PAIRS - 2) as i:
        step(i, list(range(2, PAIRS)), True, True)
    step(None, [PAIRS], False, True)


ROT_SWAP = list(range(8, 16)) + list(range(8)) + list(range(16, 32))


def dve_fox_gates(m, dve, take):
    s, b, v = m.sem, m.bank, m.nc.vector
    dve_norm_rstd(m, dve, "fox")
    dve.wait_ge(*m.upto("fox_logits", 1))
    for t in range(TT):
        v.scalar_tensor_tensor(out=m.gate_f[:, 0, t, :], in0=b[2][:, 8 * t:8 * t + 8], scalar=m.rcol[:, t:t + 1], in1=m.b_f[:, :],
                               op0=ALU.mult, op1=ALU.add).then_inc(s("fox_z"), 1)
    dve.wait_ge(*m.upto("fox_norm_in", 1))
    take("q", 0), take("k", 0)
    z, e, log_f, ln, u, rec = (m.gate_f[:, n, :, :] for n in range(6))
    dve.wait_ge(*m.upto("fox_gate_steps", 2))
    v.tensor_scalar(u, e, 1.0, None, ALU.add).then_inc(s("fox_log1p"), 1)
    dve.wait_ge(*m.upto("fox_log1p", 1))
    v.scalar_tensor_tensor(out=e, in0=u, scalar=-1.0, in1=e, op0=ALU.add, op1=ALU.subtract).then_inc(s("fox_log1p"), 1)
    v.reciprocal(rec, u).then_inc(s("fox_log1p"), 1)
    dve.wait_ge(*m.upto("fox_log1p", 3))
    v.tensor_tensor(e, e, rec, ALU.mult).then_inc(s("fox_log1p"), 1)
    dve.wait_ge(*m.upto("fox_gate_steps", 3))
    v.scalar_tensor_tensor(out=log_f, in0=z, scalar=0.0, in1=ln, op0=ALU.min, op1=ALU.subtract).then_inc(s("fox_log1p"), 1)
    dve.wait_ge(*m.upto("fox_log1p", 5))
    v.tensor_tensor(log_f, log_f, e, ALU.add).then_inc(s("fox_log_f"), 1)
    take("q", 1)
    dve.wait_ge(*m.upto("fox_sums", 1))
    v.tensor_copy(m.c_cols[:, :, :].rearrange("p t h -> p (t h)"), b[4][:, 128:128 + 8 * TT]).then_inc(s("fox_c_cols"), 1)
    take("k", 1)


def dve_lambda(m, dve):
    s, v = m.sem, m.nc.vector
    dve.wait_ge(*m.upto("lam_in", 64))
    for n in range(2):
        v.tensor_tensor(m.lam_in[:, n, :] if n == 0 else m.lam_in[:, 2, :], m.lam_in[:, 2 * n, :], m.lam_in[:, 2 * n + 1, :], ALU.mult)\
            .then_inc(s("lam_products"), 1)
        dve.wait_ge(*m.upto("lam_products", n + 1))
        v.tensor_reduce(m.lam[:, n:n + 1], m.lam_in[:, 2 * n, :], AX, ALU.add).then_inc(s("lam_dots"), 1)
    v.tensor_scalar(m.lam[:, 6:7], col(m, "diff_subln", 0), 1.0 - LAMBDA_INIT, None, ALU.mult).then_inc(s("lam_steps"), 1)
    dve.wait_ge(*m.upto("lam_exp", 1))
    v.tensor_tensor(m.lam[:, 4:5], m.lam[:, 2:3], m.lam[:, 3:4], ALU.subtract).then_inc(s("lam_steps"), 1)
    dve.wait_ge(*m.upto("lam_steps", 2))
    v.tensor_scalar(m.lam[:, 5:6], m.lam[:, 4:5], LAMBDA_INIT, -1.0, ALU.add, ALU.mult).then_inc(s("lam_steps"), 1)
    dve.wait_ge(*m.upto("fox_wf_hi", 1))
    v.tensor_tensor(m.wf_lo[:, :, :], m.wf[:, :, :], m.wf_hi[:, :, :].bitcast(F32), ALU.subtract).then_inc(s("fox_wf_lo"), 1)
    dve.wait_ge(*m.upto("lam_steps", 3))


def dve_relu_mlp(m, dve, t, norm, then):
    s, b, v = m.sem, m.bank, m.nc.vector

    def up(gs, i=None):
        for j in range(2):
            dve.wait_ge(*m.upto(f"{t}_relu", along(i, [2 * g + j + 1 for g in gs])))
            v.tensor_tensor(m.square[:, j, :], m.relu[:, j, :], m.relu[:, j, :], ALU.mult).then_inc(s(f"{t}_squared"), 1)
            dve.wait_ge(*m.upto(f"{t}_squared", along(i, [2 * g + j + 1 for g in gs])))
            dve.wait_ge(*m.upto(f"{t}_a_hi", along(i, [2 * g + j + 1 for g in gs])))
            at = 2 * (gs[0] % 2) + j
            v.tensor_tensor(m.act_lo[:, at, :], m.square[:, j, :], m.act_hi[:, at, :].bitcast(F32), ALU.subtract).then_inc(s(f"{t}_a_lo"), 1)

    def adder(gs, i=None):
        def add(n):
            dve_add_block(m, dve, t, n, b[4 + n % 4], [f"{t}.d{g}" for g in gs], n, i, gs, gs[0] == 0)
        return add

    def down(gs, i=None):
        for n in range(KC):
            adder(gs, i)(n)

    up([0])
    up([1])
    dve.wait_ge(*m.upto(f"{norm}_done", KC))
    down([0])
    with dve.Fori(0, (G1 - 2) // 2) as i:
        for e in range(2):
            up(range(2 + e, G1, 2), i)
            down(range(1 + e, G1 - 1, 2), i)
    dve_last_blocks(m, dve, adder([G1 - 1]), t, KC * (G1 - 1), then)


def dve_swiglu(m, dve, t, then):
    s, b, v = m.sem, m.bank, m.nc.vector

    def gate(gs, i=None):
        if gs[0] == 0:
            dve_norm_rstd(m, dve, t)
            dve.wait_ge(*m.upto(f"{t}_norm_in", 1))
        for j in range(2):
            dve.wait_ge(*m.upto("blocks_done", block_done(i, [f"{t}.g{g}" for g in gs], j)))
            if gs[0]:
                dve.wait_ge(*m.upto(f"{t}_silu", along(i, [2 * g + j - 1 for g in gs])))
            v.tensor_tensor(m.gate[:, j, :], b[j][:, :], m.rb[:, :], ALU.mult).then_inc(s(f"{t}_g_in"), 1)

    def up(gs, i=None):
        at = 2 * (gs[0] % 2)
        for j in range(2):
            dve.wait_ge(*m.upto("blocks_done", block_done(i, [f"{t}.u{g}" for g in gs], j)))
            v.tensor_tensor(m.up[:, j, :], b[2 + j][:, :], m.rb[:, :], ALU.mult).then_inc(s(f"{t}_u_in"), 1)
            dve.wait_ge(*m.upto(f"{t}_u_in", along(i, [2 * g + j + 1 for g in gs])))
            dve.wait_ge(*m.upto(f"{t}_silu", along(i, [2 * g + j + 1 for g in gs])))
            v.tensor_tensor(m.prod[:, j, :], m.up[:, j, :], m.silu[:, j, :], ALU.mult).then_inc(s(f"{t}_prod"), 1)
            dve.wait_ge(*m.upto(f"{t}_prod", along(i, [2 * g + j + 1 for g in gs])))
            dve.wait_ge(*m.upto(f"{t}_a_hi", along(i, [2 * g + j + 1 for g in gs])))
            v.tensor_tensor(m.act_lo[:, at + j, :], m.prod[:, j, :], m.act_hi[:, at + j, :].bitcast(F32), ALU.subtract)\
                .then_inc(s(f"{t}_a_lo"), 1)

    def adder(gs, i=None):
        def add(n):
            dve_add_block(m, dve, t, n, b[4 + n % 4], [f"{t}.d{g}" for g in gs], n, i, gs, gs[0] == 0)
        return add

    def down(gs, i=None):
        for n in range(KC):
            adder(gs, i)(n)

    gate([0]), up([0])
    gate([1]), up([1]), down([0])
    with dve.Fori(0, (G2 - 3) // 2) as i:
        for e in range(2):
            gs = range(2 + e, G2 - 1, 2)
            gate(gs, i), up(gs, i), down(range(1 + e, G2 - 2, 2), i)
    gate([G2 - 1]), up([G2 - 1]), down([G2 - 2])
    dve_last_blocks(m, dve, adder([G2 - 1]), t, KC * (G2 - 1), then)


def dve_retention(m, dve, then):
    s, b, v = m.sem, m.bank, m.nc.vector

    def step(i, hs, project, attend):
        def left_before(sem, per, more):
            dve.wait_ge(*m.upto(f"ret_{sem}", along(i, [per * (x - 1) + more for x in hs])))

        def take(x):
            out, scale = (m.q, 1.0) if x == "q" else (m.k, RET_SCALE)
            t = [m.rtmp[:, n, :] for n in range(4)]
            steps = s(f"ret_{x}_steps")

            def before(n):
                dve.wait_ge(steps, along(i, [5 * h + n for h in hs]))

            for j in range(2):
                dve.wait_ge(*m.upto("blocks_done", block_done(i, [f"ret.{x}{h}" for h in hs], j)))
                v.scalar_tensor_tensor(out=t[j], in0=b[j][:, :], scalar=scale, in1=m.rb[:, :], op0=ALU.mult, op1=ALU.mult)\
                    .then_inc(s(f"ret_{x}_in"), 1)
            dve.wait_ge(*m.upto(f"ret_{x}_in", along(i, [2 * h + 2 for h in hs])))
            v.tensor_tensor(t[2], t[0], m.ret_cos, ALU.mult).then_inc(steps, 1)
            v.tensor_tensor(t[3], t[1], m.ret_sin, ALU.mult).then_inc(steps, 1)
            before(2)
            v.tensor_tensor(out[:, 0, :], t[2], t[3], ALU.subtract).then_inc(steps, 1)
            before(3)
            v.tensor_tensor(t[2], t[0], m.ret_sin, ALU.mult).then_inc(steps, 1)
            v.tensor_tensor(t[3], t[1], m.ret_cos, ALU.mult).then_inc(steps, 1)
            before(5)
            v.tensor_tensor(out[:, 1, :], t[2], t[3], ALU.add).then_inc(s(f"ret_{x}_roped"), 1)

        if attend:
            head = along(i, [h - 1 for h in hs]) if hs[0] > 1 else hs[0] - 1
            for n, kb in enumerate((0, 1, 3, 2)):
                bank, at = TURN_AT[kb]
                w = T - kb * P
                left_before("scores", TT, (1, 3, 3, 4)[n])
                decay = m.decay[:, bass.ds(head, 1), 0:w] if i is not None else m.decay[:, head, 0:w]
                v.tensor_tensor(m.ra[:, TURNED[kb]:TURNED[kb] + w], b[2 + bank][:, at:at + w], decay, ALU.mult).then_inc(s("ret_decayed"), 1)
        if project:
            if hs[0] == 0:
                dve_norm_rstd(m, dve, "ret")
                dve.wait_ge(*m.upto("ret_norm_in", 1))
                dve.wait_ge(*m.upto("ret_tables_in", 16))
            take("q")
        if attend:
            for q in range(TT):
                left_before("values", TT, q + 1)
                v.bn_stats(m.y_stats[:, q, :], b[2 + q][:, :]).then_inc(s("ret_y_stats"), 1)
            left_before("y_stats", TT, TT)
            v.memset(m.y_shift[:, :], 0.0).then_inc(s("ret_y_cleared"), 1)
            for q in range(TT):
                v.bn_aggr(m.y_mean[:, q, :], m.y_stats[:, q, :]).then_inc(s("ret_y_mean"), 1)
            left_before("y_std", 1, 1)
            v.reciprocal(m.y_rstd[:, :], m.y_std[:, :]).then_inc(s("ret_y_rstd"), 1)
            left_before("y_rstd", 1, 1)
            v.scalar_tensor_tensor(out=m.y_shift[:, :], in0=m.y_mean[:, :, 0], scalar=-1.0, in1=m.y_rstd[:, :], op0=ALU.mult, op1=ALU.mult)\
                .then_inc(s("ret_y_shift"), 1)
            left_before("g_in", 2 * TT, 2 * TT)
            for q in range(TT):
                left_before("y_normed", TT, q + 1)
                v.tensor_tensor(m.ry[:, q, :], m.ry[:, q, :], m.rg[:, q, :], ALU.mult).then_inc(s("ret_gated"), 1)
        if project:
            take("k")
        if attend:
            for c in range(4):
                left_before("o_hi", 4, c + 1)
                v.tensor_tensor(m.act_lo[:, c, :], b[2 + c][:, :], m.act_hi[:, c, :].bitcast(F32), ALU.subtract).then_inc(s("ret_o_lo"), 1)

            def add(n):
                dve_add_block(m, dve, "ret", n, b[4 + n % 4], [f"ret.o{n // 4}{h - 1}" for h in hs], n % 4, i, [h - 1 for h in hs], hs[0] == 1)
            if project:
                for n in range(KC):
                    add(n)
            else:
                dve_last_blocks(m, dve, add, "ret", KC * (RH - 1), then)

    step(None, [0], True, False)
    step(None, [1], True, True)
    with dve.Fori(0, RH - 2) as i:
        step(i, list(range(2, RH)), True, True)
    step(None, [RH], False, True)


def dve_end(m, dve):
    s, b, v = m.sem, m.bank, m.nc.vector
    dve.wait_ge(*m.upto("out_norm_std", 1))
    v.reciprocal(m.rcol[:, 0:TT], m.std[:, 0:TT]).then_inc(s("out_rcol"), 1)
    dve.wait_ge(*m.upto("out_rcol", 1))
    dve.wait_ge(*m.upto("gain_in", 16))
    for t in range(TT):
        for half in range(2):
            n = 2 * t + half
            dve.wait_ge(*m.upto("out_turned", n + 1))
            v.scalar_tensor_tensor(out=m.x_tok[:, t, 512 * half:512 * half + 512], in0=b[1 + n % 4][:, :], scalar=m.rcol[:, t:t + 1],
                                   in1=m.gain_final[:, 512 * half:512 * half + 512], op0=ALU.mult, op1=ALU.mult).then_inc(s("out_rows"), 1)


def dve_program(m, dve):
    s = m.sem
    dve_start(m, dve)
    dve.wait_ge(*m.upto("x_scaled", KC))
    dve_pairs(m, dve, "mla", ("mean", "ln0"))
    dve_layernorm(m, dve, "ln0", "ffn0", "ln_mix_g", "ln_mix_b", 0)
    dve_rope(m, dve, "diff", 2)
    dve_relu_mlp(m, dve, "ffn0", "ln0", ("mean", "ln1"))
    dve_layernorm(m, dve, "ln1", "diff", "ln_ffn_g", "ln_ffn_b", 0)
    dve_lambda(m, dve)
    dve.wait_ge(*m.upto("diff_rope_made", 2))
    dve.wait_ge(*m.upto("ln1_done", KC))
    dve_pairs(m, dve, "diff", ("mean", "ln2"))
    dve_layernorm(m, dve, "ln2", "ffn1", "ln_mix_g", "ln_mix_b", 1)
    dve_relu_mlp(m, dve, "ffn1", "ln2", ("mean", "ln3"))
    dve_layernorm(m, dve, "ln3", None, "ln_ffn_g", "ln_ffn_b", 1)
    for k in range(KC):
        dve_input_low(m, dve, "fox", "norm_mix_2", 0, k)
    dve_pairs(m, dve, "fox", ("input", "sw0", "norm_ffn_2", 0))
    dve_swiglu(m, dve, "sw0", ("input", "ret", "norm_mix_2", 1))
    dve_retention(m, dve, ("input", "sw1", "norm_ffn_2", 1))
    dve_swiglu(m, dve, "sw1", ("none",))
    dve_end(m, dve)


def two_blocks(nc, dram):
    with ExitStack() as ctx:
        m = memory(nc, ctx, dram)
        block = ctx.enter_context(nc.Block())

        @block.sync
        def _(sp):
            sp_program(m, sp)

        @block.gpsimd
        def _(pool):
            pool_program(m, pool)

        @block.scalar
        def _(act):
            act_program(m, act)

        @block.tensor
        def _(pe):
            pe_program(m, pe)

        @block.vector
        def _(dve):
            dve_program(m, dve)


def constants():
    at = np.arange(P)
    c = {"c_square": np.zeros((P, 3 * P + 4), np.float32)}
    c["c_square"][:, 0:P] = np.eye(P)
    c["c_square"][:, P:2 * P] = np.where(at[None, :] > at[:, None], MASKED, 0.0)
    c["c_square"][:, 2 * P:3 * P] = at[:, None] <= at[None, :]
    mla = 10000.0 ** (-np.arange(0, ROPE, 2) / ROPE)
    rot = 500000.0 ** (-np.arange(0, 16, 2) / 16)
    c["c_square"][:, 3 * P] = mla[at % 32]
    c["c_square"][:, 3 * P + 1] = np.where(at % 64 < 32, -1.0, 1.0)
    c["c_square"][:, 3 * P + 2] = np.where(at % 64 < 16, rot[at % 8], 0.0)
    c["c_square"][:, 3 * P + 3] = np.where(at % 64 < 8, -1.0, 1.0)
    c["c_sel"] = np.repeat(np.eye(8, dtype=np.float32)[:, :, None], P, axis=2)
    key, query = at[:, None], np.arange(T)[None, :]
    decay = [np.where(key // 64 <= query // 64, (1.0 - 2.0 ** (-5.0 - h)) ** np.abs(query - key), 0.0) for h in range(RH)]
    inv = (10000.0 ** (-np.arange(P) / P)).astype(np.float32)
    ang = np.arange(T, dtype=np.float32)[None, :] * inv[:, None]
    c["c_ret"] = np.concatenate([*decay, np.cos(ang), np.sin(ang)], axis=1).astype(np.float32)
    return c


_INS = ["x", "positions", "ln_mix_g", "ln_mix_b", "mla_w_dq", "mla_q_norm", "mla_w_uq", "mla_w_dkv", "mla_kv_norm", "mla_w_ukv",
        "mla_w_o", "diff_w_qkv", "diff_lambda_q1", "diff_lambda_k1", "diff_lambda_q2", "diff_lambda_k2", "diff_subln", "diff_w_o",
        "ln_ffn_g", "ln_ffn_b", "ffn_w_up", "ffn_w_down", "norm_mix_2", "norm_ffn_2", "fox_w_in_2", "fox_b_f_2", "fox_w_out_2",
        "ret_w_in_2", "ret_w_out_2", "ffn_w_in_2", "ffn_w_out_2", "final_norm_2"]


def kernel(**inputs):
    import concourse.bacc as bacc
    from concourse.bass_utils import run_bass_kernel_spmd

    nc = bacc.Bacc("TRN2", target_bir_lowering=False, num_devices=1)
    arrays, dram = {}, {}
    given = {name: np.ascontiguousarray(inputs[name]) for name in _INS}
    for name, a in {**given, **constants()}.items():
        arrays[f"in_{name}"] = a
        dram[name] = nc.dram_tensor(f"in_{name}", a.shape, mybir.dt.from_np(a.dtype), kind="ExternalInput").ap()
    dram["out"] = nc.dram_tensor("out_0", (1, T, D), F32, kind="ExternalOutput").ap()
    two_blocks(nc, dram)
    r = run_bass_kernel_spmd(nc, [arrays], core_ids=[0])
    return r.results[0]["out_0"]
```

```python
import math
from contextlib import ExitStack

import concourse.bass as bass
import numpy as np
from concourse import mybir

F32 = mybir.dt.float32
F32R = mybir.dt.float32r
I32 = mybir.dt.int32
ACT = mybir.ActivationFunctionType
ALU = mybir.AluOpType
AX = mybir.AxisListType.X

P = 128
T = 512
TT = T // P
D = 1024
KC = D // P
PAIRS = 4
NOPE, ROPE, MV = 128, 64, 128
QL, KVL = 384, 256
FF = 4096
G1 = FF // 256
FF2 = 2816
G2 = FF2 // 256
RH, RDK, RDV = 4, 256, 512
ALPHA = 4 ** 0.25
LN_EPS, RMS_EPS = 1e-5, 1e-6
LAMBDA_INIT = 0.8 - 0.6 * math.exp(-0.3)
MLA_SCALE = (NOPE + ROPE) ** -0.5
DIFF_SCALE = 64 ** -0.5
FOX_SCALE = 128 ** -0.5
RET_SCALE = RDK ** -0.5
SLOT = 3 * 384 + 2 * 512
MASKED = -1e30
TWO_PI = (6.28125, 0.0019340515136718750, 2 * math.pi - 6.28125 - 0.0019340515136718750)
ROUND = 12582912.0

ROWS = {}
for _name, _n in (("ln_mix_g", 16), ("ln_mix_b", 16), ("ln_ffn_g", 16), ("ln_ffn_b", 16), ("norm_mix_2", 16),
                  ("norm_ffn_2", 16), ("mla_q_norm", 3), ("mla_kv_norm", 2), ("diff_subln", 1)):
    ROWS[_name] = (sum(n for _, n in ROWS.values()), _n)
NROWS = sum(n for _, n in ROWS.values())

PLAIN_SCORES = [(q, [(q, 0, 0)]) for q in range(TT)]
DIFF_SCORES = [(1, [(0, 0, 384), (2, 0, 0)]), (4, [(0, 1, 384), (2, 1, 0)]), (2, [(1, 0, 0), (1, 1, 256)]),
               (0, [(3, 0, 0)]), (3, [(3, 1, 0)])]
TURN_AT = {0: (0, 0), 1: (1, 0), 3: (1, 384), 2: (2, 0)}
TURNED = {kb: 512 * b + c for kb, (b, c) in TURN_AT.items()}
PACKED = {q: P * (q * (q + 1) // 2) for q in range(TT)}


def score_tiles(t):
    tiles = []
    for bank, places in DIFF_SCORES if t == "diff" else PLAIN_SCORES:
        end = len(tiles) + len(places)
        tiles += [(q, n, bank, at, end) for q, n, at in places]
    return tiles


def query_tiles(t):
    counts = {}
    for n, (q, *_) in enumerate(score_tiles(t)):
        counts[q] = n + 1
    return sorted(counts.items(), key=lambda x: x[1])


def output_banks(t):
    return (5, 6, 7) if t == "diff" else (4, 5, 6, 7)


def along(i, counts):
    counts = list(counts)
    if i is None:
        assert len(counts) == 1
        return counts[0]
    step = counts[1] - counts[0]
    assert counts == [counts[0] + step * n for n in range(len(counts))] and counts[0] > 0
    return i * step + counts[0] if step else counts[0]


def plan():
    units, blocks = [], []

    def unit(name, dmas=1):
        units.append((name, dmas))

    def done(name, *parts):
        blocks.extend((name, x) for x in parts)

    unit("kv"), done("kv", 0, 1)
    unit("pe", 3), done("pe", 0, 1)
    unit("cq"), done("cq", 0, 1)
    for p in range(PAIRS + 1):
        if p < PAIRS:
            unit(f"mla.p{p}", 5), done(f"mla.p{p}", "q0", "k0", "q1", "k1", "pe", "v0", "v1", "v2", "v3")
        if p:
            unit(f"mla.o{p - 1}"), done(f"mla.o{p - 1}", *range(KC))

    def relu_mlp(t):
        for g in range(G1 + 1):
            if g < G1:
                unit(f"{t}.u{g}"), done(f"{t}.u{g}", 0, 1)
            if g:
                unit(f"{t}.d{g - 1}"), done(f"{t}.d{g - 1}", *range(KC))

    def pairs(t):
        for p in range(PAIRS + 1):
            if p < PAIRS:
                unit(f"{t}.q{p}"), unit(f"{t}.k{p}"), unit(f"{t}.v{p}")
                for j in range(2):
                    done(f"{t}.q{p}", j), done(f"{t}.k{p}", j)
                done(f"{t}.v{p}", *range(TT))
            if p:
                unit(f"{t}.o{p - 1}"), done(f"{t}.o{p - 1}", *range(KC))

    def swiglu(t):
        for g in range(G2 + 1):
            if g < G2:
                unit(f"{t}.g{g}"), done(f"{t}.g{g}", 0, 1)
                unit(f"{t}.u{g}"), done(f"{t}.u{g}", 0, 1)
            if g:
                unit(f"{t}.d{g - 1}"), done(f"{t}.d{g - 1}", *range(KC))

    relu_mlp("ffn0")
    pairs("diff")
    relu_mlp("ffn1")
    pairs("fox")
    swiglu("sw0")
    for h in range(RH + 1):
        if h < RH:
            for x in "qk":
                unit(f"ret.{x}{h}"), done(f"ret.{x}{h}", 0, 1)
            for x in "vg":
                for half in range(2):
                    unit(f"ret.{x}{half}{h}"), done(f"ret.{x}{half}{h}", *range(TT))
        if h:
            for half in range(2):
                unit(f"ret.o{half}{h - 1}"), done(f"ret.o{half}{h - 1}", *range(4))
    swiglu("sw1")
    return units, blocks


UNITS, BLOCKS = plan()
NU = len(UNITS)
INDEX = {name: n for n, (name, _) in enumerate(UNITS)}
BLOCK = {b: n + 1 for n, b in enumerate(BLOCKS)}
UNIT_DONE = {}
for (_name, _), _n in BLOCK.items():
    UNIT_DONE[_name] = max(_n, UNIT_DONE.get(_name, 0))
LANDED, _sum = [], [0, 0]
for _n, (_name, _dmas) in enumerate(UNITS):
    _sum[_n % 2] += 16 * _dmas
    LANDED.append(_sum[_n % 2])

HEADS = 2 * PAIRS
ONCE_PER_HEAD = {"q_in": HEADS, "k_in": HEADS, "o_hi": HEADS, "o_lo": HEADS, "row_rec": TT * HEADS, "values": HEADS,
                 "turned": 3 * HEADS, "turned_in": 3 * HEADS, "probs": TT * HEADS, "v_in": TT * PAIRS, "acc": KC * PAIRS}
SHARED = [
    ("layernorm", ("ln0", "ln1", "ln2", "ln3"),
     {"summed": KC - 1, "mean": 1, "centered": KC, "sq": KC, "sums": 1, "std": 1, "rstd": 1, "scaled": KC, "done": KC}),
    ("input", ("mla", "ffn0", "diff", "ffn1", "fox", "sw0", "ret", "sw1"), {"h_hi": KC, "h_lo": KC}),
    ("rms", ("fox", "sw0", "ret", "sw1"),
     {"sq": KC, "sq_summed": KC - 1, "norm_sums": 1, "norm_std": 1, "norm_rcol": 1, "norm_diag": TT, "norm_spread": 1, "norm_in": 1}),
    ("relu_mlp", ("ffn0", "ffn1"), {"relu": 2 * G1, "squared": 2 * G1, "a_hi": 2 * G1, "a_lo": 2 * G1, "acc": KC * G1}),
    ("swiglu", ("sw0", "sw1"), {"g_in": 2 * G2, "u_in": 2 * G2, "silu": 2 * G2, "prod": 2 * G2, "a_hi": 2 * G2,
                                "a_lo": 2 * G2, "acc": KC * G2}),
    ("softmax", ("mla", "diff", "fox"), ONCE_PER_HEAD),
    ("rope", ("mla", "diff"), {"rope_steps": 8, "rope_abs": 1, "rope_made": 2}),
]
COUNTED = {f"{stage}_{event}": (f"{kind}_{event}", total * n)
           for kind, stages, events in SHARED for n, stage in enumerate(stages) for event, total in events.items()}
for _event in ("scores", "masked", "neg_max", "exps"):
    for _stage, _n in (("mla", 0), ("diff", 1), ("fox", 3)):
        COUNTED[f"{_stage}_{_event}"] = (f"softmax_{_event}", _n * TT * HEADS)


def slot(names):
    s = {INDEX[n] % 2 for n in names}
    assert len(s) == 1
    return s.pop()


def block_done(i, names, part):
    return along(i, [BLOCK[n, part] for n in names])


def after(names, by=1):
    return [UNITS[INDEX[n] + by][0] for n in names]


class Memory:

    def __init__(self, nc, dram):
        self.nc, self.dram = nc, dram


def memory(nc, ctx, dram):
    def sb(name, shape, dt=F32):
        return ctx.enter_context(nc.sbuf_tensor(name, shape, dt))

    m = Memory(nc, dram)
    sems = {}

    def sem(name):
        name = COUNTED.get(name, (name, 0))[0]
        if name not in sems:
            sems[name] = ctx.enter_context(nc.semaphore(name))
        return sems[name]

    def upto(name, n):
        return sem(name), n + COUNTED.get(name, (name, 0))[1]

    m.sem, m.upto = sem, upto
    m.bank = [ctx.enter_context(nc.psum_tensor(f"bank{n}", [P, 512], F32)) for n in range(8)]

    m.w_raw, m.w_hi, m.w_lo = sb("w_raw", [P, 2, SLOT]), sb("w_hi", [P, 2, SLOT], F32R), sb("w_lo", [P, 2, SLOT], F32R)
    m.x = sb("x_residual", [P, KC, T])
    m.h_hi, m.h_lo = sb("h_hi", [P, KC, T], F32R), sb("h_lo", [P, KC, T], F32R)
    m.act_hi, m.act_lo = sb("act_hi", [P, 7, T], F32R), sb("act_lo", [P, 7, T], F32R)
    tok = sb("tokbuf", [P, KC * T])
    m.x_tok = tok[:, :].rearrange("p (t d) -> p t d", t=TT)
    m.sq = tok[:, :].rearrange("p (k t) -> p k t", k=KC)
    m.neg_c = m.sq
    m.decay = tok[:, 0:RH * T].rearrange("p (h t) -> p h t", h=RH)
    m.ret_cos, m.ret_sin = tok[:, RH * T:RH * T + T], tok[:, RH * T + T:RH * T + 2 * T]
    m.ret_tables = tok[:, 0:(RH + 2) * T]

    work = sb("work", [P, 11520])

    def view(at, n, a=None):
        w = work[:, at:at + n]
        return w if a is None else w.rearrange("p (a b) -> p a b", a=a)

    m.rows = view(0, P)
    m.q, m.k, m.v = view(0, 1024, 2), view(1024, 1024, 2), view(2048, 1024, TT)
    m.q_pe, m.k_pe = view(3072, 512), view(3584, 512)
    m.probs, m.probs2, m.turned = view(4096, 1280), view(5376, 1280), view(6656, 1280)
    m.tmp = view(7936, 1536, 3)
    m.sel, m.c_rows = view(5376, 1024, 8), view(3584, 512)
    m.rv, m.rg, m.ra, m.ry, m.rtmp = view(2048, 2048, TT), view(4096, 2048, TT), view(6144, 1280), view(7424, 2048, TT), view(9472, 2048, 4)
    m.relu, m.square = view(0, 1024, 2), view(1024, 1024, 2)
    m.gate, m.silu, m.up, m.prod = view(0, 1024, 2), view(1024, 1024, 2), view(2048, 1024, 2), view(3072, 1024, 2)
    m.out_sq = view(4096, 4096, 8)
    m.rb_q = view(9472, 512)
    m.pos, m.ang, m.turns = view(9984, 512), view(10496, 512), view(11008, 512)

    m.rb = sb("rstd_rows", [P, T])
    m.diag = sb("diag", [P, TT, P])
    m.rope_cos, m.rope_sin = sb("rope_cos", [P, T]), sb("rope_sin", [P, T])
    m.consts = sb("consts", [P, 3 * P + 4])
    m.ident, m.causal, m.tri = (m.consts[:, P * n:P * n + P] for n in range(3))
    m.rope_cols = m.consts[:, 3 * P:3 * P + 4]
    m.ones, m.mean_w = sb("ones", [P, P]), sb("mean_weights", [P, P])
    m.cols = sb("cols", [P, NROWS])
    m.eps = sb("eps", [P, 3])
    m.std, m.rcol = sb("std", [P, 2 * TT]), sb("rstd_cols", [P, 2 * TT])
    m.neg_max, m.row_sum, m.row_rec = sb("neg_max", [P, 8]), sb("row_sum", [P, 8]), sb("row_rec", [P, 8])
    m.lam_in, m.lam = sb("lam_in", [P, 4, 64]), sb("lam", [P, 8])
    m.gain_final = sb("wf_then_gain", [P, D])
    m.wf = m.gain_final[:, :].rearrange("p (k n) -> p k n", k=KC)
    m.wf_hi, m.wf_lo = (a[:, 0:2, :].rearrange("p c t -> p (c t)").rearrange("p (k n) -> p k n", k=KC) for a in (m.act_hi, m.act_lo))
    m.b_f, m.gate_f, m.c_cols = sb("b_f", [P, 8]), sb("gate_f", [P, 6, TT, 8]), sb("c_cols", [P, TT, 8])
    m.y_stats, m.y_mean = sb("y_stats", [P, TT, 6]), sb("y_mean", [P, TT, 2])
    m.y_std, m.y_rstd, m.y_shift = sb("y_std", [P, TT]), sb("y_rstd", [P, TT]), sb("y_shift", [P, TT])
    return m


def col(m, name, n):
    at = ROWS[name][0] + n
    return m.cols[:, at:at + 1]


def weight(m, names, width, kc):
    s = slot(names)
    return tuple(w[:, s, 0:width].rearrange("p (k n) -> p k n", k=kc) for w in (m.w_hi, m.w_lo))


def sp_program(m, sp):
    d, s = m.dram, m.sem

    def raw(names, at, width, kc=None):
        v = m.w_raw[:, slot(names), at:at + width]
        return v.rearrange("p (k n) -> p k n", k=kc) if kc else v

    def load(names, parts, i=None):
        if INDEX[names[0]] >= 2:
            sp.wait_ge(*m.upto("w_lo_ready", along(i, [INDEX[n] - 1 for n in names])))
        for dst, src in parts:
            sp.dma_start(dst, src).then_inc(s(f"w_landed{slot(names)}"), 16)

    def cols(w, first, n):
        return w.rearrange("(k p) n -> p k n", p=P)[:, :, bass.ds(first, n)]

    def rows(w, first, n, c0=0, c1=D):
        return w.rearrange("(k p) n -> p k n", p=P)[:, bass.ds(first, n), c0:c1]

    def wide(names, w, firsts, i=None):
        load(names, [(raw(names, 0, 2048, KC), cols(w, along(i, firsts) if i is not None else firsts[0], 256))], i)

    def tall(names, w, firsts, i=None):
        load(names, [(raw(names, 0, 2048, 2), rows(w, along(i, firsts) if i is not None else firsts[0], 2))], i)

    sp.dma_start(m.consts[:, :], d["c_square"]).then_inc(s("consts_in"), 16)
    wide(["kv"], d["mla_w_dkv"][0], [0])
    for t in range(TT):
        sp.dma_start(m.x_tok[:, t, :], d["x"][0, t * P:(t + 1) * P, :]).then_inc(s(f"x{t}_in"), 16)
    pe_cols = m.w_raw[:, slot(["pe"]), 0:2048].rearrange("p (k n) -> p k n", k=KC)
    load(["pe"], [(pe_cols[:, :, 0:64], cols(d["mla_w_dkv"][0], KVL, ROPE)),
                  (pe_cols[:, :, 64:128], cols(d["mla_w_dkv"][0], KVL, ROPE)),
                  (pe_cols[:, :, 128:256], cols(d["mla_w_dq"][0], 0, P))])
    for name, (at, n) in ROWS.items():
        v = d[name]
        v = v.rearrange("l (k p) -> (l k) p", p=P)
        sp.dma_start(m.rows[at:at + n, :], v).then_inc(s("rows_in"), 16)
    sp.dma_start(m.pos.bitcast(I32), d["positions"].broadcast_to([P, T])).then_inc(s("pos_in"), 16)
    wide(["cq"], d["mla_w_dq"][0], [P])

    def mla_pair(p):
        n = [f"mla.p{p}"]
        uq = raw(n, 0, 1152, 3)
        parts = [(uq[:, :, at:at + width], cols(d["mla_w_uq"][0], p * 2 * (NOPE + ROPE) + first, width)) for at, first, width in
                 ((0, 0, NOPE), (NOPE, NOPE + ROPE, NOPE), (2 * NOPE, NOPE, ROPE), (2 * NOPE + ROPE, 2 * NOPE + ROPE, ROPE))]
        load(n, parts + [(raw(n, 1152, 1024, 2), cols(d["mla_w_ukv"][0], p * 512, 512))])

    mla_pair(0)
    for n, x in enumerate(("q1", "k1", "q2", "k2")):
        sp.dma_start(m.lam_in[:, n, :], d[f"diff_lambda_{x}"].broadcast_to([P, 64])).then_inc(s("lam_in"), 16)
    sp.dma_start(m.wf[:, :, 0:8], cols(d["fox_w_in_2"][0], 3 * D, 8)).then_inc(s("wf_in"), 16)
    sp.dma_start(m.wf[:, :, 8:P], cols(d["fox_w_in_2"][0], 3 * D + 8 - P, P - 8)).then_inc(s("wf_in"), 16)
    sp.dma_start(m.b_f[:, :], d["fox_b_f_2"].broadcast_to([P, 8])).then_inc(s("wf_in"), 16)
    for p in range(1, PAIRS):
        mla_pair(p)
        tall([f"mla.o{p - 1}"], d["mla_w_o"][0], [2 * p - 2])
    tall([f"mla.o{PAIRS - 1}"], d["mla_w_o"][0], [2 * PAIRS - 2])

    def relu_mlp(t, layer, before_loop=None):
        up, down = d["ffn_w_up"][layer], d["ffn_w_down"][layer]
        wide([f"{t}.u0"], up, [0])
        if before_loop:
            before_loop()
        with sp.Fori(0, G1 - 1) as i:
            gs = range(G1 - 1)
            wide([f"{t}.u{g + 1}" for g in gs], up, [256 * (g + 1) for g in gs], i)
            load([f"{t}.d{g}" for g in gs], [(raw([f"{t}.d{g}" for g in gs], 0, 2048, 2), rows(down, i * 2, 2))], i)
        tall([f"{t}.d{G1 - 1}"], down, [2 * (G1 - 1)])

    def pairs(t, w_in, w_out):
        for n, x in enumerate("qkv"):
            wide([f"{t}.{x}0"], w_in, [D * n])
        with sp.Fori(0, PAIRS - 1) as i:
            ps = range(1, PAIRS)
            for n, x in enumerate("qkv"):
                wide([f"{t}.{x}{p}" for p in ps], w_in, [D * n + 256 * p for p in ps], i)
            names = [f"{t}.o{p - 1}" for p in ps]
            load(names, [(raw(names, 0, 2048, 2), rows(w_out, i * 2, 2))], i)
        tall([f"{t}.o{PAIRS - 1}"], w_out, [2 * (PAIRS - 1)])

    def swiglu(t, layer):
        w_in, w_out = d["ffn_w_in_2"][layer], d["ffn_w_out_2"][layer]
        wide([f"{t}.g0"], w_in, [0])
        wide([f"{t}.u0"], w_in, [FF2])
        with sp.Fori(0, (G2 - 1) // 2) as i:
            for e in range(2):
                gs = range(1 + e, G2, 2)
                wide([f"{t}.g{g}" for g in gs], w_in, [256 * g for g in gs], i)
                wide([f"{t}.u{g}" for g in gs], w_in, [FF2 + 256 * g for g in gs], i)
                names = [f"{t}.d{g - 1}" for g in gs]
                load(names, [(raw(names, 0, 2048, 2), rows(w_out, i * 4 + 2 * e, 2))], i)
        tall([f"{t}.d{G2 - 1}"], w_out, [2 * (G2 - 1)])

    def positions_again():
        sp.wait_ge(*m.upto("mla_rope_made", 2))
        sp.dma_start(m.pos.bitcast(I32), d["positions"].broadcast_to([P, T])).then_inc(s("pos_in"), 16)

    relu_mlp("ffn0", 0, positions_again)
    pairs("diff", d["diff_w_qkv"][0], d["diff_w_o"][0])
    relu_mlp("ffn1", 1)

    wide(["fox.q0"], d["fox_w_in_2"][0], [0])
    for n, x in enumerate("kv"):
        wide([f"fox.{x}0"], d["fox_w_in_2"][0], [D * (n + 1)])
    sp.wait_ge(*m.upto("diff_acc", 8 * PAIRS))
    sp.dma_start(m.sel[0:8, :, :], d["c_sel"]).then_inc(s("sel_in"), 16)
    with sp.Fori(0, PAIRS - 1) as i:
        ps = range(1, PAIRS)
        for n, x in enumerate("qkv"):
            wide([f"fox.{x}{p}" for p in ps], d["fox_w_in_2"][0], [D * n + 256 * p for p in ps], i)
        names = [f"fox.o{p - 1}" for p in ps]
        load(names, [(raw(names, 0, 2048, 2), rows(d["fox_w_out_2"][0], i * 2, 2))], i)
    tall([f"fox.o{PAIRS - 1}"], d["fox_w_out_2"][0], [2 * (PAIRS - 1)])

    sp.wait_ge(*m.upto("fox_wf_lo", 1))
    sp.dma_start(m.gain_final[:, :], d["final_norm_2"].rearrange("(a n) -> a n", a=1).broadcast_to([P, D]))\
        .then_inc(s("gain_in"), 16)
    swiglu("sw0", 0)

    w_in, w_out = d["ret_w_in_2"][0], d["ret_w_out_2"][0]

    def ret_head(hs, i=None):
        at = (lambda first, width: along(i, [first + width * h for h in hs]) if i is not None else first + width * hs[0])
        for n, x in enumerate("qk"):
            names = [f"ret.{x}{h}" for h in hs]
            load(names, [(raw(names, 0, 2048, KC), cols(w_in, at(D * n, RDK), 256))], i)
        for n, x in enumerate("vg"):
            for half in range(2):
                names = [f"ret.{x}{half}{h}" for h in hs]
                load(names, [(raw(names, 0, 2048, KC), cols(w_in, at(2 * D + 2 * D * n + 256 * half, RDV), 256))], i)

    def ret_out(hs, i=None):
        for half in range(2):
            names = [f"ret.o{half}{h}" for h in hs]
            first = i * 4 if i is not None else 4 * hs[0]
            load(names, [(raw(names, 0, 2048, 4), rows(w_out, first, 4, 512 * half, 512 * half + 512))], i)

    load(["ret.q0"], [(raw(["ret.q0"], 0, 2048, KC), cols(w_in, 0, 256))])
    for name, first in (("k0", D), ("v00", 2 * D)):
        wide([f"ret.{name}"], w_in, [first])
    sp.wait_ge(*m.upto("ret_norm_sums", 1))
    sp.dma_start(m.ret_tables, d["c_ret"]).then_inc(s("ret_tables_in"), 16)
    for name, first in (("v10", 2 * D + 256), ("g00", 4 * D), ("g10", 4 * D + 256)):
        wide([f"ret.{name}"], w_in, [first])
    with sp.Fori(0, RH - 1) as i:
        ret_head(range(1, RH), i)
        ret_out(range(RH - 1), i)
    ret_out([RH - 1])
    swiglu("sw1", 1)

    for t in range(TT):
        sp.wait_ge(*m.upto("out_rows", 2 * (t + 1)))
        sp.dma_start(d["out"][0, t * P:(t + 1) * P, :], m.x_tok[:, t, :]).then_inc(s("out_stored"), 16)
    sp.wait_ge(*m.upto("out_stored", 16 * TT))


def pool_program(m, pool):
    s, nc = m.sem, m.nc

    def split_low(n, sl, width):
        pool.wait_ge(*m.upto("w_hi_ready", n))
        nc.gpsimd.tensor_tensor(m.w_lo[:, sl, 0:width], m.w_raw[:, sl, 0:width], m.w_hi[:, sl, 0:width].bitcast(F32),
                                ALU.subtract).then_inc(s("w_lo_ready"), 1)

    first_plain = INDEX["ffn0.u0"]
    for n in range(first_plain):
        split_low(n + 1, n % 2, SLOT if UNITS[n][0].startswith("mla.p") else 2048)
    split_low(first_plain + 1, first_plain % 2, 2048)
    rest = NU - first_plain - 1
    assert rest % 2 == 1
    with pool.Fori(0, rest // 2) as i:
        for e in range(2):
            split_low(i * 2 + (first_plain + 2 + e), (first_plain + 1 + e) % 2, 2048)
    split_low(NU, (NU - 1) % 2, 2048)


def pe_weights(m, pe, names, i=None):
    pe.wait_ge(*m.upto("w_lo_ready", along(i, [INDEX[n] + 1 for n in names])))


def pe_features(m, out, w, c0, x, kc, ready=None, done="blocks_done"):
    mm = m.nc.tensor.matmul
    for k in range(kc):
        if ready:
            ready(k)
        hi, lo = w[0][:, k, c0:c0 + P], w[1][:, k, c0:c0 + P]
        mm(out, hi, x[0][:, k, :], start=k == 0, stop=False)
        mm(out, hi, x[1][:, k, :], start=False, stop=False)
        last = mm(out, lo, x[0][:, k, :], start=False, stop=k == kc - 1)
    last.then_inc(m.sem(done), 1)


def pe_tokens(m, out, w, x, kc, t, n=256, c0=0):
    mm = m.nc.tensor.matmul
    for k in range(kc):
        hi, lo = x[0][:, k, t * P:(t + 1) * P], x[1][:, k, t * P:(t + 1) * P]
        mm(out, hi, w[0][:, k, c0:c0 + n], start=k == 0, stop=False)
        mm(out, hi, w[1][:, k, c0:c0 + n], start=False, stop=False)
        last = mm(out, lo, w[0][:, k, c0:c0 + n], start=False, stop=k == kc - 1)
    return last


def pe_first_blocks(m, pe, t, blocks):
    mm = m.nc.tensor.matmul
    for k in range(KC):
        pe.wait_ge(*m.upto(f"{t}_h_hi", k + 1))
        for out, w, c0 in blocks:
            mm(out, w[0][:, k, c0:c0 + P], m.h_hi[:, k, :], start=k == 0, stop=False)
            mm(out, w[1][:, k, c0:c0 + P], m.h_hi[:, k, :], start=False, stop=False)
    for k in range(KC):
        pe.wait_ge(*m.upto(f"{t}_h_lo", k + 1))
        for out, w, c0 in blocks:
            last = mm(out, w[0][:, k, c0:c0 + P], m.h_lo[:, k, :], start=False, stop=k == KC - 1)
            if k == KC - 1:
                last.then_inc(m.sem("blocks_done"), 1)


def pe_sums(m, squares, out):
    for t in range(TT):
        last = m.nc.tensor.matmul(out[:, t:t + 1], squares[:, t * P:(t + 1) * P], m.ones[:, 0:1], start=True, stop=True)
    return last


def pe_spread(m, out):
    for t in range(TT):
        last = m.nc.tensor.matmul(out[:, t * P:(t + 1) * P], m.ones[:, :], m.diag[:, t, :], start=True, stop=True)
    return last


def h_ready(m, pe, t):
    def ready(k):
        pe.wait_ge(*m.upto(f"{t}_h_hi", k + 1))
        pe.wait_ge(*m.upto(f"{t}_h_lo", k + 1))
    return ready


def pe_start(m, pe):
    s, b, nc = m.sem, m.bank, m.nc
    h = (m.h_hi, m.h_lo)
    pe.wait_ge(*m.upto("consts_in", 16))
    for t in range(TT):
        pe.wait_ge(*m.upto(f"x{t}_in", 16))
        for k in range(KC):
            last = nc.tensor.transpose(b[k][:, t * P:(t + 1) * P], m.x_tok[:, t, k * P:(k + 1) * P], m.ident)
            if t == TT - 1:
                last.then_inc(s("x_turned"), 1)
    pe_weights(m, pe, ["kv"])
    pe.wait_ge(*m.upto("x_scaled", 2))
    pe_first_blocks(m, pe, "mla", [(b[j][:, :], weight(m, ["kv"], 2048, KC), j * P) for j in range(2)])
    pe.wait_ge(*m.upto("rows_in", 16 * len(ROWS)))
    pe.wait_ge(*m.upto("x_scaled", KC))
    nc.tensor.transpose(b[7][:, 0:NROWS], m.rows[0:NROWS, :], m.ident[0:NROWS, 0:NROWS]).then_inc(s("cols_turned"), 1)
    for n, name in enumerate(("pe", "cq")):
        pe_weights(m, pe, [name])
        for j in range(2):
            pe_features(m, b[2 + 2 * n + j][:, :], weight(m, [name], 2048, KC), j * P, h, KC)
    pe.wait_ge(*m.upto("set_up", 2))
    for n, (first, summed) in enumerate(((0, 1), (2, 3))):
        pe.wait_ge(*m.upto("lat_sq_summed", summed))
        pe_sums(m, m.sq[:, first, :], b[n][:, 0:TT]).then_inc(s("lat_sums"), 1)
    for n in range(2):
        pe.wait_ge(*m.upto("lat_diag", TT * (n + 1)))
        pe_spread(m, b[n]).then_inc(s("lat_spread"), 1)


def pe_turn(m, pe, t, c):
    s, b, nc = m.sem, m.bank, m.nc
    pe.wait_ge(*m.upto(f"{t}_probs", c(4, 4)))
    for kbs in ((0,), (1, 3), (2,)):
        for kb in kbs:
            bank, at = TURN_AT[kb]
            for q in range(kb, TT):
                src = m.probs[:, PACKED[q] + kb * P:PACKED[q] + kb * P + P]
                last = nc.tensor.transpose(b[bank][:, at + (q - kb) * P:at + (q - kb) * P + P], src, m.ident)
        last.then_inc(s(f"{t}_turned"), 1)


def pe_values(m, pe, t, c, j, out):
    s, nc = m.sem, m.nc
    for n, kb in enumerate((0, 1, 3, 2)):
        pe.wait_ge(*m.upto(f"{t}_turned_in", c(3, (1, 2, 2, 3)[n])))
        w = T - kb * P
        last = nc.tensor.matmul(out[:, kb * P:T], m.v[:, kb, j * P:(j + 1) * P], m.turned[:, TURNED[kb]:TURNED[kb] + w],
                                start=n == 0, stop=n == 3, skip_group_check=True)
    last.then_inc(s(f"{t}_values"), 1)


def pe_pairs(m, pe, t):
    s, b, mm = m.sem, m.bank, m.nc.tensor.matmul
    u0, u1, o_bank = b[5], b[6], b[7]
    h = (m.h_hi, m.h_lo)
    q_lat, kv_lat = (m.act_hi[:, 2:5, :], m.act_lo[:, 2:5, :]), (m.act_hi[:, 0:2, :], m.act_lo[:, 0:2, :])
    heads_out = (m.act_hi[:, 5:7, :], m.act_lo[:, 5:7, :])

    def step(i, ps, project, attend):
        first = ps[0] == 0

        def left(sem, per, more):
            pe.wait_ge(*m.upto(f"{t}_{sem}", along(i, [per * p + more for p in ps])))

        def left_before(sem, per, more):
            pe.wait_ge(*m.upto(f"{t}_{sem}", along(i, [per * (p - 1) + more for p in ps])))

        def output_added(bank):
            n = max(n for n in range(KC) if output_banks(t)[n % len(output_banks(t))] == bank) + 1
            pe.wait_ge(*m.upto(f"{t}_acc", along(i, [KC * (p - 2) + n for p in ps])))

        def per_head(j, back=1):
            def c(per, more):
                return along(i, [per * (2 * (p - back) + j) + more for p in ps])
            return c

        def unit(x):
            return [f"mla.p{p}" if t == "mla" else f"{t}.{x}{p}" for p in ps]

        def parts(x):
            sl = slot(unit(x))
            at, n, k = (0, 1152, 3) if x == "q" else (1152, 1024, 2)
            return tuple(w[:, sl, at:at + n].rearrange("p (k n) -> p k n", k=k) for w in (m.w_hi, m.w_lo))

        q_bank, k_bank, v_bank, rotated_bank = (u0, u0), (u1, u1), (u0, u1), u0
        if first and t == "mla":
            q_bank, k_bank, v_bank, rotated_bank = (u0, b[4]), (u1, o_bank), (b[2], b[3]), b[1]
        elif first:
            q_bank, k_bank, v_bank = (u0, b[0]), (u1, b[1]), (o_bank, u1)

        def queries_and_keys():
            pe_weights(m, pe, unit("k"))
            pe_first_blocks(m, pe, t, [(u0[:, :], weight(m, unit("q"), 2048, KC), 0), (u1[:, :], weight(m, unit("k"), 2048, KC), 0)])

        def queries(j):
            if first:
                pass
            elif j == 1:
                left("q_in", 2, 1)
            elif ps[0] == 1:
                left_before("v_in", TT, TT)
            elif ps[0] > 1:
                output_added(5)
            if t == "mla":
                if j == 0:
                    pe_weights(m, pe, unit("q"), i)
                pe_features(m, q_bank[j][:, :], parts("q"), j * NOPE, q_lat, 3)
            else:
                if j == 0:
                    pe_weights(m, pe, unit("q"), i)
                pe_features(m, q_bank[j][:, :], weight(m, unit("q"), 2048, KC), j * P, h, KC)

        def keys(j):
            if first:
                pass
            elif j == 1:
                left("k_in", 2, 1)
            elif ps[0] == 1:
                left_before("v_in", TT, TT)
            elif ps[0] > 1:
                output_added(6)
            if t == "mla":
                pe_features(m, k_bank[j][:, :], parts("k"), j * (NOPE + MV), kv_lat, 2)
            else:
                if j == 0:
                    pe_weights(m, pe, unit("k"), i)
                pe_features(m, k_bank[j][:, :], weight(m, unit("k"), 2048, KC), j * P, h, KC)

        def rotated_queries():
            if first:
                pe.wait_ge(*m.upto("lat_rows", 2))
            else:
                left("q_in", 2, 2)
            pe_features(m, rotated_bank[:, :], parts("q"), 2 * NOPE, q_lat, 3)

        def values(tile):
            if tile == 0 and t != "mla":
                pe_weights(m, pe, unit("v"), i)
            if tile == 0 and not first:
                left("pe_in", 1, 1) if t == "mla" else left("q_in", 2, 2)
            elif tile == 2 and not (first and t == "mla"):
                left("k_in", 2, 1 if first else 2)
            out = v_bank[tile // 2][:, 256 * (tile % 2):256 * (tile % 2) + 256]
            if t == "mla":
                w = tuple(a.rearrange("p k (j n) -> p k j n", j=2)[:, :, :, NOPE:NOPE + MV] for a in parts("k"))
                for k in range(2):
                    hi, lo = (a[:, k, tile * P:(tile + 1) * P] for a in kv_lat)
                    mm(out, hi, w[0][:, k], start=k == 0, stop=False)
                    mm(out, hi, w[1][:, k], start=False, stop=False)
                    last = mm(out, lo, w[0][:, k], start=False, stop=k == 1)
            else:
                last = pe_tokens(m, out, weight(m, unit("v"), 2048, KC), h, KC, tile)
            last.then_inc(s("blocks_done"), 1)

        def scores(j, back=1):
            ready = left_before if back else left
            second = first and t != "mla"
            ready("q_in", 2, 2 if second else j + 1)
            ready("k_in", 2, 2 if second else j + 1)
            if t == "mla":
                ready("pe_in", 1, 1)
            if t == "mla" and first:
                left("v_in", TT, TT)
            for nth, (q, n, bank, at, _) in enumerate(score_tiles(t)):
                w = (q + 1) * P
                tile = slice(q * P, (q + 1) * P)
                out = b[bank][:, at:at + w]
                if t == "diff":
                    half = slice(64 * n, 64 * n + 64)
                    if (n, bank) == (1, 2):
                        pe.wait_ge(*m.upto("diff_scores", per_head(j, back)(2 * TT, nth)))
                    mm(out, m.q[half, j, tile], m.k[half, j, 0:w], start=True, stop=True).then_inc(s("diff_scores"), 1)
                    continue
                last = mm(out, m.q[:, j, tile], m.k[:, j, 0:w], start=True, stop=t != "mla")
                if t == "mla":
                    half = slice(ROPE * j, ROPE * j + ROPE)
                    last = mm(out, m.q_pe[half, tile], m.k_pe[half, 0:w], start=False, stop=True)
                last.then_inc(s(f"{t}_scores"), 1)

        def attention(j):
            c = per_head(j)
            pe_turn(m, pe, t, c)
            if j == 1:
                pe.wait_ge(*m.upto("diff_o_taken" if t == "diff" else f"{t}_o_lo", c(1, 0)))
            elif ps[0] > 1:
                output_added(7)
            else:
                left_before("k_in", 2, 2)
            left_before("v_in", TT, TT)
            pe_values(m, pe, t, c, j, o_bank)

        def head_sums(j):
            if t == "diff" and attend:
                pe.wait_ge(*m.upto("diff_o_sq", per_head(j)(1, 1)))
                pe_sums(m, m.tmp[:, 1, :], o_bank[:, 0:TT]).then_inc(s("diff_sub_sums"), 1)

        def head_spread(j):
            if t == "diff" and attend:
                pe.wait_ge(*m.upto("diff_sub_diag", per_head(j)(TT, TT)))
                pe_spread(m, o_bank).then_inc(s("diff_sub_spread"), 1)

        def output():
            names = [f"{t}.o{p - 1}" for p in ps]
            pe_weights(m, pe, names, i)
            if project:
                left("v_in", TT, TT)
            left_before("o_lo", 2, 2)
            banks = output_banks(t)
            for n in range(KC):
                if n >= len(banks):
                    left_before("acc", KC, n - len(banks) + 1)
                pe_features(m, b[banks[n % len(banks)]][:, :], weight(m, names, 2048, 2), n * P, heads_out, 2)

        gates = pe_fox_gates(m, pe) if t == "fox" and first else [lambda: None] * 5
        if first and t != "mla":
            queries_and_keys()
        elif project:
            queries(0), keys(0)
        if attend:
            attention(0), scores(1)
        if project:
            queries(1), gates[0]()
        head_sums(0)
        if project:
            keys(1), gates[1]()
            if t == "mla":
                rotated_queries()
        head_spread(0)
        if attend:
            attention(1)
        if project:
            values(0)
        head_sums(1)
        if project:
            values(1), gates[2](), values(2)
        head_spread(1)
        if project:
            values(3), gates[3](), gates[4]()
            scores(0, back=0)
        if attend:
            output()

    if t == "mla":
        pe.wait_ge(*m.upto("lat_lo", 5))
    step(None, [0], True, False)
    step(None, [1], True, True)
    with pe.Fori(0, PAIRS - 2) as i:
        step(i, list(range(2, PAIRS)), True, True)
    step(None, [PAIRS], False, True)


def pe_fox_gates(m, pe):
    s, b, mm, nc = m.sem, m.bank, m.nc.tensor.matmul, m.nc

    def norm_sums_and_logits():
        pe_norm_sums(m, pe, "fox", b[4])
        pe.wait_ge(*m.upto("fox_wf_lo", 1))
        pe_features(m, b[2][:, :], (m.wf_hi, m.wf_lo), 0, (m.h_hi, m.h_lo), KC, done="fox_logits")

    def norm_spread_and_turn_logits():
        pe_norm_spread(m, pe, "fox", b[3])
        pe.wait_ge(*m.upto("fox_logit_rows", 1))
        for t in range(TT):
            last = nc.tensor.transpose(b[2][:, 8 * t:8 * t + 8], m.c_rows[0:8, t * P:(t + 1) * P], m.ident[0:8, 0:8])
        last.then_inc(s("fox_logits_turned"), 1)

    def running_sums():
        pe.wait_ge(*m.upto("fox_log_f", 1))
        for q in range(TT):
            for t in range(q + 1):
                last = mm(b[4][:, 128 + 8 * q:136 + 8 * q], m.tri if t == q else m.ones[:, :], m.gate_f[:, 2, t, :],
                          start=t == 0, stop=t == q)
        last.then_inc(s("fox_sums"), 1)

    def turn_sums():
        pe.wait_ge(*m.upto("fox_c_cols", 1))
        for t in range(TT):
            last = nc.tensor.transpose(b[0][0:8, t * P:(t + 1) * P], m.c_cols[:, t, :], m.ident)
        last.then_inc(s("fox_c_turned"), 1)

    def spread_sums():
        pe.wait_ge(*m.upto("fox_c_rows", 1))
        pe.wait_ge(*m.upto("sel_in", 16))
        pe.wait_ge(*m.upto("fox_v_in", 2))
        for n in range(8):
            if n >= 2:
                pe.wait_ge(*m.upto("fox_neg_c", n - 1))
            mm(b[4 + 3 * (n % 2)][:, :], m.sel[0:8, n, :], m.c_rows[0:8, :], start=True, stop=True).then_inc(s("fox_c_spread"), 1)

    return [norm_sums_and_logits, norm_spread_and_turn_logits, running_sums, turn_sums, spread_sums]


def pe_layernorm(m, pe, t, done, count):
    s, b = m.sem, m.bank
    pe.wait_ge(*m.upto(f"{t}_summed", KC - 1))
    m.nc.tensor.matmul(b[0][:, :], m.mean_w[:, :], m.rb[:, :], start=True, stop=False)
    pe.wait_ge(*m.upto(done, count))
    m.nc.tensor.matmul(b[0][:, :], m.mean_w[:, :], m.x[:, KC - 1, :], start=False, stop=True).then_inc(s(f"{t}_mean"), 1)
    for k in range(KC):
        pe.wait_ge(*m.upto(f"{t}_sq", k + 1))
        last = m.nc.tensor.matmul(b[1][:, :], m.ones[:, :], m.sq[:, k, :], start=k == 0, stop=k == KC - 1)
    last.then_inc(s(f"{t}_sums"), 1)


def pe_relu_mlp(m, pe, t):
    b = m.bank
    h = (m.h_hi, m.h_lo)

    def up(gs, i=None):
        names = [f"{t}.u{g}" for g in gs]
        pe_weights(m, pe, names, i)
        w = weight(m, names, 2048, KC)
        if gs[0] == 0:
            pe_first_blocks(m, pe, t, [(b[j][:, :], w, j * P) for j in range(2)])
            return
        for j in range(2):
            pe.wait_ge(*m.upto(f"{t}_relu", along(i, [2 * g + j - 1 for g in gs])))
            pe_features(m, b[j][:, :], w, j * P, h, KC)

    def down(gs, i=None):
        names = [f"{t}.d{g}" for g in gs]
        at = 2 * (gs[0] % 2)
        pe_weights(m, pe, names, i)
        pe.wait_ge(*m.upto(f"{t}_a_lo", along(i, [2 * g + 2 for g in gs])))
        for n in range(KC):
            if gs[0] or n >= 4:
                pe.wait_ge(*m.upto(f"{t}_acc", along(i, [KC * g + n - 3 for g in gs])))
            pe_features(m, b[4 + n % 4][:, :], weight(m, names, 2048, 2), n * P,
                        (m.act_hi[:, at:at + 2, :], m.act_lo[:, at:at + 2, :]), 2)

    up([0])
    up([1])
    down([0])
    with pe.Fori(0, (G1 - 2) // 2) as i:
        for e in range(2):
            up(range(2 + e, G1, 2), i)
            down(range(1 + e, G1 - 1, 2), i)
    down([G1 - 1])


def pe_swiglu(m, pe, t):
    b = m.bank
    h = (m.h_hi, m.h_lo)

    def wide(x, gs, i, j):
        first = x == "g" and gs[0] == 0 and j == 0
        names = [f"{t}.{x}{g}" for g in gs]
        if j == 0:
            pe_weights(m, pe, names, i)
        if gs[0]:
            pe.wait_ge(*m.upto(f"{t}_{x}_in", along(i, [2 * g + j - 1 for g in gs])))
        pe_features(m, b[j + 2 * (x == "u")][:, :], weight(m, names, 2048, KC), j * P, h, KC, h_ready(m, pe, t) if first else None)

    def down(gs, i=None):
        names = [f"{t}.d{g}" for g in gs]
        at = 2 * (gs[0] % 2)
        pe_weights(m, pe, names, i)
        pe.wait_ge(*m.upto(f"{t}_a_lo", along(i, [2 * g + 2 for g in gs])))
        for n in range(KC):
            if gs[0] or n >= 4:
                pe.wait_ge(*m.upto(f"{t}_acc", along(i, [KC * g + n - 3 for g in gs])))
            pe_features(m, b[4 + n % 4][:, :], weight(m, names, 2048, 2), n * P,
                        (m.act_hi[:, at:at + 2, :], m.act_lo[:, at:at + 2, :]), 2)

    for j in range(2):
        wide("g", [0], None, j)
    pe_norm_sums(m, pe, t, b[5])
    wide("u", [0], None, 0)
    pe_norm_spread(m, pe, t, b[4])
    wide("u", [0], None, 1)
    for x in "gu":
        for j in range(2):
            wide(x, [1], None, j)
    down([0])
    with pe.Fori(0, (G2 - 3) // 2) as i:
        for e in range(2):
            gs = range(2 + e, G2 - 1, 2)
            for x in "gu":
                for j in range(2):
                    wide(x, gs, i, j)
            down(range(1 + e, G2 - 2, 2), i)
    for x in "gu":
        for j in range(2):
            wide(x, [G2 - 1], None, j)
    down([G2 - 2])
    down([G2 - 1])


def pe_norm_sums(m, pe, t, bank):
    pe.wait_ge(*m.upto(f"{t}_sq_summed", KC - 1))
    pe_sums(m, m.sq[:, 0, :], bank[:, 0:TT]).then_inc(m.sem(f"{t}_norm_sums"), 1)


def pe_norm_spread(m, pe, t, bank):
    pe.wait_ge(*m.upto(f"{t}_norm_diag", TT))
    pe_spread(m, bank).then_inc(m.sem(f"{t}_norm_spread"), 1)


def pe_retention(m, pe):
    s, b, mm, nc = m.sem, m.bank, m.nc.tensor.matmul, m.nc
    h = (m.h_hi, m.h_lo)

    def step(i, hs, project, attend):
        first = hs[0] == 0

        def left(sem, per, more):
            pe.wait_ge(*m.upto(f"ret_{sem}", along(i, [per * x + more for x in hs])))

        def left_before(sem, per, more):
            pe.wait_ge(*m.upto(f"ret_{sem}", along(i, [per * (x - 1) + more for x in hs])))

        def features(x, j):
            names = [f"ret.{x}{n}" for n in hs]
            if j == 0:
                pe_weights(m, pe, names, i)
            if x == "k" and not first:
                left("q_in", 2, j + 1)
            elif not first:
                left_before("g_in", 2 * TT, 2 * TT)
            bank = b[2 + j] if first and x == "k" else b[j]
            pe_features(m, bank[:, :], weight(m, names, 2048, KC), j * P, h, KC,
                        h_ready(m, pe, "ret") if first and x == "q" and j == 0 else None)

        def tokens(x, half):
            names = [f"ret.{x}{half}{n}" for n in hs]
            pe_weights(m, pe, names, i)
            for t in range(TT):
                if x == "v" and half == 0:
                    if t < 2:
                        left("q_in" if first else "k_in", 2, t + 1)
                    elif hs[0] > 1:
                        pe.wait_ge(*m.upto("ret_acc", along(i, [KC * (n - 2) + KC for n in hs])))
                else:
                    before = ("v", 0) if half else ("v", 1)
                    if x == "v" or half == 0:
                        left("v_in", 2 * TT, TT * before[1] + t + 1)
                    else:
                        left("g_in", 2 * TT, t + 1)
                pe_tokens(m, b[(0, 1, 6, 7)[t]][:, 0:256], weight(m, names, 2048, KC), h, KC, t).then_inc(s("blocks_done"), 1)

        def scores():
            left_before("k_roped", 1, 1)
            for kb in (0, 1, 3, 2):
                bank, at = TURN_AT[kb]
                if kb == 2 and hs[0] > 1:
                    pe.wait_ge(*m.upto("ret_acc", along(i, [KC * (n - 2) + 5 for n in hs])))
                for j in range(2):
                    last = mm(b[2 + bank][:, at:at + T - kb * P], m.k[:, j, kb * P:(kb + 1) * P], m.q[:, j, kb * P:T],
                              start=j == 0, stop=j == 1)
                last.then_inc(s("ret_scores"), 1)

        def values():
            left_before("decayed", TT, TT)
            left_before("v_in", 2 * TT, 2 * TT)
            for q in range(TT):
                if q == 3 and hs[0] > 1:
                    pe.wait_ge(*m.upto("ret_acc", along(i, [KC * (n - 2) + 6 for n in hs])))
                for kb in range(q + 1):
                    at = TURNED[kb] + (q - kb) * P
                    last = mm(b[2 + q][:, :], m.ra[:, at:at + P], m.rv[:, kb, :], start=kb == 0, stop=kb == q)
                last.then_inc(s("ret_values"), 1)

        def turn():
            left_before("gated", TT, TT)
            for c in range(4):
                for q in range(TT):
                    last = nc.tensor.transpose(b[2 + c][:, q * P:(q + 1) * P], m.ry[:, q, c * P:(c + 1) * P], m.ident)
                last.then_inc(s("ret_turned"), 1)

        def output():
            left_before("o_lo", 4, 4)
            for half in range(2):
                names = [f"ret.o{half}{n - 1}" for n in hs]
                pe_weights(m, pe, names, i)
                for n in range(4):
                    if half:
                        left_before("acc", KC, n + 1)
                    elif n >= 2 and project:
                        left("g_in", 2 * TT, TT + n + 1)
                    pe_features(m, b[4 + n][:, :], weight(m, names, 2048, 4), n * P,
                                (m.act_hi[:, 0:4, :], m.act_lo[:, 0:4, :]), 4)

        if attend:
            scores()
        if project:
            features("q", 0), features("q", 1)
        if first:
            pe_norm_sums(m, pe, "ret", b[5])
        if attend:
            values()
        if project:
            features("k", 0)
        if first:
            pe_norm_spread(m, pe, "ret", b[4])
        if project:
            features("k", 1)
        if attend:
            turn()
        if project:
            for x in "vg":
                tokens(x, 0), tokens(x, 1)
        if attend:
            output()

    step(None, [0], True, False)
    step(None, [1], True, True)
    with pe.Fori(0, RH - 2) as i:
        step(i, list(range(2, RH)), True, True)
    step(None, [RH], False, True)


def pe_end(m, pe):
    s, b = m.sem, m.bank
    for half in range(2):
        pe.wait_ge(*m.upto("sw1_acc", KC * (G2 - 1) + 4 * half + 4))
        for t in range(TT):
            for k in range(4):
                last = m.nc.tensor.transpose(b[4 * half + t][:, k * P:(k + 1) * P], m.x[:, 4 * half + k, t * P:(t + 1) * P], m.ident)
            last.then_inc(s("out_turned"), 1)


def pe_program(m, pe):
    pe_start(m, pe)
    pe_pairs(m, pe, "mla")
    pe_layernorm(m, pe, "ln0", "mla_acc", KC * PAIRS)
    pe_relu_mlp(m, pe, "ffn0")
    pe_layernorm(m, pe, "ln1", "ffn0_acc", KC * G1)
    pe_pairs(m, pe, "diff")
    pe_layernorm(m, pe, "ln2", "diff_acc", KC * PAIRS)
    pe_relu_mlp(m, pe, "ffn1")
    pe_layernorm(m, pe, "ln3", "ffn1_acc", KC * G1)
    pe_pairs(m, pe, "fox")
    pe_swiglu(m, pe, "sw0")
    pe_retention(m, pe)
    pe_swiglu(m, pe, "sw1")
    pe_end(m, pe)


def act_split(m, act, names, i=None):
    n0, sl = INDEX[names[0]], slot(names)
    width = SLOT if names[0].startswith("mla.p") else 2048
    act.wait_ge(*m.upto(f"w_landed{sl}", along(i, [LANDED[INDEX[n]] for n in names])))
    if n0 >= 2:
        act.wait_ge(*m.upto("blocks_done", along(i, [UNIT_DONE[UNITS[INDEX[n] - 2][0]] for n in names])))
    m.nc.scalar.activation(m.w_hi[:, sl, 0:width], m.w_raw[:, sl, 0:width], ACT.Copy).then_inc(m.sem("w_hi_ready"), 1)


def act_rope(m, act, t, steps):
    s, run = m.sem, m.nc.scalar.activation
    c = 2 * (t == "diff")
    act.wait_ge(*m.upto(f"{t}_rope_steps", steps))
    act.wait_ge(*m.upto("set_up", 5))
    run(m.rope_sin[:, :], m.ang, ACT.Sin, scale=m.rope_cols[:, c + 1:c + 2]).then_inc(s(f"{t}_rope_made"), 1)
    run(m.turns, m.ang, ACT.Abs).then_inc(s(f"{t}_rope_abs"), 1)
    act.wait_ge(*m.upto(f"{t}_rope_abs", 1))
    run(m.rope_cos[:, :], m.turns, ACT.Sin, scale=-1.0, bias=m.eps[:, 2:3]).then_inc(s(f"{t}_rope_made"), 1)


def act_start(m, act):
    s, b, run = m.sem, m.bank, m.nc.scalar.activation
    act_split(m, act, ["kv"])

    def residual(k):
        act.wait_ge(*m.upto("mla_h_lo", k + 1))
        run(m.x[:, k, :], b[k][:, :], ACT.Copy, scale=ALPHA).then_inc(s("x_scaled"), 1)

    for k in range(KC):
        act.wait_ge(*m.upto("x_turned", k + 1))
        run(m.h_hi[:, k, :], b[k][:, :], ACT.Copy).then_inc(s("mla_h_hi"), 1)
        if k >= 2:
            residual(k - 2)
    act_split(m, act, ["pe"])
    for k in range(KC - 2, KC):
        residual(k)
    act.wait_ge(*m.upto("cols_turned", 1))
    run(m.cols[:, :], b[7][:, 0:NROWS], ACT.Copy).then_inc(s("cols_in"), 1)
    act_rope(m, act, "mla", ROPE_STEPS)
    act_split(m, act, ["cq"])

    def latent(n, bank, name, part, gain, at):
        act.wait_ge(*m.upto("blocks_done", BLOCK[name, part]))
        if n == 0:
            act.wait_ge(*m.upto("cols_in", 1))
        run(m.act_hi[:, n, :], bank[:, :], ACT.Copy, scale=col(m, gain, at)).then_inc(s("lat_hi"), 1)
        run(m.sq[:, n, :], bank[:, :], ACT.Square).then_inc(s("lat_sq"), 1)

    latent(0, b[0], "kv", 0, "mla_kv_norm", 0)
    latent(1, b[1], "kv", 1, "mla_kv_norm", 1)
    latent(2, b[3], "pe", 1, "mla_q_norm", 0)
    act_split(m, act, ["mla.p0"])
    latent(3, b[4], "cq", 0, "mla_q_norm", 1)
    latent(4, b[5], "cq", 1, "mla_q_norm", 2)
    for n, width in enumerate((KVL, QL)):
        act.wait_ge(*m.upto("lat_sums", n + 1))
        run(m.std[:, TT * n:TT * n + TT], b[n][:, 0:TT], ACT.Sqrt, scale=1 / width, bias=m.eps[:, 1:2])\
            .then_inc(s("lat_std"), 1)
    for n, (bank, rows) in enumerate(((b[0], m.rb[:, :]), (b[1], m.rb_q))):
        act.wait_ge(*m.upto("lat_spread", n + 1))
        run(rows, bank[:, :], ACT.Copy).then_inc(s("lat_rows"), 1)


def act_std(m, act, t, bank):
    s, run = m.sem, m.nc.scalar.activation
    act.wait_ge(*m.upto(f"{t}_norm_sums", 1))
    run(m.std[:, 0:TT], bank[:, 0:TT], ACT.Sqrt, scale=1 / D, bias=m.eps[:, 1:2]).then_inc(s(f"{t}_norm_std"), 1)


def act_rows(m, act, t, bank):
    act.wait_ge(*m.upto(f"{t}_norm_spread", 1))
    m.nc.scalar.activation(m.rb[:, :], bank[:, :], ACT.Copy).then_inc(m.sem(f"{t}_norm_in"), 1)


def act_input(m, act, t, done, count, gain, row):
    s, run = m.sem, m.nc.scalar.activation
    for k in range(KC):
        act.wait_ge(*m.upto(done, count + k + 1))
        run(m.h_hi[:, k, :], m.x[:, k, :], ACT.Copy, scale=col(m, gain, KC * row + k)).then_inc(s(f"{t}_h_hi"), 1)
        run(m.sq[:, k, :], m.x[:, k, :], ACT.Square).then_inc(s(f"{t}_sq"), 1)


def act_layernorm(m, act, t, to, shift, row, second):
    s, run = m.sem, m.nc.scalar.activation
    for k in range(KC):
        act.wait_ge(*m.upto(f"{t}_centered", k + 1))
        run(m.sq[:, k, :], m.x[:, k, :], ACT.Square).then_inc(s(f"{t}_sq"), 1)
    act_split(m, act, [second])
    if to == "fox":
        act.wait_ge(*m.upto("wf_in", 48))
        run(m.wf_hi, m.wf[:, :, :], ACT.Copy).then_inc(s("fox_wf_hi"), 1)
    act.wait_ge(*m.upto(f"{t}_sums", 1))
    run(m.rb[:, :], m.bank[1][:, :], ACT.Sqrt, scale=1 / D, bias=m.eps[:, 0:1]).then_inc(s(f"{t}_std"), 1)
    for k in range(KC):
        act.wait_ge(*m.upto(f"{t}_scaled", k + 1))
        if to != "fox":
            run(m.h_hi[:, k, :], m.x[:, k, :], ACT.Identity, bias=col(m, shift, KC * row + k)).then_inc(s(f"{to}_h_hi"), 1)
            continue
        run(m.x[:, k, :], m.x[:, k, :], ACT.Identity, bias=col(m, shift, KC * row + k)).then_inc(s(f"{t}_done"), 1)
        act.wait_ge(*m.upto(f"{t}_done", k + 1))
        run(m.h_hi[:, k, :], m.x[:, k, :], ACT.Copy, scale=col(m, "norm_mix_2", k)).then_inc(s("fox_h_hi"), 1)


def act_pairs(m, act, t):
    s, b, run = m.sem, m.bank, m.nc.scalar.activation
    u0, u1, o_bank = b[5], b[6], b[7]

    def step(i, ps, project, attend):
        def per_head(j, back=1):
            def c(per, more):
                return along(i, [per * (2 * (p - back) + j) + more for p in ps])
            return c

        def exps(j, back=1):
            c = per_head(j, back)
            maps = 2 if t == "diff" else 1
            for q, n, bank, at, end in score_tiles(t):
                w = (q + 1) * P
                out = (m.probs, m.probs2)[n][:, PACKED[q]:PACKED[q] + w]
                src = out if t == "fox" else b[bank][:, at:at + w]
                act.wait_ge(*m.upto(f"{t}_neg_max", c(TT * maps, end)))
                run(out, src, ACT.Exp, bias=m.neg_max[:, maps * q + n:maps * q + n + 1],
                    accum_out=m.row_sum[:, maps * q + n:maps * q + n + 1]).then_inc(s(f"{t}_exps"), 1)

        def turned(j):
            for n, w in enumerate((512, 512, 256)):
                act.wait_ge(*m.upto(f"{t}_turned", per_head(j)(3, n + 1)))
                run(m.turned[:, 512 * n:512 * n + w], b[n][:, 0:w], ACT.Copy).then_inc(s(f"{t}_turned_in"), 1)

        def head_out(j):
            act.wait_ge(*m.upto(f"{t}_values", per_head(j)(1, 1)))
            if t == "diff":
                run(m.tmp[:, 0, :], o_bank[:, :], ACT.Copy).then_inc(s("diff_o_raw"), 1)
                run(m.tmp[:, 1, :], o_bank[:, :], ACT.Square).then_inc(s("diff_o_sq"), 1)
            else:
                run(m.act_hi[:, 5 + j, :], o_bank[:, :], ACT.Copy).then_inc(s(f"{t}_o_hi"), 1)

        def head_std(j):
            if t == "diff" and attend:
                act.wait_ge(*m.upto("diff_sub_sums", per_head(j)(1, 1)))
                run(m.std[:, 0:TT], o_bank[:, 0:TT], ACT.Sqrt, scale=1 / 128, bias=m.eps[:, 1:2]).then_inc(s("diff_sub_std"), 1)

        def head_hi(j):
            if t == "diff" and attend:
                act.wait_ge(*m.upto("diff_o_taken", per_head(j)(1, 1)))
                run(m.act_hi[:, 5 + j, :], m.tmp[:, 2, :], ACT.Copy).then_inc(s("diff_o_hi"), 1)

        def values(tiles):
            names = [f"mla.p{p}" if t == "mla" else f"{t}.v{p}" for p in ps]
            banks = (u0, u1) if ps[0] else (b[2], b[3]) if t == "mla" else (o_bank, u1)
            for tile in tiles:
                part = tile | 1
                act.wait_ge(*m.upto("blocks_done", block_done(i, names, f"v{part}" if t == "mla" else part)))
                src = banks[tile // 2][:, 256 * (tile % 2):256 * (tile % 2) + 256]
                scale = 1.0 if t == "diff" else m.rcol[:, tile:tile + 1]
                run(m.v[:, tile, :], src, ACT.Copy, scale=scale).then_inc(s(f"{t}_v_in"), 1)

        def split(names):
            act_split(m, act, names, i)

        if t == "mla" and attend:
            split([f"mla.o{p - 1}" for p in ps] if project else after(["mla.o3"]))
        if t == "mla" and project and not attend:
            split(["mla.p1"])
        if t == "fox" and ps[0] == 0:
            act_fox_gates(m, act, lambda: split(["fox.v0"]), lambda: split(["fox.q1"]))
        if attend:
            turned(0), head_out(0), exps(1)
        head_std(0)
        if project and t != "mla" and not (t == "fox" and ps[0] == 0):
            split([f"{t}.v{p}" for p in ps])
        head_hi(0)
        if attend:
            turned(1), head_out(1)
        if project and t != "mla" and not (t == "fox" and ps[0] == 0):
            split([f"{t}.o{p - 1}" for p in ps] if attend else [f"{t}.q1"])
        if project:
            values([0, 1])
        head_std(1)
        if project:
            values([2])
        head_hi(1)
        if project:
            values([3])
            if t == "fox" and ps[0] == 0:
                act_fox_sums(m, act)
            if t != "mla" and not attend:
                split([f"{t}.k1"])
            exps(0, back=0)
            if t == "mla" and attend:
                split([f"mla.p{p + 1}" if p < PAIRS - 1 else f"mla.o{p}" for p in ps])
            elif attend:
                last = [f"{t}.o{p - 1}" for p in ps]
                split(after(last, 1))
                split(after(last, 2))

    step(None, [0], True, False)
    step(None, [1], True, True)
    with act.Fori(0, PAIRS - 2) as i:
        step(i, list(range(2, PAIRS)), True, True)
    step(None, [PAIRS], False, True)


def act_fox_gates(m, act, split_v, split_q):
    s, b, run = m.sem, m.bank, m.nc.scalar.activation
    act_std(m, act, "fox", b[4])
    split_v()
    act.wait_ge(*m.upto("fox_logits", 1))
    run(m.c_rows[0:8, :], b[2][0:8, :], ACT.Copy).then_inc(s("fox_logit_rows"), 1)
    act_rows(m, act, "fox", b[3])
    e = m.gate_f[:, 1, :, :]
    act.wait_ge(*m.upto("fox_z", TT))
    run(e, m.gate_f[:, 0, :, :], ACT.Abs).then_inc(s("fox_gate_steps"), 1)
    act.wait_ge(*m.upto("fox_gate_steps", 1))
    run(e, e, ACT.Exp, scale=-1.0).then_inc(s("fox_gate_steps"), 1)
    act.wait_ge(*m.upto("fox_log1p", 1))
    run(m.gate_f[:, 3, :, :], m.gate_f[:, 4, :, :], ACT.Ln).then_inc(s("fox_gate_steps"), 1)
    split_q()
    act.wait_ge(*m.upto("fox_c_turned", 1))
    run(m.c_rows[0:8, :], b[0][0:8, :], ACT.Copy, scale=-1.0).then_inc(s("fox_c_rows"), 1)


def act_fox_sums(m, act):
    s = m.sem
    for n in range(8):
        act.wait_ge(*m.upto("fox_c_spread", n + 1))
        m.nc.scalar.activation(m.neg_c[:, n, :], m.bank[4 + 3 * (n % 2)][:, :], ACT.Copy).then_inc(s("fox_neg_c"), 1)


def act_relu_mlp(m, act, t):
    s, b, run = m.sem, m.bank, m.nc.scalar.activation

    def up(gs, i=None):
        names = [f"{t}.u{g}" for g in gs]
        if gs[0]:
            act_split(m, act, after(names), i)
        for j in range(2):
            act.wait_ge(*m.upto("blocks_done", block_done(i, names, j)))
            if gs[0]:
                act.wait_ge(*m.upto(f"{t}_squared", along(i, [2 * g + j - 1 for g in gs])))
            run(m.relu[:, j, :], b[j][:, :], ACT.Relu).then_inc(s(f"{t}_relu"), 1)
            act.wait_ge(*m.upto(f"{t}_relu", along(i, [2 * g + j + 1 for g in gs])))
            run(m.act_hi[:, 2 * (gs[0] % 2) + j, :], m.relu[:, j, :], ACT.Square).then_inc(s(f"{t}_a_hi"), 1)

    def down(gs, i=None):
        act_split(m, act, after([f"{t}.d{g}" for g in gs]), i)

    up([0])
    up([1])
    if t == "ffn0":
        act.wait_ge(*m.upto("mla_pe_in", PAIRS))
        act_rope(m, act, "diff", ROPE_STEPS)
    down([0])
    with act.Fori(0, (G1 - 2) // 2) as i:
        for e in range(2):
            up(range(2 + e, G1, 2), i)
            down(range(1 + e, G1 - 1, 2), i)
    down([G1 - 1])


def act_swiglu(m, act, t, last):
    s, b, run = m.sem, m.bank, m.nc.scalar.activation

    def gate(gs, i=None):
        act_split(m, act, after([f"{t}.g{g}" for g in gs]), i)
        if gs[0] == 0:
            act_std(m, act, t, b[5])
            act_rows(m, act, t, b[4])
        for j in range(2):
            act.wait_ge(*m.upto(f"{t}_g_in", along(i, [2 * g + j + 1 for g in gs])))
            run(m.silu[:, j, :], m.gate[:, j, :], ACT.Silu).then_inc(s(f"{t}_silu"), 1)

    def up(gs, i=None):
        act_split(m, act, after([f"{t}.u{g}" for g in gs]), i)
        for j in range(2):
            act.wait_ge(*m.upto(f"{t}_prod", along(i, [2 * g + j + 1 for g in gs])))
            run(m.act_hi[:, 2 * (gs[0] % 2) + j, :], m.prod[:, j, :], ACT.Copy).then_inc(s(f"{t}_a_hi"), 1)

    def down(gs, i=None):
        if not (last and gs[-1] == G2 - 1):
            act_split(m, act, after([f"{t}.d{g}" for g in gs]), i)

    gate([0]), up([0])
    gate([1]), up([1]), down([0])
    with act.Fori(0, (G2 - 3) // 2) as i:
        for e in range(2):
            gs = range(2 + e, G2 - 1, 2)
            gate(gs, i), up(gs, i), down(range(1 + e, G2 - 2, 2), i)
    gate([G2 - 1]), up([G2 - 1]), down([G2 - 2])
    down([G2 - 1])


def act_retention(m, act):
    s, b, run = m.sem, m.bank, m.nc.scalar.activation

    def step(i, hs, project, attend):
        def left_before(sem, per, more):
            act.wait_ge(*m.upto(f"ret_{sem}", along(i, [per * (x - 1) + more for x in hs])))

        def split(names):
            act_split(m, act, names, i)

        if project:
            split([f"ret.k{n}" for n in hs])
            if hs[0] == 0:
                act_std(m, act, "ret", b[5])
                act_rows(m, act, "ret", b[4])
            split([f"ret.v0{n}" for n in hs])
        if attend:
            left_before("y_mean", TT, TT)
            run(m.y_std[:, :], m.y_mean[:, :, 1], ACT.Sqrt, bias=m.eps[:, 1:2]).then_inc(s("ret_y_std"), 1)
            left_before("y_shift", 1, 1)
            for q in range(TT):
                run(m.ry[:, q, :], b[2 + q][:, :], ACT.Identity, scale=m.y_rstd[:, q:q + 1], bias=m.y_shift[:, q:q + 1])\
                    .then_inc(s("ret_y_normed"), 1)
        if project:
            split([f"ret.v1{n}" for n in hs])
        if attend:
            for c in range(4):
                left_before("turned", 4, c + 1)
                run(m.act_hi[:, c, :], b[2 + c][:, :], ACT.Copy).then_inc(s("ret_o_hi"), 1)
        if project:
            for x in "vg":
                for half in range(2):
                    names = [f"ret.{x}{half}{n}" for n in hs]
                    if (x, half) != ("v", 0):
                        split(after(names))
                    if x == "g" and half == 0 and attend:
                        left_before("gated", TT, TT)
                    for t in range(TT):
                        act.wait_ge(*m.upto("blocks_done", block_done(i, names, t)))
                        out = (m.rv if x == "v" else m.rg)[:, t, 256 * half:256 * half + 256]
                        run(out, b[(0, 1, 6, 7)[t]][:, 0:256], ACT.Copy if x == "v" else ACT.Silu, scale=m.rcol[:, t:t + 1])\
                            .then_inc(s(f"ret_{x}_in"), 1)
        if attend:
            for half in range(2):
                split(after([f"ret.o{half}{n - 1}" for n in hs]))

    step(None, [0], True, False)
    step(None, [1], True, True)
    with act.Fori(0, RH - 2) as i:
        step(i, list(range(2, RH)), True, True)
    step(None, [RH], False, True)


def act_end(m, act):
    s, b, run = m.sem, m.bank, m.nc.scalar.activation
    for n in range(2 * TT):
        act.wait_ge(*m.upto("out_turned", n + 1))
        run(m.out_sq[:, n, :], b[n][:, :], ACT.Square, accum_out=m.row_sum[:, n:n + 1]).then_inc(s("out_sq"), 1)
    act.wait_ge(*m.upto("out_sums", 1))
    run(m.std[:, 0:TT], m.row_sum[:, 0:TT], ACT.Sqrt, scale=1 / D, bias=m.eps[:, 1:2]).then_inc(s("out_std"), 1)


def act_program(m, act):
    s = m.sem
    act_start(m, act)
    act_pairs(m, act, "mla")
    act_layernorm(m, act, "ln0", "ffn0", "ln_mix_b", 0, "ffn0.u1")
    act_relu_mlp(m, act, "ffn0")
    act_layernorm(m, act, "ln1", "diff", "ln_ffn_b", 0, "diff.k0")
    run = m.nc.scalar.activation
    act.wait_ge(*m.upto("lam_dots", 2))
    run(m.lam[:, 2:4], m.lam[:, 0:2], ACT.Exp).then_inc(s("lam_exp"), 1)
    act_pairs(m, act, "diff")
    act_layernorm(m, act, "ln2", "ffn1", "ln_mix_b", 1, "ffn1.u1")
    act_relu_mlp(m, act, "ffn1")
    act_layernorm(m, act, "ln3", "fox", "ln_ffn_b", 1, "fox.k0")
    for k in range(KC):
        m.nc.scalar.activation(m.sq[:, k, :], m.x[:, k, :], ACT.Square).then_inc(s("fox_sq"), 1)
    act_pairs(m, act, "fox")
    act_input(m, act, "sw0", "fox_acc", KC * (PAIRS - 1), "norm_ffn_2", 0)
    act_swiglu(m, act, "sw0", False)
    act_input(m, act, "ret", "sw0_acc", KC * (G2 - 1), "norm_mix_2", 1)
    act_retention(m, act)
    act_input(m, act, "sw1", "ret_acc", KC * (RH - 1), "norm_ffn_2", 1)
    act_swiglu(m, act, "sw1", True)
    act_end(m, act)


ROPE_STEPS = 8


def dve_rope(m, dve, t, n_in):
    s, v = m.sem, m.nc.vector
    c = 2 * (t == "diff")
    step = [0]

    def done(ins):
        ins.then_inc(s(f"{t}_rope_steps"), 1)
        step[0] += 1
        if step[0] < ROPE_STEPS:
            dve.wait_ge(*m.upto(f"{t}_rope_steps", step[0]))

    dve.wait_ge(*m.upto("pos_in", 16 * n_in))
    dve.wait_ge(*m.upto("consts_in", 16))
    done(v.tensor_copy(m.ang, m.pos.bitcast(I32)))
    done(v.tensor_scalar(m.ang, m.ang, m.rope_cols[:, c:c + 1], None, ALU.mult))
    done(v.tensor_scalar(m.turns, m.ang, 1 / (2 * math.pi), ROUND, ALU.mult, ALU.add))
    done(v.tensor_scalar(m.turns, m.turns, -ROUND, None, ALU.add))
    for part in TWO_PI:
        done(v.scalar_tensor_tensor(out=m.ang, in0=m.turns, scalar=-part, in1=m.ang, op0=ALU.mult, op1=ALU.add))
    done(v.tensor_scalar(m.ang, m.ang, -3.1415925, 3.1415925, ALU.max, ALU.min))


def dve_rstd(m, dve, t, count=1):
    s, v = m.sem, m.nc.vector
    v.reciprocal(m.rcol[:, 0:TT], m.std[:, 0:TT]).then_inc(s(f"{t}_rcol"), 1)
    dve.wait_ge(*m.upto(f"{t}_rcol", count))
    for k in range(TT):
        v.tensor_scalar(m.diag[:, k, :], m.ident, m.rcol[:, k:k + 1], None, ALU.mult).then_inc(s(f"{t}_diag"), 1)


def dve_rotate(m, dve, out, src, swapped, turned, sem_steps, before):
    s, v = m.sem, m.nc.vector
    for n in range(4):
        v.tensor_copy(swapped[32 * n:32 * n + 32, :], src[32 * (n ^ 1):32 * (n ^ 1) + 32, :]).then_inc(s(sem_steps), 1)
    v.tensor_tensor(turned, src, m.rope_cos[:, :], ALU.mult).then_inc(s(sem_steps), 1)
    dve.wait_ge(*m.upto(sem_steps, before(4)))
    v.tensor_tensor(swapped, swapped, m.rope_sin[:, :], ALU.mult).then_inc(s(sem_steps), 1)
    dve.wait_ge(*m.upto(sem_steps, before(6)))
    return v.tensor_tensor(out, turned, swapped, ALU.add)


def dve_start(m, dve):
    s, b, v = m.sem, m.bank, m.nc.vector
    v.memset(m.ones[:, :], 1.0).then_inc(s("set_up"), 1)
    v.memset(m.mean_w[:, :], 1.0 / D).then_inc(s("set_up"), 1)
    for n, value in enumerate((LN_EPS, RMS_EPS, math.pi / 2)):
        v.memset(m.eps[:, n:n + 1], value).then_inc(s("set_up"), 1)
    for k in range(KC):
        dve.wait_ge(*m.upto("mla_h_hi", k + 1))
        v.tensor_tensor(m.h_lo[:, k, :], b[k][:, :], m.h_hi[:, k, :].bitcast(F32), ALU.subtract).then_inc(s("mla_h_lo"), 1)
    dve_rope(m, dve, "mla", 1)

    def latent(n, bank, gain, at):
        dve.wait_ge(*m.upto("lat_sq", n + 1))
        v.scalar_tensor_tensor(out=m.act_lo[:, n, :], in0=bank[:, :], scalar=col(m, gain, at), in1=m.act_hi[:, n, :].bitcast(F32),
                               op0=ALU.mult, op1=ALU.subtract).then_inc(s("lat_lo"), 1)

    def sum_squares(to, n, before):
        if before:
            dve.wait_ge(*m.upto("lat_sq_summed", before))
        v.tensor_tensor(m.sq[:, to, :], m.sq[:, to, :], m.sq[:, n, :], ALU.add).then_inc(s("lat_sq_summed"), 1)

    latent(0, b[0], "mla_kv_norm", 0)
    latent(1, b[1], "mla_kv_norm", 1)
    sum_squares(0, 1, 0)
    dve.wait_ge(*m.upto("blocks_done", BLOCK["pe", 0]))
    dve.wait_ge(*m.upto("mla_rope_made", 2))
    dve_rotate(m, dve, m.k_pe, b[2][:, :], m.tmp[:, 0, :], m.tmp[:, 1, :], "k_pe_steps", lambda n: n).then_inc(s("k_pe_in"), 1)
    latent(2, b[3], "mla_q_norm", 0)
    latent(3, b[4], "mla_q_norm", 1)
    sum_squares(2, 3, 0)
    latent(4, b[5], "mla_q_norm", 2)
    sum_squares(2, 4, 2)
    for n in range(2):
        at = TT * n
        dve.wait_ge(*m.upto("lat_std", n + 1))
        v.reciprocal(m.rcol[:, at:at + TT], m.std[:, at:at + TT]).then_inc(s("lat_rcol"), 1)
        dve.wait_ge(*m.upto("lat_rcol", n + 1))
        if n:
            dve.wait_ge(*m.upto("lat_spread", 1))
        for k in range(TT):
            v.tensor_scalar(m.diag[:, k, :], m.ident, m.rcol[:, at + k:at + k + 1], None, ALU.mult).then_inc(s("lat_diag"), 1)


def dve_add_block(m, dve, t, n, bank, names, part, i, steps, first):
    s, v = m.sem, m.nc.vector
    dve.wait_ge(*m.upto("blocks_done", block_done(i, names, part)))
    if not first:
        dve.wait_ge(*m.upto(f"{t}_acc", along(i, [KC * (g - 1) + n + 1 for g in steps])))
    v.tensor_tensor(m.x[:, n, :], m.x[:, n, :], bank[:, :], ALU.add).then_inc(s(f"{t}_acc"), 1)


def dve_sum_chunk(m, dve, t, done, count, k):
    s, v = m.sem, m.nc.vector
    dve.wait_ge(*m.upto(done, count + k + 1))
    if k:
        dve.wait_ge(*m.upto(f"{t}_summed", k))
        v.tensor_tensor(m.rb[:, :], m.rb[:, :], m.x[:, k, :], ALU.add).then_inc(s(f"{t}_summed"), 1)
    else:
        v.tensor_copy(m.rb[:, :], m.x[:, k, :]).then_inc(s(f"{t}_summed"), 1)


def dve_layernorm(m, dve, t, to, gain, shift, row):
    s, b, v = m.sem, m.bank, m.nc.vector
    dve.wait_ge(*m.upto(f"{t}_mean", 1))
    for k in range(KC):
        v.tensor_tensor(m.x[:, k, :], m.x[:, k, :], b[0][:, :], ALU.subtract).then_inc(s(f"{t}_centered"), 1)
    if to == "fox":
        dve.wait_ge(*m.upto("fox_wf_hi", 1))
        v.tensor_tensor(m.wf_lo, m.wf[:, :, :], m.wf_hi.bitcast(F32), ALU.subtract).then_inc(s("fox_wf_lo"), 1)
    dve.wait_ge(*m.upto(f"{t}_std", 1))
    v.reciprocal(m.rb[:, :], m.rb[:, :]).then_inc(s(f"{t}_rstd"), 1)
    dve.wait_ge(*m.upto(f"{t}_rstd", 1))
    dve.wait_ge(*m.upto(f"{t}_sq", KC))
    for k in range(KC):
        v.scalar_tensor_tensor(out=m.x[:, k, :], in0=m.x[:, k, :], scalar=col(m, gain, KC * row + k), in1=m.rb[:, :],
                               op0=ALU.mult, op1=ALU.mult).then_inc(s(f"{t}_scaled"), 1)
    if to == "fox":
        for k in range(KC):
            dve_input_low(m, dve, "fox", "norm_mix_2", 0, k)
        dve_sum_squares(m, dve, "fox")
        return
    for k in range(KC):
        dve.wait_ge(*m.upto(f"{to}_h_hi", k + 1))
        v.scalar_tensor_tensor(out=m.h_lo[:, k, :], in0=m.x[:, k, :], scalar=col(m, shift, KC * row + k),
                               in1=m.h_hi[:, k, :].bitcast(F32), op0=ALU.add, op1=ALU.subtract).then_inc(s(f"{to}_h_lo"), 1)

    for k in range(KC):
        v.tensor_scalar(m.x[:, k, :], m.x[:, k, :], col(m, shift, KC * row + k), ALPHA, ALU.add, ALU.mult)\
            .then_inc(s(f"{t}_done"), 1)


def dve_input_low(m, dve, t, gain, row, k):
    s, v = m.sem, m.nc.vector
    dve.wait_ge(*m.upto(f"{t}_h_hi", k + 1))
    v.scalar_tensor_tensor(out=m.h_lo[:, k, :], in0=m.x[:, k, :], scalar=col(m, gain, KC * row + k),
                           in1=m.h_hi[:, k, :].bitcast(F32), op0=ALU.mult, op1=ALU.subtract).then_inc(s(f"{t}_h_lo"), 1)


def dve_sum_squares(m, dve, t):
    for k in range(1, KC):
        dve.wait_ge(*m.upto(f"{t}_sq", k + 1))
        if k > 1:
            dve.wait_ge(*m.upto(f"{t}_sq_summed", k - 1))
        m.nc.vector.tensor_tensor(m.sq[:, 0, :], m.sq[:, 0, :], m.sq[:, k, :], ALU.add).then_inc(m.sem(f"{t}_sq_summed"), 1)


def dve_norm_rstd(m, dve, t):
    dve.wait_ge(*m.upto(f"{t}_norm_std", 1))
    dve_rstd(m, dve, f"{t}_norm")


def dve_last_blocks(m, dve, add, t, count, then):
    for n in range(KC + 1):
        if n < KC:
            add(n)
        if 0 < n < KC and then[0] == "mean":
            dve_sum_chunk(m, dve, then[1], f"{t}_acc", count, n - 1)
        elif n and then[0] == "input":
            dve_input_low(m, dve, *then[1:], n - 1)
    if then[0] == "input":
        dve_sum_squares(m, dve, then[1])


def dve_pairs(m, dve, t, then):
    s, b, v = m.sem, m.bank, m.nc.vector
    u0, u1, o_bank = b[5], b[6], b[7]

    def step(i, ps, project, attend):
        def per_head(j, back=1):
            def c(per, more):
                return along(i, [per * (2 * (p - back) + j) + more for p in ps])
            return c

        def unit(x):
            return [f"mla.p{p}" if t == "mla" else f"{t}.{x}{p}" for p in ps]

        maps = 2 if t == "diff" else 1

        def maxima(j, back=1):
            c = per_head(j, back)
            for nth, (q, n, bank, at, end) in enumerate(score_tiles(t)):
                w = (q + 1) * P
                dve.wait_ge(*m.upto(f"{t}_scores", c(TT * maps, end)))
                if t == "fox":
                    head = along(i, [2 * (p - back) + j for p in ps]) if ps[0] > 1 else 2 * (ps[0] - back) + j
                    neg_c = m.neg_c[:, bass.ds(head, 1), 0:w] if i is not None else m.neg_c[:, head, 0:w]
                    c_col = m.c_cols[:, q, bass.ds(head, 1)]
                    src = m.probs[:, PACKED[q]:PACKED[q] + w]
                    v.scalar_tensor_tensor(out=src, in0=neg_c, scalar=c_col, in1=b[bank][:, at:at + w],
                                           op0=ALU.add, op1=ALU.add).then_inc(s("fox_forgot"), 1)
                    dve.wait_ge(*m.upto("fox_forgot", c(TT, q + 1)))
                else:
                    src = b[bank][:, at:at + w]
                last = src[:, q * P:w]
                v.tensor_tensor(last, last, m.causal, ALU.add).then_inc(s(f"{t}_masked"), 1)
                dve.wait_ge(*m.upto(f"{t}_masked", c(TT * maps, nth + 1)))
                v.tensor_reduce(m.neg_max[:, maps * q + n:maps * q + n + 1], src, AX, ALU.max, negate=True).then_inc(s(f"{t}_neg_max"), 1)

        def normalize(j, back=1, nths=range(TT)):
            c = per_head(j, back)
            for nth in nths:
                q, exps = query_tiles(t)[nth]
                dve.wait_ge(*m.upto(f"{t}_exps", c(TT * maps, exps)))
                rec = m.row_rec[:, maps * q:maps * q + maps]
                v.reciprocal(rec, m.row_sum[:, maps * q:maps * q + maps]).then_inc(s(f"{t}_row_rec"), 1)
                dve.wait_ge(*m.upto(f"{t}_row_rec", c(TT, nth + 1)))
                w = (q + 1) * P
                out = m.probs[:, PACKED[q]:PACKED[q] + w]
                if t == "diff":
                    second = m.probs2[:, PACKED[q]:PACKED[q] + w]
                    v.tensor_scalar(second, second, rec[:, 1:2], m.lam[:, 5:6], ALU.mult, ALU.mult).then_inc(s("diff_second"), 1)
                    dve.wait_ge(*m.upto("diff_second", c(TT, nth + 1)))
                    v.scalar_tensor_tensor(out=out, in0=out, scalar=rec[:, 0:1], in1=second, op0=ALU.mult, op1=ALU.add).then_inc(s("diff_probs"), 1)
                else:
                    v.tensor_scalar(out, out, rec, None, ALU.mult).then_inc(s(f"{t}_probs"), 1)

        def take(x, j):
            part = f"{x}{j}" if t == "mla" else j
            dve.wait_ge(*m.upto("blocks_done", block_done(i, unit(x), part)))
            bank, out = ((u0, m.q) if x == "q" else (u1, m.k))
            if ps[0] == 0 and j == 1:
                bank = b[{"q": 4, "k": 7}[x] if t == "mla" else {"q": 0, "k": 1}[x]]
            if t == "diff":
                n = [2 * p + j for p in ps]
                scale = DIFF_SCALE if x == "q" else 1.0
                swapped, turned = (m.rtmp[:, 2 * (x == "k") + e, :] for e in range(2))
                if ps[0] or j:
                    dve.wait_ge(*m.upto(f"diff_{x}_in", along(i, n)))
                steps = f"diff_{x}_steps"
                v.scalar_tensor_tensor(out=turned, in0=bank[:, :], scalar=scale, in1=m.rope_cos[:, :],
                                       op0=ALU.mult, op1=ALU.mult).then_inc(s(steps), 1)
                v.stream_shuffle(swapped, bank[:, :], ROT_SWAP).then_inc(s(steps), 1)
                dve.wait_ge(*m.upto(steps, along(i, [3 * a + 2 for a in n])))
                v.scalar_tensor_tensor(out=swapped, in0=swapped, scalar=scale, in1=m.rope_sin[:, :], op0=ALU.mult, op1=ALU.mult).then_inc(s(steps), 1)
                dve.wait_ge(*m.upto(steps, along(i, [3 * a + 3 for a in n])))
                v.tensor_tensor(out[:, j, :], turned, swapped, ALU.add).then_inc(s(f"diff_{x}_in"), 1)
                return
            rows = m.rb_q if t == "mla" and x == "q" else m.rb[:, :]
            scale = 1.0 if x == "k" else MLA_SCALE if t == "mla" else FOX_SCALE
            v.scalar_tensor_tensor(out=out[:, j, :], in0=bank[:, :], scalar=scale, in1=rows, op0=ALU.mult, op1=ALU.mult)\
                .then_inc(s(f"{t}_{x}_in"), 1)

        def take_rotated():
            dve.wait_ge(*m.upto("blocks_done", block_done(i, unit("q"), "pe")))
            if ps[0]:
                dve.wait_ge(*m.upto("mla_pe_in", along(i, ps)))
            src = u0 if ps[0] else b[1]
            v.scalar_tensor_tensor(out=m.tmp[:, 2, :], in0=src[:, :], scalar=MLA_SCALE, in1=m.rb_q, op0=ALU.mult, op1=ALU.mult)\
                .then_inc(s("mla_pe_scaled"), 1)
            dve.wait_ge(*m.upto("mla_pe_scaled", along(i, [p + 1 for p in ps])))
            dve_rotate(m, dve, m.q_pe, m.tmp[:, 2, :], m.tmp[:, 0, :], m.tmp[:, 1, :], "mla_pe_steps",
                       lambda n: along(i, [6 * p + n for p in ps])).then_inc(s("mla_pe_in"), 1)

        def head_low(j):
            dve.wait_ge(*m.upto(f"{t}_o_hi", per_head(j)(1, 1)))
            src = m.tmp[:, 2, :] if t == "diff" else o_bank[:, :]
            v.tensor_tensor(m.act_lo[:, 5 + j, :], src, m.act_hi[:, 5 + j, :].bitcast(F32), ALU.subtract).then_inc(s(f"{t}_o_lo"), 1)

        def head_rstd(j):
            if t == "diff" and attend:
                dve.wait_ge(*m.upto("diff_sub_std", per_head(j)(1, 1)))
                dve_rstd(m, dve, "diff_sub", per_head(j)(1, 1))

        def head_norm(j):
            dve.wait_ge(*m.upto("diff_sub_spread", per_head(j)(1, 1)))
            dve.wait_ge(*m.upto("diff_o_raw", per_head(j)(1, 1)))
            v.scalar_tensor_tensor(out=m.tmp[:, 2, :], in0=m.tmp[:, 0, :], scalar=m.lam[:, 6:7], in1=o_bank[:, :],
                                   op0=ALU.mult, op1=ALU.mult).then_inc(s("diff_o_taken"), 1)
            head_low(j)

        if t == "fox" and ps[0] == 0:
            dve_fox_gates(m, dve, take)
        if t == "mla" and ps[0] == 0:
            dve.wait_ge(*m.upto("lat_rows", 2))
        if project and not (t == "fox" and ps[0] == 0):
            take("q", 0), take("k", 0)
        if t == "mla" and not attend:
            take_rotated()
        if attend:
            if t != "diff":
                head_low(0)
            maxima(1), normalize(1)
        head_rstd(0)
        if project and not (t == "fox" and ps[0] == 0):
            take("q", 1)
            if t != "diff":
                take("k", 1)
        if project and attend and t == "mla":
            take_rotated()
        if attend:
            if t == "diff":
                head_norm(0)
            if t != "diff":
                head_low(1)
        if project and t == "diff":
            take("k", 1)
        head_rstd(1)
        if attend and t == "diff":
            head_norm(1)
        if t == "fox" and ps[0] == 0:
            dve.wait_ge(*m.upto("fox_neg_c", 8))
        if project:
            maxima(0, back=0)
        if project and not attend:
            normalize(0, back=0)
        if attend:
            banks = output_banks(t)

            def add(n):
                dve_add_block(m, dve, t, n, b[banks[n % len(banks)]], [f"{t}.o{p - 1}" for p in ps], n, i, [p - 1 for p in ps], ps[0] == 1)
            if project:
                for n in range(KC):
                    add(n)
                    if 1 <= n <= TT:
                        normalize(0, 0, [n - 1])
            else:
                dve_last_blocks(m, dve, add, t, KC * (PAIRS - 1), then)

    step(None, [0], True, False)
    step(None, [1], True, True)
    with dve.Fori(0, PAIRS - 2) as i:
        step(i, list(range(2, PAIRS)), True, True)
    step(None, [PAIRS], False, True)


ROT_SWAP = list(range(8, 16)) + list(range(8)) + list(range(16, 32))


def dve_fox_gates(m, dve, take):
    s, b, v = m.sem, m.bank, m.nc.vector
    dve_norm_rstd(m, dve, "fox")
    dve.wait_ge(*m.upto("fox_logits_turned", 1))
    for t in range(TT):
        v.scalar_tensor_tensor(out=m.gate_f[:, 0, t, :], in0=b[2][:, 8 * t:8 * t + 8], scalar=m.rcol[:, t:t + 1], in1=m.b_f[:, :],
                               op0=ALU.mult, op1=ALU.add).then_inc(s("fox_z"), 1)
    z, e, log_f, ln, u, rec = (m.gate_f[:, n, :, :] for n in range(6))
    dve.wait_ge(*m.upto("fox_gate_steps", 2))
    v.tensor_scalar(u, e, 1.0, None, ALU.add).then_inc(s("fox_log1p"), 1)
    dve.wait_ge(*m.upto("fox_log1p", 1))
    v.scalar_tensor_tensor(out=e, in0=u, scalar=-1.0, in1=e, op0=ALU.add, op1=ALU.subtract).then_inc(s("fox_log1p"), 1)
    v.reciprocal(rec, u).then_inc(s("fox_log1p"), 1)
    dve.wait_ge(*m.upto("fox_log1p", 3))
    v.tensor_tensor(e, e, rec, ALU.mult).then_inc(s("fox_log1p"), 1)
    dve.wait_ge(*m.upto("fox_norm_in", 1))
    take("q", 0), take("k", 0)
    dve.wait_ge(*m.upto("fox_gate_steps", 3))
    v.scalar_tensor_tensor(out=log_f, in0=z, scalar=0.0, in1=ln, op0=ALU.min, op1=ALU.subtract).then_inc(s("fox_log1p"), 1)
    dve.wait_ge(*m.upto("fox_log1p", 5))
    v.tensor_tensor(log_f, log_f, e, ALU.add).then_inc(s("fox_log_f"), 1)
    take("q", 1)
    dve.wait_ge(*m.upto("fox_sums", 1))
    v.tensor_copy(m.c_cols[:, :, :].rearrange("p t h -> p (t h)"), b[4][:, 128:128 + 8 * TT]).then_inc(s("fox_c_cols"), 1)
    take("k", 1)


def dve_lambda(m, dve):
    s, v = m.sem, m.nc.vector
    dve.wait_ge(*m.upto("lam_in", 64))
    for n in range(2):
        v.tensor_tensor(m.lam_in[:, n, :] if n == 0 else m.lam_in[:, 2, :], m.lam_in[:, 2 * n, :], m.lam_in[:, 2 * n + 1, :], ALU.mult)\
            .then_inc(s("lam_products"), 1)
        dve.wait_ge(*m.upto("lam_products", n + 1))
        v.tensor_reduce(m.lam[:, n:n + 1], m.lam_in[:, 2 * n, :], AX, ALU.add).then_inc(s("lam_dots"), 1)
    v.tensor_scalar(m.lam[:, 6:7], col(m, "diff_subln", 0), 1.0 - LAMBDA_INIT, None, ALU.mult).then_inc(s("lam_steps"), 1)
    dve.wait_ge(*m.upto("lam_exp", 1))
    v.tensor_tensor(m.lam[:, 4:5], m.lam[:, 2:3], m.lam[:, 3:4], ALU.subtract).then_inc(s("lam_steps"), 1)
    dve.wait_ge(*m.upto("lam_steps", 2))
    v.tensor_scalar(m.lam[:, 5:6], m.lam[:, 4:5], LAMBDA_INIT, -1.0, ALU.add, ALU.mult).then_inc(s("lam_steps"), 1)
    dve.wait_ge(*m.upto("lam_steps", 3))


def dve_relu_mlp(m, dve, t, norm, then):
    s, b, v = m.sem, m.bank, m.nc.vector

    def up(gs, i=None):
        for j in range(2):
            dve.wait_ge(*m.upto(f"{t}_relu", along(i, [2 * g + j + 1 for g in gs])))
            v.tensor_tensor(m.square[:, j, :], m.relu[:, j, :], m.relu[:, j, :], ALU.mult).then_inc(s(f"{t}_squared"), 1)
            dve.wait_ge(*m.upto(f"{t}_squared", along(i, [2 * g + j + 1 for g in gs])))
            dve.wait_ge(*m.upto(f"{t}_a_hi", along(i, [2 * g + j + 1 for g in gs])))
            at = 2 * (gs[0] % 2) + j
            v.tensor_tensor(m.act_lo[:, at, :], m.square[:, j, :], m.act_hi[:, at, :].bitcast(F32), ALU.subtract).then_inc(s(f"{t}_a_lo"), 1)

    def adder(gs, i=None):
        def add(n):
            dve_add_block(m, dve, t, n, b[4 + n % 4], [f"{t}.d{g}" for g in gs], n, i, gs, gs[0] == 0)
        return add

    def down(gs, i=None):
        for n in range(KC):
            adder(gs, i)(n)

    up([0])
    if t == "ffn0":
        dve_rope(m, dve, "diff", 2)
    up([1])
    dve.wait_ge(*m.upto(f"{norm}_done", KC))
    down([0])
    with dve.Fori(0, (G1 - 2) // 2) as i:
        for e in range(2):
            up(range(2 + e, G1, 2), i)
            down(range(1 + e, G1 - 1, 2), i)
    dve_last_blocks(m, dve, adder([G1 - 1]), t, KC * (G1 - 1), then)


def dve_swiglu(m, dve, t, then):
    s, b, v = m.sem, m.bank, m.nc.vector

    def gate(gs, i=None):
        if gs[0] == 0:
            dve_norm_rstd(m, dve, t)
            dve.wait_ge(*m.upto(f"{t}_norm_in", 1))
        for j in range(2):
            dve.wait_ge(*m.upto("blocks_done", block_done(i, [f"{t}.g{g}" for g in gs], j)))
            if gs[0]:
                dve.wait_ge(*m.upto(f"{t}_silu", along(i, [2 * g + j - 1 for g in gs])))
            v.tensor_tensor(m.gate[:, j, :], b[j][:, :], m.rb[:, :], ALU.mult).then_inc(s(f"{t}_g_in"), 1)

    def up(gs, i=None):
        at = 2 * (gs[0] % 2)
        for j in range(2):
            dve.wait_ge(*m.upto("blocks_done", block_done(i, [f"{t}.u{g}" for g in gs], j)))
            v.tensor_tensor(m.up[:, j, :], b[2 + j][:, :], m.rb[:, :], ALU.mult).then_inc(s(f"{t}_u_in"), 1)
            dve.wait_ge(*m.upto(f"{t}_u_in", along(i, [2 * g + j + 1 for g in gs])))
            dve.wait_ge(*m.upto(f"{t}_silu", along(i, [2 * g + j + 1 for g in gs])))
            v.tensor_tensor(m.prod[:, j, :], m.up[:, j, :], m.silu[:, j, :], ALU.mult).then_inc(s(f"{t}_prod"), 1)
            dve.wait_ge(*m.upto(f"{t}_prod", along(i, [2 * g + j + 1 for g in gs])))
            dve.wait_ge(*m.upto(f"{t}_a_hi", along(i, [2 * g + j + 1 for g in gs])))
            v.tensor_tensor(m.act_lo[:, at + j, :], m.prod[:, j, :], m.act_hi[:, at + j, :].bitcast(F32), ALU.subtract)\
                .then_inc(s(f"{t}_a_lo"), 1)

    def adder(gs, i=None):
        def add(n):
            dve_add_block(m, dve, t, n, b[4 + n % 4], [f"{t}.d{g}" for g in gs], n, i, gs, gs[0] == 0)
        return add

    def down(gs, i=None):
        for n in range(KC):
            adder(gs, i)(n)

    gate([0]), up([0])
    gate([1]), up([1]), down([0])
    with dve.Fori(0, (G2 - 3) // 2) as i:
        for e in range(2):
            gs = range(2 + e, G2 - 1, 2)
            gate(gs, i), up(gs, i), down(range(1 + e, G2 - 2, 2), i)
    gate([G2 - 1]), up([G2 - 1]), down([G2 - 2])
    dve_last_blocks(m, dve, adder([G2 - 1]), t, KC * (G2 - 1), then)


def dve_retention(m, dve, then):
    s, b, v = m.sem, m.bank, m.nc.vector

    def step(i, hs, project, attend):
        def left_before(sem, per, more):
            dve.wait_ge(*m.upto(f"ret_{sem}", along(i, [per * (x - 1) + more for x in hs])))

        def take(x):
            out, scale = (m.q, 1.0) if x == "q" else (m.k, RET_SCALE)
            t = [m.rtmp[:, n, :] for n in range(4)]
            steps = s(f"ret_{x}_steps")

            def before(n):
                dve.wait_ge(steps, along(i, [5 * h + n for h in hs]))

            for j in range(2):
                dve.wait_ge(*m.upto("blocks_done", block_done(i, [f"ret.{x}{h}" for h in hs], j)))
                bank = b[2 + j] if hs[0] == 0 and x == "k" else b[j]
                v.scalar_tensor_tensor(out=t[j], in0=bank[:, :], scalar=scale, in1=m.rb[:, :], op0=ALU.mult, op1=ALU.mult)\
                    .then_inc(s(f"ret_{x}_in"), 1)
            dve.wait_ge(*m.upto(f"ret_{x}_in", along(i, [2 * h + 2 for h in hs])))
            v.tensor_tensor(t[2], t[0], m.ret_cos, ALU.mult).then_inc(steps, 1)
            v.tensor_tensor(t[3], t[1], m.ret_sin, ALU.mult).then_inc(steps, 1)
            before(2)
            v.tensor_tensor(out[:, 0, :], t[2], t[3], ALU.subtract).then_inc(steps, 1)
            before(3)
            v.tensor_tensor(t[2], t[0], m.ret_sin, ALU.mult).then_inc(steps, 1)
            v.tensor_tensor(t[3], t[1], m.ret_cos, ALU.mult).then_inc(steps, 1)
            before(5)
            v.tensor_tensor(out[:, 1, :], t[2], t[3], ALU.add).then_inc(s(f"ret_{x}_roped"), 1)

        if attend:
            head = along(i, [h - 1 for h in hs]) if hs[0] > 1 else hs[0] - 1
            for n, kb in enumerate((0, 1, 3, 2)):
                bank, at = TURN_AT[kb]
                w = T - kb * P
                left_before("scores", TT, (1, 3, 3, 4)[n])
                decay = m.decay[:, bass.ds(head, 1), 0:w] if i is not None else m.decay[:, head, 0:w]
                v.tensor_tensor(m.ra[:, TURNED[kb]:TURNED[kb] + w], b[2 + bank][:, at:at + w], decay, ALU.mult).then_inc(s("ret_decayed"), 1)
        if project:
            if hs[0] == 0:
                dve_norm_rstd(m, dve, "ret")
                dve.wait_ge(*m.upto("ret_norm_in", 1))
                dve.wait_ge(*m.upto("ret_tables_in", 16))
            take("q")
        if attend:
            for q in range(TT):
                left_before("values", TT, q + 1)
                v.bn_stats(m.y_stats[:, q, :], b[2 + q][:, :]).then_inc(s("ret_y_stats"), 1)
            left_before("y_stats", TT, TT)
            v.memset(m.y_shift[:, :], 0.0).then_inc(s("ret_y_cleared"), 1)
            for q in range(TT):
                v.bn_aggr(m.y_mean[:, q, :], m.y_stats[:, q, :]).then_inc(s("ret_y_mean"), 1)
            left_before("y_std", 1, 1)
            v.reciprocal(m.y_rstd[:, :], m.y_std[:, :]).then_inc(s("ret_y_rstd"), 1)
            left_before("y_rstd", 1, 1)
            v.scalar_tensor_tensor(out=m.y_shift[:, :], in0=m.y_mean[:, :, 0], scalar=-1.0, in1=m.y_rstd[:, :], op0=ALU.mult, op1=ALU.mult)\
                .then_inc(s("ret_y_shift"), 1)
            left_before("g_in", 2 * TT, 2 * TT)
            for q in range(TT):
                left_before("y_normed", TT, q + 1)
                v.tensor_tensor(m.ry[:, q, :], m.ry[:, q, :], m.rg[:, q, :], ALU.mult).then_inc(s("ret_gated"), 1)
        if project:
            take("k")
        if attend:
            for c in range(4):
                left_before("o_hi", 4, c + 1)
                v.tensor_tensor(m.act_lo[:, c, :], b[2 + c][:, :], m.act_hi[:, c, :].bitcast(F32), ALU.subtract).then_inc(s("ret_o_lo"), 1)

            def add(n):
                dve_add_block(m, dve, "ret", n, b[4 + n % 4], [f"ret.o{n // 4}{h - 1}" for h in hs], n % 4, i, [h - 1 for h in hs], hs[0] == 1)
            if project:
                for n in range(KC):
                    add(n)
            else:
                dve_last_blocks(m, dve, add, "ret", KC * (RH - 1), then)

    step(None, [0], True, False)
    step(None, [1], True, True)
    with dve.Fori(0, RH - 2) as i:
        step(i, list(range(2, RH)), True, True)
    step(None, [RH], False, True)


def dve_end(m, dve):
    s, b, v = m.sem, m.bank, m.nc.vector
    dve.wait_ge(*m.upto("out_sq", 2 * TT))
    v.tensor_tensor(m.row_sum[:, 0:TT], m.row_sum[:, 0:TT], m.row_sum[:, TT:2 * TT], ALU.add).then_inc(s("out_sums"), 1)
    dve.wait_ge(*m.upto("out_std", 1))
    v.reciprocal(m.rcol[:, 0:TT], m.std[:, 0:TT]).then_inc(s("out_rcol"), 1)
    dve.wait_ge(*m.upto("out_rcol", 1))
    dve.wait_ge(*m.upto("gain_in", 16))
    for t in range(TT):
        for half in range(2):
            v.scalar_tensor_tensor(out=m.x_tok[:, t, 512 * half:512 * half + 512], in0=b[4 * half + t][:, :], scalar=m.rcol[:, t:t + 1],
                                   in1=m.gain_final[:, 512 * half:512 * half + 512], op0=ALU.mult, op1=ALU.mult).then_inc(s("out_rows"), 1)


def dve_program(m, dve):
    dve_start(m, dve)
    dve.wait_ge(*m.upto("x_scaled", KC))
    dve_pairs(m, dve, "mla", ("mean", "ln0"))
    dve_layernorm(m, dve, "ln0", "ffn0", "ln_mix_g", "ln_mix_b", 0)
    dve_relu_mlp(m, dve, "ffn0", "ln0", ("mean", "ln1"))
    dve_layernorm(m, dve, "ln1", "diff", "ln_ffn_g", "ln_ffn_b", 0)
    dve_lambda(m, dve)
    dve.wait_ge(*m.upto("diff_rope_made", 2))
    dve.wait_ge(*m.upto("ln1_done", KC))
    dve_pairs(m, dve, "diff", ("mean", "ln2"))
    dve_layernorm(m, dve, "ln2", "ffn1", "ln_mix_g", "ln_mix_b", 1)
    dve_relu_mlp(m, dve, "ffn1", "ln2", ("mean", "ln3"))
    dve_layernorm(m, dve, "ln3", "fox", "ln_ffn_g", "ln_ffn_b", 1)
    dve_pairs(m, dve, "fox", ("input", "sw0", "norm_ffn_2", 0))
    dve_swiglu(m, dve, "sw0", ("input", "ret", "norm_mix_2", 1))
    dve_retention(m, dve, ("input", "sw1", "norm_ffn_2", 1))
    dve_swiglu(m, dve, "sw1", ("none",))
    dve_end(m, dve)


def two_blocks(nc, dram):
    with ExitStack() as ctx:
        m = memory(nc, ctx, dram)
        block = ctx.enter_context(nc.Block())

        @block.sync
        def _(sp):
            sp_program(m, sp)

        @block.gpsimd
        def _(pool):
            pool_program(m, pool)

        @block.scalar
        def _(act):
            act_program(m, act)

        @block.tensor
        def _(pe):
            pe_program(m, pe)

        @block.vector
        def _(dve):
            dve_program(m, dve)


def constants():
    at = np.arange(P)
    c = {"c_square": np.zeros((P, 3 * P + 4), np.float32)}
    c["c_square"][:, 0:P] = np.eye(P)
    c["c_square"][:, P:2 * P] = np.where(at[None, :] > at[:, None], MASKED, 0.0)
    c["c_square"][:, 2 * P:3 * P] = at[:, None] <= at[None, :]
    mla = 10000.0 ** (-np.arange(0, ROPE, 2) / ROPE)
    rot = 500000.0 ** (-np.arange(0, 16, 2) / 16)
    c["c_square"][:, 3 * P] = mla[at % 32]
    c["c_square"][:, 3 * P + 1] = np.where(at % 64 < 32, -1.0, 1.0)
    c["c_square"][:, 3 * P + 2] = np.where(at % 64 < 16, rot[at % 8], 0.0)
    c["c_square"][:, 3 * P + 3] = np.where(at % 64 < 8, -1.0, 1.0)
    c["c_sel"] = np.repeat(np.eye(8, dtype=np.float32)[:, :, None], P, axis=2)
    key, query = at[:, None], np.arange(T)[None, :]
    decay = [np.where(key // 64 <= query // 64, (1.0 - 2.0 ** (-5.0 - h)) ** np.abs(query - key), 0.0) for h in range(RH)]
    inv = (10000.0 ** (-np.arange(P) / P)).astype(np.float32)
    ang = np.arange(T, dtype=np.float32)[None, :] * inv[:, None]
    c["c_ret"] = np.concatenate([*decay, np.cos(ang), np.sin(ang)], axis=1).astype(np.float32)
    return c


_INS = ["x", "positions", "ln_mix_g", "ln_mix_b", "mla_w_dq", "mla_q_norm", "mla_w_uq", "mla_w_dkv", "mla_kv_norm", "mla_w_ukv",
        "mla_w_o", "diff_w_qkv", "diff_lambda_q1", "diff_lambda_k1", "diff_lambda_q2", "diff_lambda_k2", "diff_subln", "diff_w_o",
        "ln_ffn_g", "ln_ffn_b", "ffn_w_up", "ffn_w_down", "norm_mix_2", "norm_ffn_2", "fox_w_in_2", "fox_b_f_2", "fox_w_out_2",
        "ret_w_in_2", "ret_w_out_2", "ffn_w_in_2", "ffn_w_out_2", "final_norm_2"]


def kernel(**inputs):
    import concourse.bacc as bacc
    from concourse.bass_utils import run_bass_kernel_spmd

    nc = bacc.Bacc("TRN2", target_bir_lowering=False, num_devices=1)
    arrays, dram = {}, {}
    given = {name: np.ascontiguousarray(inputs[name]) for name in _INS}
    for name, a in {**given, **constants()}.items():
        arrays[f"in_{name}"] = a
        dram[name] = nc.dram_tensor(f"in_{name}", a.shape, mybir.dt.from_np(a.dtype), kind="ExternalInput").ap()
    dram["out"] = nc.dram_tensor("out_0", (1, T, D), F32, kind="ExternalOutput").ap()
    two_blocks(nc, dram)
    r = run_bass_kernel_spmd(nc, [arrays], core_ids=[0])
    return r.results[0]["out_0"]
```
